# Optimizing a Trainium2 kernel written in Bass

```python
import jax, jax.numpy as jnp
from jax import lax
import numpy as np
import math

D_MODEL = 1024
BATCH = 1
SEQ = 256
DEPTH = 2

N_A = DEPTH // 2
N_B = DEPTH - N_A
POOL_WINDOWS = (2, 4, 8, 16)
POOL_GROUPS = len(POOL_WINDOWS)
GC = D_MODEL // POOL_GROUPS
N_HEADS = 16
HEAD_DIM = D_MODEL // N_HEADS
D_FF = 4 * D_MODEL
Q_BLOCK = 128
EPS = 1e-6


def rms_norm(x, g):
    xf = x.astype(jnp.float32)
    y = xf * lax.rsqrt(jnp.mean(xf * xf, axis=-1, keepdims=True) + EPS)
    return (y * g.astype(jnp.float32)).astype(x.dtype)

def pool_mixer(h, w_grp, scale):
    B, S, D = h.shape
    hf = h.astype(jnp.float32)
    cp = jnp.concatenate([jnp.zeros((B, 1, D), jnp.float32), lax.cumsum(hf, axis=1)], axis=1)
    pos = jnp.arange(S, dtype=jnp.int32)
    outs = []
    for g, w in enumerate(POOL_WINDOWS):
        sl = slice(g * GC, (g + 1) * GC)
        upper = cp[:, 1:, sl]
        lower = jnp.concatenate([jnp.zeros((B, w - 1, GC), jnp.float32), cp[:, :S + 1 - w, sl]], axis=1)
        count = jnp.minimum(pos + 1, w).astype(jnp.float32)[None, :, None]
        outs.append((upper - lower) / count - hf[:, :, sl])
    y = jnp.stack(outs, axis=2)
    y = jnp.einsum('bsgc,gcd->bsgd', y, w_grp.astype(jnp.float32)).reshape(B, S, D)
    return (y * scale.astype(jnp.float32)).astype(h.dtype)

def stick_breaking_attention(q, k, v):
    S = q.shape[2]
    inv_sqrt_d = 1.0 / float(np.sqrt(HEAD_DIM))
    outs = []
    for i in range(S // Q_BLOCK):
        kv_len = (i + 1) * Q_BLOCK
        q_blk = q[:, :, i * Q_BLOCK:kv_len]
        k_blk = k[:, :, :kv_len]
        v_blk = v[:, :, :kv_len]
        z = jnp.einsum('bhqd,bhkd->bhqk', q_blk, k_blk,
                       preferred_element_type=jnp.float32) * inv_sqrt_d
        t_idx = i * Q_BLOCK + jnp.arange(Q_BLOCK, dtype=jnp.int32)[:, None]
        s_idx = jnp.arange(kv_len, dtype=jnp.int32)[None, :]
        mask = s_idx < t_idx
        log1m = jnp.where(mask, -jax.nn.softplus(z), 0.0)
        excl = lax.cumsum(log1m, axis=3, reverse=True) - log1m
        a = jnp.where(mask, jnp.exp(jax.nn.log_sigmoid(z) + excl), 0.0)
        outs.append(jnp.einsum('bhqk,bhkd->bhqd', a, v_blk.astype(jnp.float32)))
    return jnp.concatenate(outs, axis=2).astype(q.dtype)

def sq_relu_mlp(h, w_up, w_down):
    u = jnp.matmul(h, w_up)
    return jnp.matmul(jnp.square(jax.nn.relu(u)), w_down)

def first_inputs(seed: int = 0) -> dict:
    key = jax.random.key(seed)
    ks = jax.random.split(key, 16)
    D, HD = D_MODEL, N_HEADS * HEAD_DIM
    nrm = lambda k, shape, fan_in: jax.random.normal(k, shape, jnp.float32) * (fan_in ** -0.5)
    gain = lambda k, shape: 1.0 + 0.05 * jax.random.normal(k, shape, jnp.float32)
    return {
        "x": jax.random.normal(ks[0], (BATCH, SEQ, D), jnp.float32),
        "pool_w": nrm(ks[1], (N_A, POOL_GROUPS, GC, GC), GC),
        "pool_scale": 0.5 + jax.random.uniform(ks[2], (N_A, D), jnp.float32),
        "w_q": nrm(ks[3], (N_B, D, HD), D),
        "w_kv": nrm(ks[4], (D, 2 * HD), D),
        "kv_norm_g": gain(ks[5], (D,)),
        "w_o": nrm(ks[6], (N_B, HD, D), HD),
        "w_up": nrm(ks[7], (DEPTH, D, D_FF), D),
        "w_down": nrm(ks[8], (DEPTH, D_FF, D), D_FF),
        "mix_pre_g": gain(ks[9], (DEPTH, D)),
        "mix_post_g": gain(ks[10], (DEPTH, D)),
        "mlp_pre_g": gain(ks[11], (DEPTH, D)),
        "mlp_post_g": gain(ks[12], (DEPTH, D)),
    }

def first_block(x, pool_w, pool_scale, w_q, w_kv, kv_norm_g, w_o, w_up, w_down,
              mix_pre_g, mix_post_g, mlp_pre_g, mlp_post_g):
    B, S, D = x.shape
    HD = N_HEADS * HEAD_DIM
    k = v = None
    for layer in range(DEPTH):
        h = rms_norm(x, mix_pre_g[layer])
        if layer < N_A:
            m = pool_mixer(h, pool_w[layer], pool_scale[layer])
        else:
            j = layer - N_A
            q = jnp.matmul(h, w_q[j]).reshape(B, S, N_HEADS, HEAD_DIM).transpose(0, 2, 1, 3)
            o = stick_breaking_attention(q, k, v)
            m = jnp.matmul(o.transpose(0, 2, 1, 3).reshape(B, S, HD), w_o[j])
        x = x + rms_norm(m, mix_post_g[layer])
        h = rms_norm(x, mlp_pre_g[layer])
        x = x + rms_norm(sq_relu_mlp(h, w_up[layer], w_down[layer]), mlp_post_g[layer])
        if layer == N_A - 1:
            kv = jnp.matmul(rms_norm(x, kv_norm_g), w_kv).reshape(B, S, 2, N_HEADS, HEAD_DIM)
            k = kv[:, :, 0].transpose(0, 2, 1, 3)
            v = kv[:, :, 1].transpose(0, 2, 1, 3)
    return x


DEPTH_2 = 1

D_MIX = D_MODEL
D_CONV = D_MIX // 2
D_ATTN = D_MIX - D_CONV
CONV_WIDTH = 3
CONV_GROUPS = 8
HEAD_DIM_2 = 64
V_DIM = 2 * HEAD_DIM_2
N_HEADS_2 = D_ATTN // V_DIM
Q_WIDTH = N_HEADS_2 * 2 * HEAD_DIM_2
D_IN = 3 * D_CONV + 2 * Q_WIDTH + N_HEADS_2 * V_DIM
N_EXPERT_GROUPS = 4
EXPERTS_PER_GROUP = 8
TOP_K = 2
D_EXPERT = D_MODEL // 2


def rms_norm_2(x, g):
    xf = x.astype(jnp.float32)
    y = xf * lax.rsqrt(jnp.mean(xf * xf, axis=-1, keepdims=True) + EPS)
    return (y * g.astype(jnp.float32)).astype(x.dtype)

def lambda_init(layer_idx):
    return 0.8 - 0.6 * math.exp(-0.3 * layer_idx)

def causal_depthwise_conv(u, w):
    K = w.shape[0]
    S = u.shape[1]
    up = jnp.pad(u, ((0, 0), (K - 1, 0), (0, 0)))
    y = up[:, 0:S, :] * w[0]
    for k in range(1, K):
        y = y + up[:, k:k + S, :] * w[k]
    return y

def short_conv_group(xc, b_gate, c_gate, conv_w, conv_out_g):
    y = b_gate * causal_depthwise_conv(c_gate * xc, conv_w)
    Bsz, S, _ = y.shape
    yg = y.reshape(Bsz, S, CONV_GROUPS, D_CONV // CONV_GROUPS)
    yg = rms_norm_2(yg, jnp.ones((D_CONV // CONV_GROUPS,), y.dtype))
    return yg.reshape(Bsz, S, D_CONV) * conv_out_g.astype(y.dtype)

def diff_attention_group(q, k, v, q_norm_g, k_norm_g, lq1, lk1, lq2, lk2, subln_g, lam_init):
    Bsz, S, _ = q.shape
    q = rms_norm_2(q.reshape(Bsz, S, N_HEADS_2, 2, HEAD_DIM_2), q_norm_g) * (HEAD_DIM_2 ** -0.5)
    k = rms_norm_2(k.reshape(Bsz, S, N_HEADS_2, 2, HEAD_DIM_2), k_norm_g)
    v = v.reshape(Bsz, S, N_HEADS_2, V_DIM)
    qT = q.transpose(0, 2, 3, 1, 4)
    kT = k.transpose(0, 2, 3, 1, 4)
    vT = v.transpose(0, 2, 1, 3)
    lam = (jnp.exp(jnp.sum(lq1.astype(jnp.float32) * lk1.astype(jnp.float32)))
           - jnp.exp(jnp.sum(lq2.astype(jnp.float32) * lk2.astype(jnp.float32)))
           + lam_init)
    key_pos = jnp.arange(S)
    n_blocks = S // Q_BLOCK

    def one_block(i):
        start = i * Q_BLOCK
        qb = lax.dynamic_slice_in_dim(qT, start, Q_BLOCK, axis=3)
        s = jnp.einsum('bhcqd,bhckd->bhcqk', qb, kT).astype(jnp.float32)
        q_pos = start + jnp.arange(Q_BLOCK)
        mask = key_pos[None, :] <= q_pos[:, None]
        s = jnp.where(mask, s, -jnp.inf)
        p = jax.nn.softmax(s, axis=-1)
        a = (p[:, :, 0] - lam * p[:, :, 1]).astype(vT.dtype)
        return jnp.einsum('bhqk,bhkv->bqhv', a, vT)

    out = lax.map(one_block, jnp.arange(n_blocks))
    out = out.transpose(1, 0, 2, 3, 4).reshape(Bsz, S, N_HEADS_2, V_DIM)
    out = rms_norm_2(out, subln_g) * (1.0 - lam_init)
    return out.reshape(Bsz, S, D_ATTN)

def hierarchical_moe(h, w_router_group, w_router_expert, w_gate, w_up, w_down):
    T = h.shape[0]
    G, E = N_EXPERT_GROUPS, EXPERTS_PER_GROUP
    p_group = jax.nn.softmax(jnp.einsum('td,dg->tg', h, w_router_group).astype(jnp.float32), axis=-1)
    g_idx = jnp.argmax(p_group, axis=-1)
    g_gate = jnp.max(p_group, axis=-1)
    logits_e = jnp.einsum('td,de->te', h, w_router_expert).astype(jnp.float32).reshape(T, G, E)
    logits_sel = jnp.take_along_axis(logits_e, g_idx[:, None, None], axis=1)[:, 0]
    top_vals, top_idx = lax.top_k(logits_sel, TOP_K)
    top_w = jax.nn.softmax(top_vals, axis=-1)
    exp_w = jnp.sum(jax.nn.one_hot(top_idx, E, dtype=jnp.float32) * top_w[..., None], axis=1)
    comb = (jax.nn.one_hot(g_idx, G, dtype=jnp.float32)[:, :, None]
            * exp_w[:, None, :] * g_gate[:, None, None]).astype(h.dtype)
    y = jnp.zeros_like(h)
    for g in range(G):
        hg = jnp.einsum('td,edf->tef', h, w_gate[g])
        hu = jnp.einsum('td,edf->tef', h, w_up[g])
        act = jax.nn.silu(hg) * hu * comb[:, g, :, None]
        y = y + jnp.einsum('tef,efd->td', act, w_down[g])
    return y

def second_inputs(seed: int = 0) -> dict:
    key = jax.random.key(seed)
    ks = jax.random.split(key, 20)
    f32 = jnp.float32
    G, E, F = N_EXPERT_GROUPS, EXPERTS_PER_GROUP, D_EXPERT

    def nrm(k, shape, scale):
        return jax.random.normal(k, shape, f32) * scale

    return {
        "x": nrm(ks[0], (BATCH, SEQ, D_MODEL), 1.0),
        "attn_norm_g": 1.0 + nrm(ks[1], (DEPTH_2, D_MODEL), 0.02),
        "w_in": nrm(ks[2], (DEPTH_2, D_MODEL, D_IN), D_MODEL ** -0.5),
        "conv_w": nrm(ks[3], (DEPTH_2, CONV_WIDTH, D_CONV), CONV_WIDTH ** -0.5),
        "conv_out_g": 1.0 + nrm(ks[4], (DEPTH_2, D_CONV), 0.02),
        "q_norm_g": 1.0 + nrm(ks[5], (DEPTH_2, HEAD_DIM_2), 0.02),
        "k_norm_g": 1.0 + nrm(ks[6], (DEPTH_2, HEAD_DIM_2), 0.02),
        "lambda_q1": nrm(ks[7], (DEPTH_2, HEAD_DIM_2), 0.1),
        "lambda_k1": nrm(ks[8], (DEPTH_2, HEAD_DIM_2), 0.1),
        "lambda_q2": nrm(ks[9], (DEPTH_2, HEAD_DIM_2), 0.1),
        "lambda_k2": nrm(ks[10], (DEPTH_2, HEAD_DIM_2), 0.1),
        "attn_subln_g": 1.0 + nrm(ks[11], (DEPTH_2, V_DIM), 0.02),
        "w_out": nrm(ks[12], (DEPTH_2, D_MIX, D_MODEL), D_MIX ** -0.5),
        "ffn_norm_g": 1.0 + nrm(ks[13], (DEPTH_2, D_MODEL), 0.02),
        "w_router_group": nrm(ks[14], (DEPTH_2, D_MODEL, G), D_MODEL ** -0.5),
        "w_router_expert": nrm(ks[15], (DEPTH_2, D_MODEL, G * E), D_MODEL ** -0.5),
        "w_exp_gate": nrm(ks[16], (DEPTH_2, G, E, D_MODEL, F), D_MODEL ** -0.5),
        "w_exp_up": nrm(ks[17], (DEPTH_2, G, E, D_MODEL, F), D_MODEL ** -0.5),
        "w_exp_down": nrm(ks[18], (DEPTH_2, G, E, F, D_MODEL), F ** -0.5),
    }

def second_block(x, attn_norm_g, w_in, conv_w, conv_out_g, q_norm_g, k_norm_g,
              lambda_q1, lambda_k1, lambda_q2, lambda_k2, attn_subln_g, w_out,
              ffn_norm_g, w_router_group, w_router_expert, w_exp_gate, w_exp_up, w_exp_down):
    Bsz, S, D = x.shape
    split_points = [D_CONV, 2 * D_CONV, 3 * D_CONV,
                    3 * D_CONV + Q_WIDTH, 3 * D_CONV + 2 * Q_WIDTH]
    h = x
    for l in range(DEPTH_2):
        lam_init = lambda_init(l)
        hn = rms_norm_2(h, attn_norm_g[l])
        proj = jnp.einsum('bsd,de->bse', hn, w_in[l])
        xc, b_gate, c_gate, q, k, v = jnp.split(proj, split_points, axis=-1)
        y_conv = short_conv_group(xc, b_gate, c_gate, conv_w[l], conv_out_g[l])
        y_attn = diff_attention_group(q, k, v, q_norm_g[l], k_norm_g[l],
                                      lambda_q1[l], lambda_k1[l], lambda_q2[l], lambda_k2[l],
                                      attn_subln_g[l], lam_init)
        mix = jnp.concatenate([y_conv, y_attn], axis=-1)
        h = h + jnp.einsum('bse,ed->bsd', mix, w_out[l])
        hn2 = rms_norm_2(h, ffn_norm_g[l]).reshape(Bsz * S, D)
        y_ffn = hierarchical_moe(hn2, w_router_group[l], w_router_expert[l],
                                 w_exp_gate[l], w_exp_up[l], w_exp_down[l])
        h = h + y_ffn.reshape(Bsz, S, D)
    return h


def setup_inputs(seed=0):
    out = dict(first_inputs(seed))
    for name, value in second_inputs(seed + 1).items():
        if name != "x":
            out[name + "_2"] = value
    return out


def reference(
    x, pool_w, pool_scale, w_q, w_kv, kv_norm_g, w_o, w_up, w_down, mix_pre_g, mix_post_g,
    mlp_pre_g, mlp_post_g, attn_norm_g_2, w_in_2, conv_w_2, conv_out_g_2, q_norm_g_2,
    k_norm_g_2, lambda_q1_2, lambda_k1_2, lambda_q2_2, lambda_k2_2, attn_subln_g_2, w_out_2,
    ffn_norm_g_2, w_router_group_2, w_router_expert_2, w_exp_gate_2, w_exp_up_2, w_exp_down_2,
):
    x = first_block(
        x, pool_w, pool_scale, w_q, w_kv, kv_norm_g, w_o, w_up, w_down, mix_pre_g, mix_post_g,
        mlp_pre_g, mlp_post_g,
    )
    return second_block(
        x, attn_norm_g_2, w_in_2, conv_w_2, conv_out_g_2, q_norm_g_2, k_norm_g_2, lambda_q1_2,
        lambda_k1_2, lambda_q2_2, lambda_k2_2, attn_subln_g_2, w_out_2, ffn_norm_g_2,
        w_router_group_2, w_router_expert_2, w_exp_gate_2, w_exp_up_2, w_exp_down_2,
    )


_drawn_inputs = setup_inputs


def setup_inputs(seed=0):
    import zlib

    import numpy as np

    out = dict(_drawn_inputs(seed))
    spreads = {}
    factors = {'attn_norm_g_2': 3.504,
     'conv_out_g_2': 12.953,
     'q_norm_g_2': 7.354,
     'k_norm_g_2': 8.0,
     'lambda_q1_2': 6.329,
     'lambda_k1_2': 5.414,
     'lambda_q2_2': 4.479,
     'lambda_k2_2': 8.0,
     'attn_subln_g_2': 8.0,
     'ffn_norm_g_2': 4.293}
    for name, (base, spread) in spreads.items():
        noise = np.random.default_rng([zlib.crc32(name.encode()), seed]).standard_normal(out[name].shape)
        drawn = base * np.exp(spread * noise) if base else spread * noise
        out[name] = __import__('jax').numpy.asarray(drawn.astype(out[name].dtype))
    for name, factor in factors.items():
        out[name] = (out[name] * factor).astype(out[name].dtype)
    return out
```

```python
from contextlib import ExitStack

import concourse.bass as bass
import numpy as np
from concourse import mybir

P = 128
D = 1024
T = 256
TT = T // P
KD = D // P
FF = 4096
COLS = 512
EPS = 1e-6
NEG = -1e30
HEADS, DH = 16, 64
WINDOWS = (2, 4, 8, 16)
HEADS2, VD = 4, 128
LAM_INIT = 0.2
NG, NE = 4, 8
FE = 512
SLOTS = 32
BATCH = P // SLOTS
GROUPS = NG * NE // BATCH
PASSES = T // SLOTS

RING = 4
CHUNK = 4096
CPB = 12

ALU = mybir.AluOpType
ACT = mybir.ActivationFunctionType
F32 = mybir.dt.float32
I32 = mybir.dt.int32
AX = mybir.AxisListType

C_IDENT, C_NTRI, C_NONE, C_STRICT, C_CAUSAL, C_BEFORE, C_ONES, C_BLOCK, C_IOTA, C_RANK, C_END = (
    0, 128, 256, 384, 512, 640, 768, 896, 1024, 1056, 1064)


def shape_constants():
    i = np.arange(P)
    row, col = i[:, None], i[None, :]
    c = np.zeros((P, C_END), np.float32)
    c[:, C_IDENT:C_IDENT + P] = row == col
    c[:, C_NTRI:C_NTRI + P] = -1.0 * (row >= col)
    c[:, C_NONE:C_NONE + P] = -1.0
    c[:, C_STRICT:C_STRICT + P] = np.where(row >= col, NEG, 0.0)
    c[:, C_CAUSAL:C_CAUSAL + P] = np.where(col > row, NEG, 0.0)
    c[:, C_BEFORE:C_BEFORE + P] = row < col
    c[:, C_ONES:C_ONES + P] = 1.0
    c[:, C_BLOCK:C_BLOCK + P] = (row // 64 == col // 64) / 64.0
    c[:, C_IOTA:C_IOTA + SLOTS] = np.arange(SLOTS)[None, :]
    c[:, C_RANK:C_RANK + NE] = (NE - np.arange(NE))[None, :]
    t = np.arange(T)
    pool = np.zeros((P, len(WINDOWS), TT, T), np.float32)
    for w, win in enumerate(WINDOWS):
        m = ((t[:, None] <= t[None, :]) & (t[:, None] > t[None, :] - win)) / np.minimum(t + 1, win)[None, :]
        m = m - np.eye(T)
        pool[:, w] = m.reshape(TT, P, T).transpose(1, 0, 2)
    return c, pool.reshape(P, -1)


N_POOL = 0
N_MLP = (1, 25)
N_KV = 17
N_WO = 23
N_IN = 41
IN_BANKS = (4, 6, 2, 4, 6)
N_WOUT = 47
N_MOE = 49
PAIRS = RING // 2
PAIR_ITERS = FF // COLS // PAIRS

N_NORMS_PRE = 6


def build(nc, a, out):
    ctx = ExitStack()
    with ctx:
        def sb(name, shape, dt=F32):
            return ctx.enter_context(nc.sbuf_tensor(name, shape, dt))

        def sem(name):
            return ctx.enter_context(nc.semaphore(name))

        ring = sb("ring", [P, RING, CHUNK])
        consts = sb("consts", [P, C_END])
        x = sb("x", [P, TT, D])
        h = sb("h", [P, TT, D])
        hT = sb("hT", [P, KD, T])
        mixT = sb("mixT", [P, KD, T])
        kbuf = sb("kbuf", [P, KD * T])
        qbuf = sb("qbuf", [P, KD * T])
        vbuf = sb("vbuf", [P, TT * D])
        aT = sb("aT", [P, 4, T])
        rT = sb("rT", [P, 4, T])
        mg = sb("mg", [P, TT, D])
        junk = sb("junk", [P, D])
        zero_t = sb("zero_t", [P, COLS])
        gains = sb("gains", [P, 6, KD])
        poolg = sb("poolg", [P, KD])
        rows = sb("rows", [P, 5, D])
        qkg = sb("qkg", [P, 2])
        qg8 = sb("qg8", [P, 1])
        convw = sb("convw", [P, 3, 4])
        convg = sb("convg", [P, 4])
        subg = sb("subg", [P, VD])
        subg8 = sb("subg8", [P, VD])
        lamv = sb("lamv", [P, 4, 64])
        lamj = sb("lamj", [P, 64])
        lam = sb("lam", [P, 8])
        wr = sb("wr", [P, KD, NG + NG * NE])
        ss = sb("ss", [P, 2])
        ms = sb("ms", [P, 2])
        lnv = sb("lnv", [P, 2])
        r0 = sb("r0", [P, 2])
        r1 = sb("r1", [P, 2])
        rstd = sb("rstd", [P, 2])
        att = sb("att", [P, 4, 3, 384])

        ps = ctx.enter_context(nc.psum_tensor("ps", [P, 8, COLS], F32))
        acc = ps[:, 0:4, :].rearrange("p (t b) c -> p t (b c)", t=TT)

        def wk(b):
            return ps[:, 4 + b, :]

        ident = consts[:, C_IDENT:C_IDENT + P]
        ntri = consts[:, C_NTRI:C_NTRI + P]
        nones = consts[:, C_NONE:C_NONE + P]
        strict = consts[:, C_STRICT:C_STRICT + P]
        causal = consts[:, C_CAUSAL:C_CAUSAL + P]
        before = consts[:, C_BEFORE:C_BEFORE + P]
        ones = consts[:, C_ONES:C_ONES + P]
        blockmean = consts[:, C_BLOCK:C_BLOCK + P]
        slot_ids = consts[:, C_IOTA:C_IOTA + SLOTS]
        rank = consts[:, C_RANK:C_RANK + NE]

        poolm = kbuf[:, :].rearrange("p (w s t) -> p w s t", w=4, s=TT)
        kT = kbuf[:, :].rearrange("p (k t) -> p k t", k=KD)
        qT = qbuf[:, :].rearrange("p (k t) -> p k t", k=KD)
        v = vbuf[:, :].rearrange("p (s d) -> p s d", s=TT)
        q2 = qbuf[:, 0:1024]
        q2n = q2.rearrange("p (m t) -> p m t", m=4)
        k2 = qbuf[:, 1024:2048]
        k2n = k2.rearrange("p (m t) -> p m t", m=4)
        sq2 = kbuf[:, 0:1024]
        wms = kbuf[:, 1024:2048]
        wr0 = mg[:, 0, :]
        wr1 = mg[:, 1, :]
        v2 = vbuf[:, 0:1024].rearrange("p (s d) -> p s d", s=TT)
        xc = vbuf[:, 1024:2048].rearrange("p (k t) -> p k t", k=4)
        convu = sb("convu", [P, 4, T + 2])
        convy = sb("convy", [P, 4, T])
        e2 = att[:, 0:2, :, :].rearrange("p a b c -> p (a b c)")[:, 0:1024].rearrange("p (u c s) -> p u c s", u=2, c=2)
        a2 = att[:, 2, :, :].rearrange("p b c -> p (b c)")[:, 0:512].rearrange("p (u s) -> p u s", u=2)
        a2T = att[:, 2, :, :].rearrange("p b c -> p (b c)")[:, 512:1024].rearrange("p (u s) -> p u s", u=2)
        o2 = att[:, 3, :, :].rearrange("p b c -> p (b c)")[:, 0:1024].rearrange("p (s d) -> p s d", s=TT)
        st2 = sb("st2", [P, 2, 8])
        sub = sb("sub", [P, 6, 8])
        small = sb("small", [P, 1024])
        posm = sb("posm", [P, TT, NG * NE])
        comb = sb("comb", [P, TT, NG * NE])
        ind = sb("ind", [P, TT, NG * NE])
        most = sb("most", [P, 1], I32)
        mostf = sb("mostf", [P, 1])
        G = kbuf[:, 0:256].rearrange("p (s c) -> p s c", s=TT)
        Gw = kbuf[:, 256:512].rearrange("p (s c) -> p s c", s=TT)
        S = kbuf[:, 512:768]
        actT = kbuf[:, 1024:1536].rearrange("p (f c) -> p f c", f=4)
        act_e = qbuf[:, 0:512]
        act_d = qbuf[:, 512:1024]
        act_r = qbuf[:, 1024:1536]
        act_t = qbuf[:, 1536:2048]
        xgT = vbuf[:, 0:1024].rearrange("p (k c) -> p k c", k=KD)
        ysb = vbuf[:, 1024:2048]
        act_s = kbuf[:, 1536:2048]
        outsb = mg

        x_loaded = sem("x_loaded")
        early_loaded = sem("early_loaded")
        early_rows = sem("early_rows")
        late_loaded = sem("late_loaded")
        slot_loaded = [sem(f"slot_loaded{i}") for i in range(RING)]
        chunks_used = sem("chunks_used")
        act_order = sem("act_order")
        dve_order = sem("dve_order")
        pe_order = sem("pe_order")
        x_ready = sem("x_ready")
        ss_ready = sem("ss_ready")
        ms_ready = sem("ms_ready")
        r0_ready = sem("r0_ready")
        h_ready = sem("h_ready")
        hT_banks = sem("hT_banks")
        hT_lo = sem("hT_lo")
        hT_hi = sem("hT_hi")
        m_ready = sem("m_ready")
        yT_banks = sem("yT_banks")
        yT_lo = sem("yT_lo")
        yT_hi = sem("yT_hi")
        scaled = sem("scaled")
        up_done = sem("up_done")
        relu_ready = sem("relu_ready")
        sq_ready = sem("sq_ready")
        proj_done = sem("proj_done")
        proj_taken = sem("proj_taken")
        v_taken = sem("v_taken")
        z_done = sem("z_done")
        absz_ready = sem("absz_ready")
        log_ready = sem("log_ready")
        lp_ready = sem("lp_ready")
        arg_done = sem("arg_done")
        prob_ready = sem("prob_ready")
        o_done = sem("o_done")
        oT_ready = sem("oT_ready")
        in_done = sem("in_done")
        raw_ready = sem("raw_ready")
        sq2_ready = sem("sq2_ready")
        ms2_done = sem("ms2_done")
        ms2_ready = sem("ms2_ready")
        rw_ready = sem("rw_ready")
        n2_ready = sem("n2_ready")
        xc_ready = sem("xc_ready")
        v2_ready = sem("v2_ready")
        s2_done = sem("s2_done")
        nm_ready = sem("nm_ready")
        e2_ready = sem("e2_ready")
        a2_ready = sem("a2_ready")
        a2T_done = sem("a2T_done")
        a2T_ready = sem("a2T_ready")
        o2_done = sem("o2_done")
        lam_dots = sem("lam_dots")
        lam_exp = sem("lam_exp")
        o2sq_ready = sem("o2sq_ready")
        subms_ready = sem("subms_ready")
        subr_ready = sem("subr_ready")
        o2n_ready = sem("o2n_ready")
        o2T_done = sem("o2T_done")
        o2T_ready = sem("o2T_ready")
        lg_done = sem("lg_done")
        gd_ready = sem("gd_ready")
        ge_ready = sem("ge_ready")
        dd_ready = sem("dd_ready")
        de_ready = sem("de_ready")
        ind_ready = sem("ind_ready")
        pos_done = sem("pos_done")
        most_ready = sem("most_ready")
        seeded = sem("seeded")
        G_ready = sem("G_ready")
        xg_done = sem("xg_done")
        S_done = sem("S_done")
        S_ready = sem("S_ready")
        xg_lo = sem("xg_lo")
        xg_hi = sem("xg_hi")
        ex_ready = sem("ex_ready")
        act_ready = sem("act_ready")
        actT_done = sem("actT_done")
        actT_ready = sem("actT_ready")
        y_lo = sem("y_lo")
        y_hi = sem("y_hi")
        moe_done = sem("moe_done")
        out_lo = sem("out_lo")
        out_hi = sem("out_hi")
        stored = sem("stored")
        zero_ready = sem("zero_ready")
        conv_gated = sem("conv_gated")
        slots_moved = sem("slots_moved")

        N_LATE = 6 + 3 + 4 + 3 + 2 + 4 + 2
        EARLY = 16 * 2
        EARLY_ROWS = 16 * 3
        LATE = 16 * N_LATE

        block = ctx.enter_context(nc.Block())

        class Order:

            def __init__(self, eng, s):
                self.eng, self.s, self.base, self.n = eng, s, 0, 0

            def __call__(self, ins):
                self.n += 1
                ins.then_inc(self.s, 1)
                self.eng.wait_ge(self.s, self.base + self.n)

        def slot(n):
            return ring[:, n % RING, :]

        def kd_rows(w):
            return w.rearrange("(p k) n -> p k n", k=KD)

        def std_rows(w):
            return w.rearrange("(m p) n -> p m n", p=P)

        def chunk_source(n):
            if n == N_POOL:
                return a["pool_w"][0].rearrange("g (c p) d -> p (g c) d", p=P), 8, 256
            if N_KV <= n < N_KV + 6:
                w, c = [("w_kv", 0), ("w_kv", 1), ("w_q", 0), ("w_q", 1), ("w_kv", 2), ("w_kv", 3)][n - N_KV]
                src = a[w] if w == "w_kv" else a[w][0]
                return kd_rows(src)[:, :, c * COLS:(c + 1) * COLS], KD, COLS
            if N_WO <= n < N_WO + 2:
                return std_rows(a["w_o"][0])[:, 4 * (n - N_WO):4 * (n - N_WO) + 4, :], 4, D
            if N_IN <= n < N_IN + 6:
                c = [3, 4, 0, 2, 1, 5][n - N_IN]
                return kd_rows(a["w_in_2"][0])[:, :, c * COLS:(c + 1) * COLS], KD, COLS
            return std_rows(a["w_out_2"][0])[:, 4 * (n - N_WOUT):4 * (n - N_WOUT) + 4, :], 4, D

        @block.sync
        def _(sp):
            sp.dma_start(x[:, :, :], a["x"][0].rearrange("(s p) d -> p s d", p=P)).then_inc(x_loaded, 16)
            sp.dma_start(consts[:, :], a["consts"]).then_inc(early_loaded, 16)
            sp.dma_start(kbuf[:, :], a["poolm"]).then_inc(early_loaded, 16)

            def load(n, src, m, w):
                if n >= RING:
                    sp.wait_ge(chunks_used, n - RING + 1)
                sp.dma_start(slot(n)[:, 0:m * w].rearrange("p (m w) -> p m w", m=m), src)\
                  .then_inc(slot_loaded[n % RING], 16)

            def mlp(layer):
                up, down = kd_rows(a["w_up"][layer]), std_rows(a["w_down"][layer])
                n0 = N_MLP[layer]

                def turn(i, first):
                    for j in range(2 * PAIRS):
                        n = n0 + j
                        if not first or n >= RING:
                            sp.wait_ge(chunks_used, i * RING + (n - RING + 1))
                        if j % 2 == 0:
                            dst = slot(n).rearrange("p (m w) -> p m w", m=KD)
                            src = up[:, :, bass.ds(i * (PAIRS * COLS) + j // 2 * COLS, COLS)]
                        else:
                            dst = slot(n).rearrange("p (m w) -> p m w", m=4)
                            src = down[:, bass.ds(i * (PAIRS * 4) + j // 2 * 4, 4), :]
                        sp.dma_start(dst, src).then_inc(slot_loaded[n % RING], 16)

                turn(0, True)
                with sp.Fori(1, PAIR_ITERS) as i:
                    turn(i, False)

            load(N_POOL, *chunk_source(N_POOL))
            mlp(0)
            for n in range(N_KV, N_WO + 2):
                load(n, *chunk_source(n))
            mlp(1)
            for n in range(N_IN, N_WOUT + 2):
                load(n, *chunk_source(n))

            gate = a["w_exp_gate_2"][0].rearrange("g e (p k) f -> p (g e) (k f)", k=KD)
            up = a["w_exp_up_2"][0].rearrange("g e (p k) f -> p (g e) (k f)", k=KD)
            down = a["w_exp_down_2"][0].rearrange("g e (m p) d -> m p (g e) d", p=P)

            def experts(g, it):
                for c in range(CPB):
                    n = N_MOE + c
                    sp.wait_ge(chunks_used, it * CPB + (n - RING + 1))
                    dst = slot(n).rearrange("p (j w) -> p j w", j=BATCH)
                    if c < 8:
                        w = gate if c < 4 else up
                        src = w[:, bass.ds(g * BATCH, BATCH), (c % 4) * 1024:(c % 4) * 1024 + 1024]
                    else:
                        src = down[c - 8][:, bass.ds(g * BATCH, BATCH), :]
                    sp.dma_start(dst, src).then_inc(slot_loaded[n % RING], 16)

            with sp.Fori(0, GROUPS) as g:
                experts(g, g)
            sp.wait_ge(most_ready, 1)
            n_most = sp.value_load(most[0:1, 0:1], min_val=0, max_val=T)
            with sp.Fori(1, PASSES) as b:
                with sp.If(n_most > b * SLOTS):
                    with sp.Fori(0, GROUPS) as g:
                        experts(g, b * GROUPS + g)

            sp.wait_ge(out_lo, 1)
            sp.dma_start(out[0, 0:P, :], outsb[:, 0, :]).then_inc(stored, 16)
            sp.wait_ge(out_hi, 1)
            sp.dma_start(out[0, P:T, :], outsb[:, 1, :]).then_inc(stored, 16)
            sp.wait_ge(stored, 32)

        @block.gpsimd
        def _(pool):
            def row(src, n):
                return src.partition_broadcast(n)

            nd = 0
            with nc.allow_non_contiguous_dma(reason="small gain vectors"):
                pool.dma_start(poolg[:, :], a["mix_pre_g"][0].rearrange("(k p) -> p k", p=P)).then_inc(early_rows, 16)
                pool.dma_start(rows[:, 0, :], row(a["pool_scale"][0], P)).then_inc(early_rows, 16)
                pool.dma_start(rows[:, 1, :], row(a["mix_post_g"][0], P)).then_inc(early_rows, 16)
                for i, src in enumerate((a["mlp_pre_g"][0], a["kv_norm_g"], a["mix_pre_g"][1], a["mlp_pre_g"][1],
                                         a["attn_norm_g_2"][0], a["ffn_norm_g_2"][0])):
                    pool.dma_start(gains[:, i, :], src.rearrange("(p k) -> p k", k=KD)).then_inc(late_loaded, 16)
                    nd += 1
                for i, src in ((2, a["mlp_post_g"][0]), (3, a["mix_post_g"][1]), (4, a["mlp_post_g"][1])):
                    pool.dma_start(rows[:, i, :], row(src, P)).then_inc(late_loaded, 16)
                    nd += 1
                for i, src in ((0, a["q_norm_g_2"]), (1, a["k_norm_g_2"])):
                    for c in range(2):
                        pool.dma_start(qkg[64 * c:64 * c + 64, i:i + 1], src.rearrange("a d -> d a")).then_inc(late_loaded, 16)
                        nd += 1
                for i in range(3):
                    pool.dma_start(convw[:, i, :], a["conv_w_2"][0, i].rearrange("(m p) -> p m", p=P)).then_inc(late_loaded, 16)
                    nd += 1
                pool.dma_start(convg[:, :], a["conv_out_g_2"][0].rearrange("(m p) -> p m", p=P)).then_inc(late_loaded, 16)
                pool.dma_start(subg[:, :], row(a["attn_subln_g_2"][0], P)).then_inc(late_loaded, 16)
                nd += 2
                for i, nm in enumerate(("lambda_q1_2", "lambda_k1_2", "lambda_q2_2", "lambda_k2_2")):
                    pool.dma_start(lamv[:, i, :], row(a[nm][0], P)).then_inc(late_loaded, 16)
                    nd += 1
                pool.dma_start(wr[:, :, 0:NG], kd_rows(a["w_router_group_2"][0])).then_inc(late_loaded, 16)
                pool.dma_start(wr[:, :, NG:], kd_rows(a["w_router_expert_2"][0])).then_inc(late_loaded, 16)
                nd += 2
            assert nd == N_LATE


        def mean_squares(pe, mm, i, bank):
            pe.wait_ge(sq2_ready, i + 1)
            for b in range(2):
                last = mm(ps[:, bank + b, :], blockmean, sq2[:, b * COLS:(b + 1) * COLS], start=True, stop=True)
            last.then_inc(ms2_done, 1)

        @block.tensor
        def _(pe):
            mm = nc.tensor.matmul

            def arrived(n, i=0):
                pe.wait_ge(slot_loaded[n % RING], i * 16 + 16 * (n // RING + 1))

            def transposes(turn):
                pe.wait_ge(h_ready, 2 * turn + 4)
                for b in range(4):
                    for k in (2 * b, 2 * b + 1):
                        for s in range(TT):
                            c = (k % 2) * T + s * P
                            last = nc.tensor.transpose(wk(b)[:, c:c + P], h[:, s, k:D:KD], ident)
                    last.then_inc(hT_banks, 1)

            def hT_arrived(turn):
                pe.wait_ge(hT_lo, turn + 1)
                pe.wait_ge(hT_hi, turn + 1)

            pe.wait_ge(early_loaded, EARLY)
            pe.wait_ge(h_ready, 2)
            for b in range(4):
                for k in (2 * b, 2 * b + 1):
                    for s in range(TT):
                        last = mm(wk(b)[:, (k % 2) * T:(k % 2) * T + T], h[:, s, k * P:(k + 1) * P], poolm[:, k // 2, s, :],
                                  start=(s == 0), stop=(s == TT - 1))
                last.then_inc(yT_banks, 1)
            arrived(N_POOL)
            pe.wait_ge(yT_lo, 1)
            pe.wait_ge(yT_hi, 1)
            pw = slot(N_POOL)[:, 0:2048].rearrange("p (m w) -> p m w", m=8)
            for s in range(TT):
                for g in range(4):
                    for c in range(2):
                        last = mm(acc[:, s, 256 * g:256 * g + 256], hT[:, 2 * g + c, s * P:(s + 1) * P], pw[:, 2 * g + c, :],
                                  start=(c == 0), stop=(c == 1))
            last.then_inc(chunks_used, 1)

            def mlp(layer, turn):
                transposes(turn)
                hT_arrived(turn)
                n0 = N_MLP[layer]
                with pe.Fori(0, PAIR_ITERS) as i:
                    for j in range(PAIRS):
                        n = n0 + 2 * j
                        arrived(n, i)
                        wu = slot(n).rearrange("p (k w) -> p k w", k=KD)
                        for f in range(4):
                            for k in range(KD):
                                last = mm(wk(f)[:, 0:T], wu[:, k, f * P:(f + 1) * P], hT[:, k, :],
                                          start=(k == 0), stop=(k == KD - 1))
                            last.then_inc(up_done if f < 3 else chunks_used, 1)
                        arrived(n + 1, i)
                        wd = slot(n + 1).rearrange("p (f w) -> p f w", f=4)
                        for f in range(4):
                            pe.wait_ge(sq_ready, i * (4 * PAIRS) + (32 * layer + 4 * j + f + 1))
                            for s in range(TT):
                                for half in range(2):
                                    last = mm(acc[:, s, half * COLS:(half + 1) * COLS], aT[:, f, s * P:(s + 1) * P],
                                              wd[:, f, half * COLS:(half + 1) * COLS],
                                              start=False, stop=False, skip_group_check=True)
                        last.then_inc(chunks_used, 1)

            def clear_acc():
                for s in range(TT):
                    for half in range(2):
                        mm(acc[:, s, half * COLS:(half + 1) * COLS], zero_t[:, 0:P], zero_t[:, 0:COLS],
                           start=True, stop=True)

            pe.wait_ge(x_ready, 2)
            pe.wait_ge(zero_ready, 1)
            clear_acc()
            mlp(0, 0)

            transposes(1)
            hT_arrived(1)
            for i in range(4):
                n = N_KV + i
                arrived(n)
                w = slot(n).rearrange("p (k w) -> p k w", k=KD)
                src = hT if i < 2 else mixT
                for f in range(4):
                    t = 4 * i + f
                    if t >= 4:
                        pe.wait_ge(proj_taken, t - 3)
                    for k in range(KD):
                        last = mm(wk(f)[:, 0:T], w[:, k, f * P:(f + 1) * P], src[:, k, :], start=(k == 0), stop=(k == KD - 1))
                    last.then_inc(proj_done if f < 3 else chunks_used, 1)
            for i in range(2):
                n = N_KV + 4 + i
                arrived(n)
                w = slot(n).rearrange("p (k w) -> p k w", k=KD)
                for s in range(TT):
                    for k in range(KD):
                        last = mm(acc[:, s, i * COLS:(i + 1) * COLS], hT[:, k, s * P:(s + 1) * P], w[:, k, :],
                                  start=(k == 0), stop=(k == KD - 1))
                last.then_inc(chunks_used, 1)

            def zbank(i):
                return ps[:, i % 6, :]

            def scores(i):
                r, m = 64 * (i % 2), i // 2
                z = zbank(i)
                mm(z[:, 0:T], kT[r:r + 64, m, 0:P], qT[r:r + 64, m, :], start=True, stop=False, skip_group_check=True)
                mm(z[:, 0:P], ident, strict, start=False, stop=False, skip_group_check=True)
                mm(z[:, T:T + P], kT[r:r + 64, m, P:T], qT[r:r + 64, m, P:T], start=False, stop=False, skip_group_check=True)
                mm(z[:, T:T + P], ident, strict, start=False, stop=True, skip_group_check=True).then_inc(z_done, 1)

            def args(i):
                z, lp = zbank(i), att[:, 2, i % 3, :]
                pe.wait_ge(lp_ready, i + 1)
                mm(z[:, 0:T], ntri, lp[:, 0:T], start=False, stop=False, skip_group_check=True)
                mm(z[:, P:T], nones, lp[:, T:T + P], start=False, stop=False, skip_group_check=True)
                mm(z[:, T:T + P], ntri, lp[:, T:T + P], start=False, stop=True, skip_group_check=True).then_inc(arg_done, 1)

            def weighted(i):
                r, m = 64 * (i % 2), i // 2
                p = att[:, 3, i % 3, :]
                o = wk(2 + m % 2)[r:r + 64, 0:T]
                pe.wait_ge(prob_ready, i + 1)
                if m >= 2 and i % 2 == 0:
                    pe.wait_ge(oT_ready, m - 1)
                mm(o, v[:, 0, i * DH:(i + 1) * DH], p[:, 0:T], start=True, stop=False, skip_group_check=True)
                last = mm(o[:, P:T], v[:, 1, i * DH:(i + 1) * DH], p[:, T:T + P], start=False, stop=True, skip_group_check=True)
                if i % 2:
                    last.then_inc(o_done, 1)

            pe.wait_ge(proj_taken, 16)
            pe.wait_ge(v_taken, 4)
            for i in range(HEADS + 3):
                if i < HEADS:
                    if i >= 6:
                        pe.wait_ge(prob_ready, i - 5)
                    scores(i)
                if 2 <= i < HEADS + 2:
                    args(i - 2)
                if i >= 3:
                    weighted(i - 3)

            def project(n0):
                for i in range(2):
                    arrived(n0 + i)
                    w = slot(n0 + i).rearrange("p (m w) -> p m w", m=4)
                    for m in range(4):
                        for s in range(TT):
                            for half in range(2):
                                last = mm(acc[:, s, half * COLS:(half + 1) * COLS], mixT[:, 4 * i + m, s * P:(s + 1) * P],
                                          w[:, m, half * COLS:(half + 1) * COLS],
                                          start=(i == 0 and m == 0), stop=(i == 1 and m == 3))
                    last.then_inc(chunks_used, 1)

            pe.wait_ge(oT_ready, 8)
            project(N_WO)
            pe.wait_ge(x_ready, 6)
            clear_acc()
            mlp(1, 2)

            transposes(3)
            hT_arrived(3)
            for i in range(5):
                n = N_IN + i
                arrived(n)
                w = slot(n).rearrange("p (k w) -> p k w", k=KD)
                b0 = IN_BANKS[i]
                if i == 3:
                    pe.wait_ge(n2_ready, 1)
                if i == 4:
                    pe.wait_ge(n2_ready, 2)
                for f in range(4):
                    for k in range(KD):
                        last = mm(ps[:, b0 + f // 2, (f % 2) * T:(f % 2) * T + T], w[:, k, f * P:(f + 1) * P], hT[:, k, :],
                                  start=(k == 0), stop=(k == KD - 1))
                last.then_inc(chunks_used, 1)
                if 1 <= i <= 2:
                    mean_squares(pe, mm, i - 1, 4 + 2 * (i - 1))
            arrived(N_IN + 5)
            w = slot(N_IN + 5).rearrange("p (k w) -> p k w", k=KD)
            for s in range(TT):
                for k in range(KD):
                    last = mm(ps[:, s, :], hT[:, k, s * P:(s + 1) * P], w[:, k, :], start=(k == 0), stop=(k == KD - 1))
            last.then_inc(chunks_used, 1)
            mean_squares(pe, mm, 2, 2)

            def scores2(u):
                s, hd = u // 4, u % 4
                nk = (s + 1) * P
                for c in range(2):
                    mm(wk(2 * (u % 2) + c)[:, 0:nk], q2n[64 * c:64 * c + 64, hd, s * P:(s + 1) * P],
                       k2n[64 * c:64 * c + 64, hd, 0:nk], start=True, stop=False)
                for c in range(2):
                    last = mm(wk(2 * (u % 2) + c)[:, s * P:nk], ident, causal, start=False, stop=True)
                last.then_inc(s2_done, 1)

            def turn2(u):
                s = u // 4
                pe.wait_ge(a2_ready, u + 1)
                if u >= 2:
                    pe.wait_ge(a2T_ready, u - 1)
                for b in range(s + 1):
                    last = nc.tensor.transpose(ps[:, 2 + u % 2, b * P:(b + 1) * P], a2[:, u % 2, b * P:(b + 1) * P], ident)
                last.then_inc(a2T_done, 1)

            def out2(u):
                s, hd = u // 4, u % 4
                pe.wait_ge(a2T_ready, u + 1)
                for b in range(s + 1):
                    last = mm(ps[:, s, hd * VD:(hd + 1) * VD], a2T[:, u % 2, b * P:(b + 1) * P],
                              v2[:, b, hd * VD:(hd + 1) * VD], start=(b == 0), stop=(b == s))
                if hd == 3:
                    last.then_inc(o2_done, 1)

            pe.wait_ge(conv_gated, 1)
            pe.wait_ge(v2_ready, 2)
            pe.wait_ge(ms2_ready, 3)
            for u in range(8 + 2):
                if u < 8:
                    if u >= 2:
                        pe.wait_ge(e2_ready, 2 * (u - 1))
                    scores2(u)
                if 1 <= u < 9:
                    turn2(u - 1)
                if u >= 2:
                    out2(u - 2)
            for s in range(TT):
                pe.wait_ge(o2n_ready, s + 1)
                for hd in range(4):
                    last = nc.tensor.transpose(wk(s)[:, hd * P:(hd + 1) * P], o2[:, s, hd * VD:(hd + 1) * VD], ident)
                last.then_inc(o2T_done, 1)
            pe.wait_ge(o2T_ready, 2)
            pe.wait_ge(n2_ready, 3)
            project(N_WOUT)

            transposes(4)
            hT_arrived(4)
            pe.wait_ge(late_loaded, LATE)
            for s in range(TT):
                for k in range(KD):
                    last = mm(wk(0)[:, 64 * s:64 * s + 36], hT[:, k, s * P:(s + 1) * P], wr[:, k, :],
                              start=(k == 0), stop=(k == KD - 1))
            last.then_inc(lg_done, 1)
            for s in range(TT):
                for half in range(2):
                    mm(acc[:, s, half * COLS:(half + 1) * COLS], ident, x[:, s, half * COLS:(half + 1) * COLS],
                       start=True, stop=True)
            pe.wait_ge(ind_ready, 1)
            mm(wk(1)[:, 0:32], before, ind[:, 0, :], start=True, stop=True)
            mm(wk(1)[:, 64:96], ones, ind[:, 0, :], start=True, stop=False)
            mm(wk(1)[:, 64:96], before, ind[:, 1, :], start=False, stop=True)
            mm(wk(1)[:, 128:160], ones, ind[:, 0, :], start=True, stop=False)
            mm(wk(1)[:, 128:160], ones, ind[:, 1, :], start=False, stop=True).then_inc(pos_done, 1)

            def experts(it):
                pe.wait_ge(G_ready, it + 1)
                for k in range(KD):
                    for s in range(TT):
                        last = mm(wk(2 + k // 4)[:, (k % 4) * P:(k % 4 + 1) * P], h[:, s, k:D:KD], G[:, s, :],
                                  start=(s == 0), stop=(s == TT - 1))
                    if k % 4 == 3:
                        last.then_inc(xg_done, 1)
                for s in range(TT):
                    last = nc.tensor.transpose(wk(0)[:, s * P:(s + 1) * P], Gw[:, s, :], ident)
                last.then_inc(S_done, 1)
                pe.wait_ge(xg_lo, it + 1)
                pe.wait_ge(xg_hi, it + 1)
                pe.wait_ge(S_ready, it + 1)
                for c in range(8):
                    arrived(N_MOE + c, it * (CPB // RING))
                    w = slot(N_MOE + c).rearrange("p (j k f) -> p j k f", j=BATCH, k=2)
                    for kk in range(2):
                        k = 2 * (c % 4) + kk
                        for j in range(BATCH):
                            q = slice(SLOTS * j, SLOTS * (j + 1))
                            last = mm(wk(c // 4)[q, :], xgT[:, k, q], w[:, j, kk, :], start=(k == 0), stop=(k == KD - 1))
                    last.then_inc(chunks_used, 1)
                pe.wait_ge(act_ready, it + 1)
                for f in range(4):
                    last = nc.tensor.transpose(wk(1)[:, f * P:(f + 1) * P], act_s[:, f * P:(f + 1) * P], ident)
                last.then_inc(actT_done, 1)
                pe.wait_ge(actT_ready, it + 1)
                for f in range(4):
                    arrived(N_MOE + 8 + f, it * (CPB // RING))
                    w = slot(N_MOE + 8 + f).rearrange("p (j d) -> p j d", j=BATCH)
                    for half in range(2):
                        for j in range(BATCH):
                            q = slice(SLOTS * j, SLOTS * (j + 1))
                            last = mm(wk(2 + half)[q, :], actT[:, f, q], w[:, j, half * COLS:(half + 1) * COLS],
                                      start=(f == 0), stop=(f == 3))
                    last.then_inc(chunks_used, 1)
                pe.wait_ge(y_lo, it + 1)
                pe.wait_ge(y_hi, it + 1)
                for s in range(TT):
                    for half in range(2):
                        last = mm(acc[:, s, half * COLS:(half + 1) * COLS], S[:, s * P:(s + 1) * P],
                                  ysb[:, half * COLS:(half + 1) * COLS], start=False, stop=False, skip_group_check=True)

            pe.wait_ge(most_ready, 1)
            n_most = pe.value_load(most[0:1, 0:1], min_val=0, max_val=T)
            with pe.Fori(0, GROUPS) as g:
                experts(g)
            with pe.Fori(1, PASSES) as b:
                with pe.If(n_most > b * SLOTS):
                    with pe.Fori(0, GROUPS) as g:
                        experts(b * GROUPS + g)
            mm(acc[:, 1, COLS:D], zero_t[:, 0:P], zero_t[:, 0:COLS], start=False, stop=True,
               skip_group_check=True).then_inc(moe_done, 1)

        @block.scalar
        def _(act):
            order = Order(act, act_order)
            fn = nc.scalar.activation

            def sum_squares(src, s):
                fn(junk[:, :], src, ACT.Square, accum_out=ss[:, s:s + 1]).then_inc(ss_ready, 1)
                act.wait_ge(ss_ready, turns[0] * 2 + s + 1)

            turns = [0]

            def rsqrt():
                act.wait_ge(ms_ready, turns[0] + 1)
                order(fn(lnv[:, :], ms[:, :], ACT.Ln))
                fn(r0[:, :], lnv[:, :], ACT.Exp, scale=-0.5).then_inc(r0_ready, 1)
                turns[0] += 1

            def pre_norm(x_count):
                for s in range(TT):
                    act.wait_ge(x_ready, x_count - 1 + s) if x_count else act.wait_ge(x_loaded, 16)
                    sum_squares(x[:, s, :], s)
                rsqrt()

            def post_norm(wait):
                wait()
                for s in range(TT):
                    sum_squares(acc[:, s, :], s)
                rsqrt()

            def take_hT(turn, gain, dst=hT):
                for k in range(4):
                    if k % 2 == 0:
                        act.wait_ge(hT_banks, 4 * turn + k // 2 + 1)
                    last = fn(dst[:, k, :], wk(k // 2)[:, (k % 2) * T:(k % 2) * T + T], ACT.Copy, scale=gains[:, gain, k:k + 1])
                return last

            act.preload_act_table_set("natural_log_exp_and_others")
            pre_norm(0)
            act.wait_ge(early_loaded, EARLY)
            act.wait_ge(early_rows, EARLY_ROWS)
            for k in range(4):
                if k % 2 == 0:
                    act.wait_ge(yT_banks, k // 2 + 1)
                last = fn(hT[:, k, :], wk(k // 2)[:, (k % 2) * T:(k % 2) * T + T], ACT.Copy, scale=poolg[:, k:k + 1])
            last.then_inc(yT_lo, 1)
            for s in range(TT):
                act.wait_ge(scaled, s + 1)
                sum_squares(mg[:, s, :], s)
            rsqrt()
            act.wait_ge(late_loaded, LATE)

            def mlp(layer, turn, x_count):
                pre_norm(x_count)
                take_hT(turn, 0 if layer == 0 else 3).then_inc(hT_lo, 1)
                n0 = N_MLP[layer]
                with act.Fori(0, PAIR_ITERS) as i:
                    for j in range(PAIRS):
                        for f in range(4):
                            if f < 3:
                                act.wait_ge(up_done, i * (3 * PAIRS) + (24 * layer + 3 * j + f + 1))
                            else:
                                act.wait_ge(chunks_used, i * RING + (n0 + 2 * j + 1))
                            fn(rT[:, f, :], wk(f)[:, 0:T], ACT.Relu).then_inc(relu_ready, 1)
                post_norm(lambda: act.wait_ge(chunks_used, n0 + 16))

            mlp(0, 0, 2)

            pre_norm(4)
            take_hT(1, 1)
            take_hT(1, 2, mixT).then_inc(hT_lo, 1)
            for t in range(16):
                i, f = t // 4, t % 4
                if f < 3:
                    act.wait_ge(proj_done, 3 * i + f + 1)
                else:
                    act.wait_ge(chunks_used, N_KV + i + 1)
                if i < 2:
                    fn(kT[:, t, :], wk(f)[:, 0:T], ACT.Copy).then_inc(proj_taken, 1)
                else:
                    fn(qT[:, t - 8, :], wk(f)[:, 0:T], ACT.Copy, scale=DH ** -0.5).then_inc(proj_taken, 1)

            for i in range(HEADS + 2):
                if i < HEADS:
                    act.wait_ge(absz_ready, i + 1)
                    order(fn(att[:, 1, i % 3, :], att[:, 0, i % 3, :], ACT.Exp))
                    fn(att[:, 1, i % 3, :], att[:, 1, i % 3, :], ACT.Ln, bias=1.0).then_inc(log_ready, 1)
                if i >= 2:
                    act.wait_ge(arg_done, i - 1)
                    fn(att[:, 3, (i - 2) % 3, :], ps[:, (i - 2) % 6, 0:384], ACT.Exp).then_inc(prob_ready, 1)
            post_norm(lambda: act.wait_ge(chunks_used, N_WO + 2))
            mlp(1, 2, 6)

            pre_norm(8)
            take_hT(3, 4).then_inc(hT_lo, 1)
            act.wait_ge(lam_dots, 1)
            fn(lam[:, 2:4], lam[:, 0:2], ACT.Exp).then_inc(lam_exp, 1)

            def wide_rsqrt(i):
                act.wait_ge(ms2_ready, i + 1)
                order(fn(wr0, wms, ACT.Ln))
                fn(wr0, wr0, ACT.Exp, scale=-0.5).then_inc(rw_ready, 1)

            for i in range(2):
                act.wait_ge(raw_ready, i + 1)
                fn(sq2, (q2, k2)[i], ACT.Square).then_inc(sq2_ready, 1)
                if i == 0:
                    wide_rsqrt(0)
                else:
                    act.wait_ge(chunks_used, N_IN + 3)
                    fn(xc.rearrange("p k t -> p (k t)"), ps[:, 2:4, :].rearrange("p b c -> p (b c)"), ACT.Copy).then_inc(xc_ready, 1)
                    wide_rsqrt(1)
            act.wait_ge(conv_gated, 1)
            fn(sq2, convy[:, :, :].rearrange("p k t -> p (k t)"), ACT.Square).then_inc(sq2_ready, 1)
            for s in range(TT):
                act.wait_ge(chunks_used, N_IN + 6)
                fn(v2[:, s, :], ps[:, s, :], ACT.Copy).then_inc(v2_ready, 1)
            wide_rsqrt(2)

            for u in range(8 + 1):
                if u < 8:
                    s = u // 4
                    nk = (s + 1) * P
                    act.wait_ge(nm_ready, u + 1)
                    for c in range(2):
                        fn(e2[:, u % 2, c, 0:nk], wk(2 * (u % 2) + c)[:, 0:nk], ACT.Exp, bias=st2[:, u % 2, c:c + 1],
                           accum_out=st2[:, u % 2, 2 + c:3 + c]).then_inc(e2_ready, 1)
                if u >= 1:
                    s = (u - 1) // 4
                    act.wait_ge(a2T_done, u)
                    fn(a2T[:, (u - 1) % 2, 0:(s + 1) * P], ps[:, 2 + (u - 1) % 2, 0:(s + 1) * P], ACT.Copy).then_inc(a2T_ready, 1)
            for s in range(TT):
                act.wait_ge(o2_done, s + 1)
                fn(sq2[:, s * COLS:(s + 1) * COLS], ps[:, s, :], ACT.Square).then_inc(o2sq_ready, 1)
            act.wait_ge(subms_ready, 1)
            order(fn(sub[:, 2, :], sub[:, 1, :], ACT.Ln))
            fn(sub[:, 3, :], sub[:, 2, :], ACT.Exp, scale=-0.5).then_inc(subr_ready, 1)
            for s in range(TT):
                act.wait_ge(o2T_done, s + 1)
                fn(mixT[:, 4:8, s * P:(s + 1) * P], wk(s).rearrange("p (m t) -> p m t", m=4), ACT.Copy).then_inc(o2T_ready, 1)

            pre_norm(10)
            take_hT(4, 5).then_inc(hT_lo, 1)
            act.wait_ge(gd_ready, 1)
            fn(small[:, 16:24], small[:, 8:16], ACT.Exp).then_inc(ge_ready, 1)
            act.wait_ge(dd_ready, 1)
            fn(small[:, 26:28], small[:, 24:26], ACT.Exp).then_inc(de_ready, 1)

            def experts(it):
                act.wait_ge(xg_done, it * 2 + 1)
                for k in range(4):
                    last = fn(xgT[:, k, :], wk(2)[:, k * P:(k + 1) * P], ACT.Copy, scale=gains[:, 5, k:k + 1])
                last.then_inc(xg_lo, 1)
                act.wait_ge(S_done, it + 1)
                fn(S, wk(0)[:, 0:T], ACT.Copy).then_inc(S_ready, 1)
                act.wait_ge(chunks_used, it * CPB + (N_MOE + 4))
                fn(act_e, wk(0), ACT.Exp, scale=-1.0).then_inc(ex_ready, 1)
                act.wait_ge(actT_done, it + 1)
                fn(actT.rearrange("p f c -> p (f c)"), wk(1), ACT.Copy).then_inc(actT_ready, 1)
                act.wait_ge(chunks_used, it * CPB + (N_MOE + 12))
                fn(ysb[:, 0:COLS], wk(2), ACT.Copy).then_inc(y_lo, 1)

            act.wait_ge(most_ready, 1)
            n_most = act.value_load(most[0:1, 0:1], min_val=0, max_val=T)
            with act.Fori(0, GROUPS) as g:
                experts(g)
            with act.Fori(1, PASSES) as b:
                with act.If(n_most > b * SLOTS):
                    with act.Fori(0, GROUPS) as g:
                        experts(b * GROUPS + g)
            act.wait_ge(moe_done, 1)
            fn(outsb[:, 0, :], acc[:, 0, :], ACT.Copy).then_inc(out_lo, 1)

        @block.vector
        def _(dve):
            order = Order(dve, dve_order)
            ve = nc.vector
            turns = [0]
            xs = [0]

            def rsqrt():
                i = turns[0]
                dve.wait_ge(ss_ready, 2 * i + 2)
                ve.tensor_scalar(ms[:, :], ss[:, :], 1.0 / D, EPS, ALU.mult, ALU.add).then_inc(ms_ready, 1)
                dve.wait_ge(r0_ready, i + 1)
                order(ve.tensor_tensor(r1[:, :], r0[:, :], r0[:, :], ALU.mult))
                order(ve.scalar_tensor_tensor(r1[:, :], r1[:, :], -0.5, ms[:, :], ALU.mult, ALU.mult))
                order(ve.scalar_tensor_tensor(rstd[:, :], r1[:, :], 1.5, r0[:, :], ALU.add, ALU.mult))
                turns[0] += 1

            def normalise():
                rsqrt()
                for s in range(TT):
                    ve.tensor_scalar(h[:, s, :], x[:, s, :], rstd[:, s:s + 1], None, ALU.mult).then_inc(h_ready, 1)

            def add_to_x():
                rsqrt()
                for s in range(TT):
                    ve.scalar_tensor_tensor(x[:, s, :], mg[:, s, :], rstd[:, s:s + 1], x[:, s, :], ALU.mult, ALU.add)\
                      .then_inc(x_ready, 1)
                xs[0] += 2
                dve.wait_ge(x_ready, xs[0])

            def post_norm(row):
                for s in range(TT):
                    dve.wait_ge(ss_ready, 2 * turns[0] + s + 1)
                    order(ve.tensor_tensor(mg[:, s, :], acc[:, s, :], rows[:, row, :], ALU.mult))
                add_to_x()

            def take_hT(turn, gain, dst=hT):
                for k in range(4, 8):
                    if k % 2 == 0:
                        dve.wait_ge(hT_banks, 4 * turn + k // 2 + 1)
                    last = ve.tensor_scalar(dst[:, k, :], wk(k // 2)[:, (k % 2) * T:(k % 2) * T + T],
                                            gains[:, gain, k:k + 1], None, ALU.mult)
                return last

            ve.memset(zero_t[:, :], 0.0).then_inc(zero_ready, 1)
            dve.wait_ge(x_loaded, 16)
            normalise()
            dve.wait_ge(early_loaded, EARLY)
            dve.wait_ge(early_rows, EARLY_ROWS)
            for k in range(4, 8):
                if k % 2 == 0:
                    dve.wait_ge(yT_banks, k // 2 + 1)
                last = ve.tensor_scalar(hT[:, k, :], wk(k // 2)[:, (k % 2) * T:(k % 2) * T + T], poolg[:, k:k + 1], None, ALU.mult)
            last.then_inc(yT_hi, 1)
            dve.wait_ge(chunks_used, 1)
            for s in range(TT):
                ve.tensor_tensor(mg[:, s, :], acc[:, s, :], rows[:, 0, :], ALU.mult).then_inc(scaled, 1)
            for s in range(TT):
                dve.wait_ge(ss_ready, 2 * turns[0] + s + 1)
                order(ve.tensor_tensor(mg[:, s, :], mg[:, s, :], rows[:, 1, :], ALU.mult))
            add_to_x()
            dve.wait_ge(late_loaded, LATE)

            def mlp(layer, turn):
                normalise()
                take_hT(turn, 0 if layer == 0 else 3).then_inc(hT_hi, 1)
                with dve.Fori(0, PAIR_ITERS) as i:
                    for j in range(PAIRS):
                        for f in range(4):
                            dve.wait_ge(relu_ready, i * (4 * PAIRS) + (32 * layer + 4 * j + f + 1))
                            ve.tensor_tensor(aT[:, f, :], rT[:, f, :], rT[:, f, :], ALU.mult).then_inc(sq_ready, 1)
                post_norm(2 if layer == 0 else 4)

            mlp(0, 0)

            normalise()
            take_hT(1, 1)
            take_hT(1, 2, mixT).then_inc(hT_hi, 1)
            for i in range(2):
                dve.wait_ge(chunks_used, N_KV + 5 + i)
                for s in range(TT):
                    ve.tensor_copy(v[:, s, i * COLS:(i + 1) * COLS], acc[:, s, i * COLS:(i + 1) * COLS]).then_inc(v_taken, 1)

            for i in range(HEADS + 4):
                if i < HEADS:
                    dve.wait_ge(z_done, i + 1)
                    order(ve.tensor_scalar(att[:, 2, i % 3, :], ps[:, i % 6, 0:384], 0.0, None, ALU.max))
                    ve.scalar_tensor_tensor(att[:, 0, i % 3, :], att[:, 2, i % 3, :], -2.0, ps[:, i % 6, 0:384],
                                            ALU.mult, ALU.add).then_inc(absz_ready, 1)
                if 1 <= i <= HEADS:
                    dve.wait_ge(log_ready, i)
                    ve.tensor_tensor(att[:, 2, (i - 1) % 3, :], att[:, 2, (i - 1) % 3, :], att[:, 1, (i - 1) % 3, :],
                                     ALU.add).then_inc(lp_ready, 1)
                if i >= 4 and i % 2 == 0:
                    m = (i - 4) // 2
                    dve.wait_ge(o_done, m + 1)
                    ve.tensor_copy(mixT[:, m, :], wk(2 + m % 2)[:, 0:T]).then_inc(oT_ready, 1)
            post_norm(3)
            mlp(1, 2)

            normalise()
            take_hT(3, 4).then_inc(hT_hi, 1)
            for c in range(2):
                order(ve.tensor_tensor(lamj[:, :], lamv[:, 2 * c, :], lamv[:, 2 * c + 1, :], ALU.mult))
                order(ve.tensor_reduce(lam[:, c:c + 1], lamj[:, :], AX.X, ALU.add))
            order(ve.tensor_scalar(qg8[:, :], qkg[:, 0:1], DH ** -0.5, None, ALU.mult))
            order(ve.tensor_scalar(subg8[:, :], subg[:, :], 1.0 - LAM_INIT, None, ALU.mult))
            ve.memset(convu[:, :, 0:2], 0.0).then_inc(lam_dots, 1)
            dve.wait_ge(lam_exp, 1)
            dve.wait_ge(lam_dots, 1)
            order(ve.tensor_tensor(lam[:, 4:5], lam[:, 3:4], lam[:, 2:3], ALU.subtract))
            order(ve.tensor_scalar(lam[:, 5:6], lam[:, 4:5], -LAM_INIT, None, ALU.add))

            def wide_rsqrt(i, bank):
                dve.wait_ge(ms2_done, i + 1)
                ve.tensor_scalar(wms, ps[:, bank:bank + 2, :].rearrange("p b c -> p (b c)"), 1.0, EPS, ALU.mult, ALU.add)\
                  .then_inc(ms2_ready, 1)
                dve.wait_ge(rw_ready, i + 1)
                order(ve.tensor_tensor(wr1, wr0, wr0, ALU.mult))
                order(ve.scalar_tensor_tensor(wr1, wr1, -0.5, wms, ALU.mult, ALU.mult))
                order(ve.scalar_tensor_tensor(wr1, wr1, 1.5, wr0, ALU.add, ALU.mult))

            def raw(i):
                dve.wait_ge(chunks_used, N_IN + 1 + i)
                ve.tensor_copy((q2, k2)[i], ps[:, 4 + 2 * i:6 + 2 * i, :].rearrange("p b c -> p (b c)")).then_inc(raw_ready, 1)

            for i in range(2):
                raw(i)
                wide_rsqrt(i, 4 + 2 * i)
                q = (q2, k2)[i]
                ve.scalar_tensor_tensor(q, q, (qg8[:, :], qkg[:, 1:2])[i], wr1, ALU.mult, ALU.mult).then_inc(n2_ready, 1)
            dve.wait_ge(xc_ready, 1)
            dve.wait_ge(chunks_used, N_IN + 4)
            order(ve.tensor_tensor(convu[:, :, 2:], ps[:, 4:6, :].rearrange("p b (k t) -> p (b k) t", k=2), xc, ALU.mult))
            for tap in (2, 1, 0):
                for m in range(4):
                    u = convu[:, m, tap:tap + T]
                    if tap == 2:
                        last = ve.tensor_scalar(convy[:, m, :], u, convw[:, tap, m:m + 1], None, ALU.mult)
                    else:
                        last = ve.scalar_tensor_tensor(convy[:, m, :], u, convw[:, tap, m:m + 1], convy[:, m, :], ALU.mult, ALU.add)
                    last.then_inc(dve_order, 1)
                    order.n += 1
                dve.wait_ge(dve_order, order.n)
            dve.wait_ge(chunks_used, N_IN + 5)
            ve.tensor_tensor(convy[:, :, :], ps[:, 6:8, :].rearrange("p b (k t) -> p (b k) t", k=2), convy[:, :, :], ALU.mult)\
              .then_inc(conv_gated, 1)
            dve.wait_ge(conv_gated, 1)
            wide_rsqrt(2, 2)
            for m in range(4):
                last = ve.scalar_tensor_tensor(mixT[:, m, :], convy[:, m, :], convg[:, m:m + 1], wr1[:, m * T:(m + 1) * T],
                                               ALU.mult, ALU.mult)
            last.then_inc(n2_ready, 1)

            for u in range(8 + 1):
                if u < 8:
                    nk = (u // 4 + 1) * P
                    dve.wait_ge(s2_done, u + 1)
                    ve.tensor_reduce(st2[:, u % 2, 0:2], ps[:, 4 + 2 * (u % 2):6 + 2 * (u % 2), 0:nk], AX.X, ALU.max,
                                     negate=True).then_inc(nm_ready, 1)
                if u >= 1:
                    w = u - 1
                    b, nk = w % 2, (w // 4 + 1) * P
                    dve.wait_ge(e2_ready, 2 * w + 2)
                    order(ve.reciprocal(st2[:, b, 4:6], st2[:, b, 2:4]))
                    order(ve.tensor_tensor(st2[:, b, 6:7], st2[:, b, 5:6], lam[:, 5:6], ALU.mult))
                    order(ve.tensor_scalar(e2[:, b, 0, 0:nk], e2[:, b, 0, 0:nk], st2[:, b, 4:5], None, ALU.mult))
                    ve.scalar_tensor_tensor(a2[:, b, 0:nk], e2[:, b, 1, 0:nk], st2[:, b, 6:7], e2[:, b, 0, 0:nk],
                                            ALU.mult, ALU.add).then_inc(a2_ready, 1)
            for s in range(TT):
                dve.wait_ge(o2sq_ready, s + 1)
                order(ve.tensor_reduce(sub[:, 0, 4 * s:4 * s + 4], sq2[:, s * COLS:(s + 1) * COLS].rearrange("p (m d) -> p m d", m=4),
                                       AX.X, ALU.add))
            ve.tensor_scalar(sub[:, 1, :], sub[:, 0, :], 1.0 / VD, EPS, ALU.mult, ALU.add).then_inc(subms_ready, 1)
            dve.wait_ge(subr_ready, 1)
            order(ve.tensor_tensor(sub[:, 4, :], sub[:, 3, :], sub[:, 3, :], ALU.mult))
            order(ve.scalar_tensor_tensor(sub[:, 4, :], sub[:, 4, :], -0.5, sub[:, 1, :], ALU.mult, ALU.mult))
            order(ve.scalar_tensor_tensor(sub[:, 5, :], sub[:, 4, :], 1.5, sub[:, 3, :], ALU.add, ALU.mult))
            for s in range(TT):
                for m in range(4):
                    last = ve.scalar_tensor_tensor(o2[:, s, m * VD:(m + 1) * VD], ps[:, s, m * VD:(m + 1) * VD],
                                                   sub[:, 5, 4 * s + m:4 * s + m + 1], subg8[:, :], ALU.mult, ALU.mult)
                last.then_inc(o2n_ready, 1)
            dve.wait_ge(chunks_used, N_WOUT + 2)
            for s in range(TT):
                ve.tensor_tensor(x[:, s, :], x[:, s, :], acc[:, s, :], ALU.add).then_inc(x_ready, 1)
            xs[0] += 2
            dve.wait_ge(x_ready, xs[0])

            normalise()
            take_hT(4, 5).then_inc(hT_hi, 1)

            def piece(c, n, *shape):
                ap = small[:, c:c + n]
                if len(shape) == 2:
                    return ap.rearrange("p (a b) -> p a b", a=shape[0])
                if len(shape) == 3:
                    return ap.rearrange("p (a b c) -> p a b c", a=shape[0], b=shape[1])
                return ap

            def over(ap, n):
                return ap.unsqueeze(2).to_broadcast([P, ap.shape[1], n])

            LG = piece(64, 72, TT, 36)
            dve.wait_ge(lg_done, 1)
            order(ve.tensor_copy(LG, wk(0)[:, 0:128].rearrange("p (s c) -> p s c", s=TT)[:, :, 0:36]))
            lgg = LG[:, :, 0:NG]
            gmax, gsum, ggate, gr = piece(0, 2), piece(2, 2), piece(4, 2), piece(6, 2)
            gd, ge = piece(8, 8, TT, NG), piece(16, 8, TT, NG)
            dd, de, w1, w2 = piece(24, 2), piece(26, 2), piece(28, 2), piece(30, 2)
            m1, m2, rr = piece(32, 2), piece(34, 2), piece(36, 2)
            goh = piece(40, 8, TT, NG)
            sel, oh1, oh2, t8, cw, o12 = (piece(140 + 16 * i, 16, TT, NE) for i in range(6))
            prod = piece(256, 64, TT, NG, NE)
            order(ve.tensor_reduce(gmax, lgg, AX.X, ALU.max))
            ve.tensor_tensor(gd, lgg, over(gmax, NG), ALU.subtract).then_inc(gd_ready, 1)
            dve.wait_ge(ge_ready, 1)
            order(ve.tensor_reduce(gsum, ge, AX.X, ALU.add))
            order(ve.reciprocal(ggate, gsum))

            def first_max(dst, src, top, n):
                order(ve.tensor_tensor(dst, src, over(top, n), ALU.is_ge))
                r = rank[:, NE - n:NE].unsqueeze(1).to_broadcast([P, TT, n])
                order(ve.tensor_tensor(dst, dst, r, ALU.mult))
                order(ve.tensor_reduce(rr, dst, AX.X, ALU.max))
                order(ve.tensor_tensor(dst, dst, over(rr, n), ALU.is_equal))

            first_max(goh, lgg, gmax, NG)
            gohb = goh.unsqueeze(3).to_broadcast([P, TT, NG, NE])
            for s in range(TT):
                order(ve.tensor_tensor(prod[:, s], LG[:, s, NG:].rearrange("p (g e) -> p g e", g=NG), gohb[:, s], ALU.mult))
            for s in range(TT):
                order(ve.tensor_reduce(sel[:, s, :], prod[:, s].rearrange("p g e -> p e g"), AX.X, ALU.add))
            order(ve.tensor_reduce(m1, sel, AX.X, ALU.max))
            first_max(oh1, sel, m1, NE)
            order(ve.scalar_tensor_tensor(t8, oh1, NEG, sel, ALU.mult, ALU.add))
            order(ve.tensor_reduce(m2, t8, AX.X, ALU.max))
            first_max(oh2, t8, m2, NE)
            ve.tensor_tensor(dd, m2, m1, ALU.subtract).then_inc(dd_ready, 1)
            order(ve.tensor_tensor(o12, oh1, oh2, ALU.add))
            for s in range(TT):
                order(ve.tensor_tensor(ind[:, s, :].rearrange("p (g e) -> p g e", g=NG), gohb[:, s],
                                       o12[:, s, :].unsqueeze(1).to_broadcast([P, NG, NE]), ALU.mult))
            ve.tensor_copy(ind[:, 0, :], ind[:, 0, :]).then_inc(ind_ready, 1)
            dve.wait_ge(de_ready, 1)
            order(ve.tensor_scalar(w2, de, 1.0, None, ALU.add))
            order(ve.reciprocal(w1, w2))
            order(ve.tensor_tensor(w1, w1, ggate, ALU.mult))
            order(ve.tensor_tensor(w2, w1, de, ALU.mult))
            order(ve.tensor_tensor(oh1, oh1, over(w1, NE), ALU.mult))
            order(ve.tensor_tensor(oh2, oh2, over(w2, NE), ALU.mult))
            order(ve.tensor_tensor(cw, oh1, oh2, ALU.add))
            for s in range(TT):
                order(ve.tensor_tensor(comb[:, s, :].rearrange("p (g e) -> p g e", g=NG), gohb[:, s],
                                       cw[:, s, :].unsqueeze(1).to_broadcast([P, NG, NE]), ALU.mult))
            dve.wait_ge(pos_done, 1)
            pos = wk(1)[:, 0:128].rearrange("p (s e) -> p s e", s=TT)[:, :, 0:NG * NE]
            order(ve.scalar_tensor_tensor(posm[:, :, :], pos, 1.0, ind[:, :, :], ALU.add, ALU.mult))
            order(ve.tensor_scalar(posm[:, :, :], posm[:, :, :], -1.0, None, ALU.add))
            order(ve.tensor_reduce(mostf[:, :], wk(1)[:, 128:160], AX.X, ALU.max))
            ve.tensor_copy(most[:, :], mostf[:, :]).then_inc(most_ready, 1)

            order_base = order.n

            def experts(g, it):
                for s in range(TT):
                    slots = slot_ids.unsqueeze(1).to_broadcast([P, BATCH, SLOTS])
                    e4 = posm[:, s, bass.ds(g * BATCH, BATCH)].unsqueeze(2).to_broadcast([P, BATCH, SLOTS])
                    w4 = comb[:, s, bass.ds(g * BATCH, BATCH)].unsqueeze(2).to_broadcast([P, BATCH, SLOTS])
                    g4 = G[:, s, :].rearrange("p (j c) -> p j c", j=BATCH)
                    order(ve.tensor_tensor(g4, slots, e4, ALU.is_equal))
                    last = ve.tensor_tensor(Gw[:, s, :].rearrange("p (j c) -> p j c", j=BATCH), g4, w4, ALU.mult)
                last.then_inc(G_ready, 1)
                dve.wait_ge(xg_done, it * 2 + 2)
                for k in range(4, 8):
                    last = ve.tensor_scalar(xgT[:, k, :], wk(3)[:, (k - 4) * P:(k - 3) * P], gains[:, 5, k:k + 1], None, ALU.mult)
                last.then_inc(xg_hi, 1)
                dve.wait_ge(ex_ready, it + 1)
                order(ve.tensor_scalar(act_d, act_e, 1.0, None, ALU.add))
                order(ve.reciprocal(act_r, act_d))
                order(ve.tensor_tensor(act_t, wk(0), act_r, ALU.mult))
                dve.wait_ge(chunks_used, it * CPB + (N_MOE + 8))
                ve.tensor_tensor(act_s, wk(1), act_t, ALU.mult).then_inc(act_ready, 1)
                dve.wait_ge(chunks_used, it * CPB + (N_MOE + 12))
                ve.tensor_copy(ysb[:, COLS:D], wk(3)).then_inc(y_hi, 1)

            PER = 5
            dve.wait_ge(most_ready, 1)
            n_most = dve.value_load(most[0:1, 0:1], min_val=0, max_val=T)
            with dve.Fori(0, GROUPS) as g:
                order.base, order.n = g * PER + order_base, 0
                experts(g, g)
                assert order.n == PER
            with dve.Fori(1, PASSES) as b:
                with dve.If(n_most > b * SLOTS):
                    ve.tensor_scalar(slot_ids, slot_ids, float(SLOTS), None, ALU.add).then_inc(slots_moved, 1)
                    with dve.Fori(0, GROUPS) as g:
                        order.base, order.n = (b * GROUPS + g) * PER + order_base, 0
                        dve.wait_ge(slots_moved, b)
                        experts(g, b * GROUPS + g)
            dve.wait_ge(moe_done, 1)
            ve.tensor_copy(outsb[:, 1, :], acc[:, 1, :]).then_inc(out_hi, 1)


_INS = ['x', 'pool_w', 'pool_scale', 'w_q', 'w_kv', 'kv_norm_g', 'w_o', 'w_up', 'w_down', 'mix_pre_g', 'mix_post_g',
        'mlp_pre_g', 'mlp_post_g', 'attn_norm_g_2', 'w_in_2', 'conv_w_2', 'conv_out_g_2', 'q_norm_g_2', 'k_norm_g_2',
        'lambda_q1_2', 'lambda_k1_2', 'lambda_q2_2', 'lambda_k2_2', 'attn_subln_g_2', 'w_out_2', 'ffn_norm_g_2',
        'w_router_group_2', 'w_router_expert_2', 'w_exp_gate_2', 'w_exp_up_2', 'w_exp_down_2']


def kernel(**inputs):
    import concourse.bacc as bacc
    from concourse.bass_utils import run_bass_kernel_spmd

    nc = bacc.Bacc("TRN2", target_bir_lowering=False, num_devices=1)
    consts, poolm = shape_constants()
    given = {name: np.ascontiguousarray(inputs[name]) for name in _INS}
    given["consts"], given["poolm"] = consts, poolm
    arrays, args = {}, {}
    for name, arr in given.items():
        arrays[f"in_{name}"] = arr
        args[name] = nc.dram_tensor(f"in_{name}", arr.shape, mybir.dt.from_np(arr.dtype), kind="ExternalInput").ap()
    out = nc.dram_tensor("out_0", (1, T, D), F32, kind="ExternalOutput").ap()
    build(nc, args, out)
    r = run_bass_kernel_spmd(nc, [arrays], core_ids=[0])
    return r.results[0]["out_0"]
```

```python
from contextlib import ExitStack

import concourse.bass as bass
import numpy as np
from concourse import mybir

P = 128
D = 1024
T = 256
TT = T // P
KD = D // P
FF = 4096
COLS = 512
EPS = 1e-6
NEG = -1e30
HEADS, DH = 16, 64
WINDOWS = (2, 4, 8, 16)
HEADS2, VD = 4, 128
LAM_INIT = 0.2
NG, NE = 4, 8
FE = 512
SLOTS = 32
BATCH = P // SLOTS
GROUPS = NG * NE // BATCH
PASSES = T // SLOTS

RING = 4
CHUNK = 4096
CPB = 12

ALU = mybir.AluOpType
ACT = mybir.ActivationFunctionType
F32 = mybir.dt.float32
F32R = mybir.dt.float32r
I32 = mybir.dt.int32
AX = mybir.AxisListType

C_IDENT, C_NTRI, C_NONE, C_STRICT, C_CAUSAL, C_BEFORE, C_ONES, C_BLOCK, C_IOTA, C_RANK, C_END = (
    0, 128, 256, 384, 512, 640, 768, 896, 1024, 1056, 1064)


def shape_constants():
    i = np.arange(P)
    row, col = i[:, None], i[None, :]
    c = np.zeros((P, C_END), np.float32)
    c[:, C_IDENT:C_IDENT + P] = row == col
    c[:, C_NTRI:C_NTRI + P] = -1.0 * (row >= col)
    c[:, C_NONE:C_NONE + P] = -1.0
    c[:, C_STRICT:C_STRICT + P] = np.where(row >= col, NEG, 0.0)
    c[:, C_CAUSAL:C_CAUSAL + P] = np.where(col > row, NEG, 0.0)
    c[:, C_BEFORE:C_BEFORE + P] = row < col
    c[:, C_ONES:C_ONES + P] = 1.0
    c[:, C_BLOCK:C_BLOCK + P] = (row // 64 == col // 64) / 64.0
    c[:, C_IOTA:C_IOTA + SLOTS] = np.arange(SLOTS)[None, :]
    c[:, C_RANK:C_RANK + NE] = (NE - np.arange(NE))[None, :]
    t = np.arange(T)
    pool = np.zeros((P, len(WINDOWS), TT, T), np.float32)
    for w, win in enumerate(WINDOWS):
        m = ((t[:, None] <= t[None, :]) & (t[:, None] > t[None, :] - win)) / np.minimum(t + 1, win)[None, :]
        m = m - np.eye(T)
        pool[:, w] = m.reshape(TT, P, T).transpose(1, 0, 2)
    return c, pool.reshape(P, -1)


N_POOL = 0
N_MLP = (1, 25)
N_KV = 17
N_WO = 23
N_IN = 41
IN_BANKS = (4, 6, 2, 4, 6)
N_WOUT = 47
N_MOE = 49
ROW_CHUNKS = {N_KV + 4, N_KV + 5, N_WO, N_WO + 1, N_IN + 5, N_WOUT, N_WOUT + 1}
PAIRS = RING // 2
PAIR_ITERS = FF // COLS // PAIRS
QI = 4 * RING
AHEAD = 2

MOE_RING = 2 * RING
MOE_SLOTS = (1, 2, 3, 0, 4, 5, 6, 7)
MOE_UNROLL = 2
MOE_FRONT = [len(range(q, N_MOE, RING)) for q in range(RING)] + [0] * RING


def build(nc, a, out):
    ctx = ExitStack()
    with ctx:
        def sem(name):
            return ctx.enter_context(nc.semaphore(name))

        top = [-(-nc.sbuf_base // 64) * 64]

        def at(name, shape, offset, dt=F32):
            return nc.alloc_sbuf_tensor_at(name, shape, dt, offset=offset)

        def region(nbytes):
            base = top[0]
            top[0] += -(-nbytes // 64) * 64
            return base

        def sb(name, shape, dt=F32):
            return at(name, shape, region(4 * int(np.prod(shape[1:]))), dt)

        K = 1024
        consts = sb("consts", [P, C_END])
        identr = sb("identr", [P, P], F32R)
        strictr = sb("strictr", [P, P], F32R)
        x = sb("x", [P, TT, D])
        h = sb("h", [P, TT, D])
        gains = sb("gains", [P, 6, KD])
        poolg = sb("poolg", [P, KD])
        row = sb("row", [P, D])
        qkg = sb("qkg", [P, 2])
        qg8 = sb("qg8", [P, 1])
        convw = sb("convw", [P, 3, 4])
        convg = sb("convg", [P, 4])
        subg = sb("subg", [P, VD])
        lamv = sb("lamv", [P, 4, 64])
        lam = sb("lam", [P, 8])
        wr = sb("wr", [P, KD, NG + NG * NE])
        wr_hi = sb("wr_hi", [P, KD, NG + NG * NE], F32R)
        wr_lo = sb("wr_lo", [P, KD, NG + NG * NE], F32R)
        ss = sb("ss", [P, 2])
        ms = sb("ms", [P, 2])
        lnv = sb("lnv", [P, 2])
        r0 = sb("r0", [P, 2])
        r1 = sb("r1", [P, 2])
        rstd = sb("rstd", [P, 2])
        st2 = sb("st2", [P, 2, 8])
        sub = sb("sub", [P, 6, 8])
        small = sb("small", [P, 320])
        posm = sb("posm", [P, TT, NG * NE])
        comb = sb("comb", [P, TT, NG * NE])
        ind = sb("ind", [P, TT, NG * NE])
        most = sb("most", [P, 1], I32)
        mostf = sb("mostf", [P, 1])

        ring = sb("ring", [P, RING, CHUNK])
        w_base = region(64 * K)
        w_hi = at("w_hi", [P, 4, 1024], w_base, F32R)
        w_lo = at("w_lo", [P, 4, 1024], w_base + 16 * K, F32R)
        mixT_hi = at("mixT_hi", [P, KD, T], w_base + 32 * K, F32R)
        mixT_lo = at("mixT_lo", [P, KD, T], w_base + 40 * K, F32R)
        hT_hi = at("hT_hi", [P, KD, T], w_base + 48 * K, F32R)
        hT_lo = at("hT_lo", [P, KD, T], w_base + 56 * K, F32R)
        ring2 = at("ring2", [P, RING, CHUNK], w_base)
        yT = at("yT", [P, KD, T], w_base + 32 * K)

        kqv = region(24 * K)
        kbuf = at("kbuf", [P, KD * T], kqv)
        qbuf = at("qbuf", [P, KD * T], kqv + 8 * K)
        vbuf = at("vbuf", [P, TT * D], kqv + 16 * K)
        aT_hi = at("aT_hi", [P, 4, T], kqv + 8 * K, F32R)
        aT_lo = at("aT_lo", [P, 4, T], kqv + 12 * K, F32R)
        rT = at("rT", [P, 4, T], kqv + 16 * K)
        aT = at("aT", [P, 4, T], kqv + 20 * K)

        scratch = region(20 * K + 64)
        mg = at("mg", [P, TT, D], scratch)
        scale_row = at("scale_row", [P, D], scratch + 8 * K)
        att = at("att", [P, 4, 3, 384], scratch)
        convu = at("convu", [P, 4, T + 2], scratch + 8 * K)
        o2 = at("o2", [P, TT, COLS], scratch + 8 * K)
        convy = at("convy", [P, 4, T], scratch + 12 * K + 64)
        e2 = at("e2", [P, 2, 2, T], scratch + 16 * K + 64)
        a2 = at("a2", [P, 2, T], kqv + 20 * K)
        a2T = at("a2T", [P, 2, T], kqv + 22 * K)
        zero_t = sb("zero_t", [P, COLS], F32R)
        assert top[0] <= nc.sbuf_usable_end, (top[0], nc.sbuf_usable_end)

        ps = ctx.enter_context(nc.psum_tensor("ps", [P, 8, COLS], F32))
        acc = ps[:, 0:4, :].rearrange("p (t b) c -> p t (b c)", t=TT)

        def wk(b):
            return ps[:, 4 + b, :]

        ident = consts[:, C_IDENT:C_IDENT + P]
        ntri = consts[:, C_NTRI:C_NTRI + P]
        nones = consts[:, C_NONE:C_NONE + P]
        strict = consts[:, C_STRICT:C_STRICT + P]
        causal = consts[:, C_CAUSAL:C_CAUSAL + P]
        before = consts[:, C_BEFORE:C_BEFORE + P]
        ones = consts[:, C_ONES:C_ONES + P]
        blockmean = consts[:, C_BLOCK:C_BLOCK + P]
        slot_ids = consts[:, C_IOTA:C_IOTA + SLOTS]
        rank = consts[:, C_RANK:C_RANK + NE]

        poolm = kbuf[:, :].rearrange("p (w s t) -> p w s t", w=4, s=TT)
        kT = kbuf[:, :].rearrange("p (k t) -> p k t", k=KD)
        qT = qbuf[:, :].rearrange("p (k t) -> p k t", k=KD)
        v = vbuf[:, :].rearrange("p (s d) -> p s d", s=TT)
        q2 = qbuf[:, 0:1024]
        q2n = q2.rearrange("p (m t) -> p m t", m=4)
        k2 = qbuf[:, 1024:2048]
        k2n = k2.rearrange("p (m t) -> p m t", m=4)
        sq2 = kbuf[:, 0:1024]
        wms = kbuf[:, 1024:2048]
        wr0 = mg[:, 0, :]
        wr1 = mg[:, 1, :]
        v2 = vbuf[:, 0:1024].rearrange("p (s d) -> p s d", s=TT)
        xc = vbuf[:, 1024:2048].rearrange("p (k t) -> p k t", k=4)
        G = kbuf[:, 0:256].rearrange("p (s c) -> p s c", s=TT)
        Gw = kbuf[:, 256:512].rearrange("p (s c) -> p s c", s=TT)
        S = kbuf[:, 512:768]
        actT = kbuf[:, 1024:1536].rearrange("p (f c) -> p f c", f=4)
        act_e = qbuf[:, 0:512]
        act_d = qbuf[:, 512:1024]
        act_r = qbuf[:, 1024:1536]
        act_t = qbuf[:, 1536:2048]
        xgT = vbuf[:, 0:1024].rearrange("p (k c) -> p k c", k=KD)
        ysb = vbuf[:, 1024:2048]
        act_s = kbuf[:, 1536:2048]
        outsb = mg

        x_loaded = sem("x_loaded")
        early_loaded = sem("early_loaded")
        early_rows = sem("early_rows")
        late_loaded = sem("late_loaded")
        slot_loaded = [sem(f"slot_loaded{i}") for i in range(MOE_RING)]
        hi_ready = sem("hi_ready")
        lo_ready = sem("lo_ready")
        quarters_used = sem("quarters_used")
        chunks_used = sem("chunks_used")
        row_loaded = sem("row_loaded")
        q_hi = sem("q_hi")
        q_lo = sem("q_lo")
        oT_hi = sem("oT_hi")
        cT_ready = sem("cT_ready")
        cT_hi = sem("cT_hi")
        o2T_hi = sem("o2T_hi")
        wr_hi_ready = sem("wr_hi_ready")
        wr_ready = sem("wr_ready")
        maskr_ready = sem("maskr_ready")
        act_order = sem("act_order")
        dve_order = sem("dve_order")
        pe_order = sem("pe_order")
        x_ready = sem("x_ready")
        ss_ready = sem("ss_ready")
        ms_ready = sem("ms_ready")
        r0_ready = sem("r0_ready")
        h_ready = sem("h_ready")
        hT_banks = sem("hT_banks")
        hT_hi_ready = sem("hT_hi_ready")
        hT_lo_ready = sem("hT_lo_ready")
        m_ready = sem("m_ready")
        yT_banks = sem("yT_banks")
        yT_lo = sem("yT_lo")
        yT_hi = sem("yT_hi")
        scaled = sem("scaled")
        relu_ready = sem("relu_ready")
        sq_hi = sem("sq_hi")
        sq_full = sem("sq_full")
        sq_ready = sem("sq_ready")
        proj_done = sem("proj_done")
        proj_taken = sem("proj_taken")
        v_taken = sem("v_taken")
        z_done = sem("z_done")
        absz_ready = sem("absz_ready")
        log_ready = sem("log_ready")
        lp_ready = sem("lp_ready")
        arg_done = sem("arg_done")
        prob_ready = sem("prob_ready")
        o_done = sem("o_done")
        oT_ready = sem("oT_ready")
        in_done = sem("in_done")
        raw_ready = sem("raw_ready")
        sq2_ready = sem("sq2_ready")
        ms2_done = sem("ms2_done")
        ms2_ready = sem("ms2_ready")
        rw_ready = sem("rw_ready")
        n2_ready = sem("n2_ready")
        xc_ready = sem("xc_ready")
        v2_ready = sem("v2_ready")
        s2_done = sem("s2_done")
        nm_ready = sem("nm_ready")
        e2_ready = sem("e2_ready")
        a2_ready = sem("a2_ready")
        a2T_done = sem("a2T_done")
        a2T_ready = sem("a2T_ready")
        o2_done = sem("o2_done")
        lam_dots = sem("lam_dots")
        lam_exp = sem("lam_exp")
        o2sq_ready = sem("o2sq_ready")
        subms_ready = sem("subms_ready")
        subr_ready = sem("subr_ready")
        o2n_ready = sem("o2n_ready")
        o2T_done = sem("o2T_done")
        o2T_ready = sem("o2T_ready")
        lg_done = sem("lg_done")
        gd_ready = sem("gd_ready")
        ge_ready = sem("ge_ready")
        dd_ready = sem("dd_ready")
        de_ready = sem("de_ready")
        ind_ready = sem("ind_ready")
        pos_done = sem("pos_done")
        most_ready = sem("most_ready")
        seeded = sem("seeded")
        G_ready = sem("G_ready")
        xg_done = sem("xg_done")
        S_done = sem("S_done")
        S_ready = sem("S_ready")
        xg_lo = sem("xg_lo")
        xg_hi = sem("xg_hi")
        ex_ready = sem("ex_ready")
        act_ready = sem("act_ready")
        actT_done = sem("actT_done")
        actT_ready = sem("actT_ready")
        y_lo = sem("y_lo")
        y_hi = sem("y_hi")
        moe_done = sem("moe_done")
        out_lo = sem("out_lo")
        out_hi = sem("out_hi")
        stored = sem("stored")
        zero_ready = sem("zero_ready")
        conv_gated = sem("conv_gated")
        slots_moved = sem("slots_moved")

        N_LATE = 6 + 4 + 3 + 2 + 4 + 2
        EARLY = 16 * 2
        EARLY_ROWS = 16 * 3
        LATE = 16 * N_LATE

        block = ctx.enter_context(nc.Block())

        class Order:

            def __init__(self, eng, s):
                self.eng, self.s, self.base, self.n = eng, s, 0, 0

            def __call__(self, ins):
                self.n += 1
                ins.then_inc(self.s, 1)
                self.eng.wait_ge(self.s, self.base + self.n)

        def slot(n):
            return ring[:, n % RING, :]

        def quarter(n, f):
            if n in ROW_CHUNKS:
                return slot(n)[:, 1024 * f:1024 * (f + 1)].rearrange("p (k w) -> p k w", k=KD)
            return slot(n).rearrange("p (k w) -> p k w", k=KD)[:, :, f * P:(f + 1) * P]

        def mlp_quarter(n, j, f):
            if j % 2:
                return slot(n)[:, 1024 * f:1024 * (f + 1)].rearrange("p (k w) -> p k w", k=KD)
            return slot(n).rearrange("p (k w) -> p k w", k=KD)[:, :, f * P:(f + 1) * P]

        def ahead_of(n, f):
            return n + (f + AHEAD) // 4, (f + AHEAD) % 4

        def moe_slot(c):
            q = MOE_SLOTS[c % MOE_RING]
            return ring[:, q, :] if q < RING else ring2[:, q - RING, :]

        def kd_rows(w):
            return w.rearrange("(p k) n -> p k n", k=KD)

        def std_rows(w):
            return w.rearrange("(m p) n -> p m n", p=P)

        def chunk_source(n):
            if n == N_POOL:
                return a["pool_w"][0].rearrange("g (c p) d -> p (g c) d", p=P), 8, 256
            if N_KV <= n < N_KV + 6:
                w, c = [("w_kv", 0), ("w_kv", 1), ("w_q", 0), ("w_q", 1), ("w_kv", 2), ("w_kv", 3)][n - N_KV]
                src = a[w] if w == "w_kv" else a[w][0]
                return kd_rows(src)[:, :, c * COLS:(c + 1) * COLS], KD, COLS
            if N_WO <= n < N_WO + 2:
                return std_rows(a["w_o"][0])[:, 4 * (n - N_WO):4 * (n - N_WO) + 4, :], 4, D
            if N_IN <= n < N_IN + 6:
                c = [3, 4, 0, 2, 1, 5][n - N_IN]
                return kd_rows(a["w_in_2"][0])[:, :, c * COLS:(c + 1) * COLS], KD, COLS
            return std_rows(a["w_out_2"][0])[:, 4 * (n - N_WOUT):4 * (n - N_WOUT) + 4, :], 4, D

        @block.sync
        def _(sp):
            sp.dma_start(x[:, :, :], a["x"][0].rearrange("(s p) d -> p s d", p=P)).then_inc(x_loaded, 16)
            sp.dma_start(consts[:, :], a["consts"]).then_inc(early_loaded, 16)
            sp.dma_start(kbuf[:, :], a["poolm"]).then_inc(early_loaded, 16)

            def load(n, src, m, w):
                if n == RING:
                    sp.wait_ge(quarters_used, 4)
                elif n > RING:
                    sp.wait_ge(lo_ready, 4 * (n - RING))
                sp.dma_start(slot(n)[:, 0:m * w].rearrange("p (m w) -> p m w", m=m), src)\
                  .then_inc(slot_loaded[n % RING], 16)

            def mlp(layer):
                up, down = kd_rows(a["w_up"][layer]), std_rows(a["w_down"][layer])
                n0 = N_MLP[layer]
                for j in range(2 * PAIRS):
                    n = n0 + j
                    if j % 2 == 0:
                        load(n, up[:, :, j // 2 * COLS:(j // 2 + 1) * COLS], KD, COLS)
                    else:
                        load(n, down[:, j // 2 * 4:j // 2 * 4 + 4, :], 4, D)
                with sp.Fori(1, PAIR_ITERS) as i:
                    for j in range(2 * PAIRS):
                        n = n0 + j
                        sp.wait_ge(lo_ready, i * QI + 4 * (n - RING))
                        if j % 2 == 0:
                            dst = slot(n).rearrange("p (m w) -> p m w", m=KD)
                            src = up[:, :, bass.ds(i * (PAIRS * COLS) + j // 2 * COLS, COLS)]
                        else:
                            dst = slot(n).rearrange("p (m w) -> p m w", m=4)
                            src = down[:, bass.ds(i * (PAIRS * 4) + j // 2 * 4, 4), :]
                        sp.dma_start(dst, src).then_inc(slot_loaded[n % RING], 16)

            load(N_POOL, *chunk_source(N_POOL))
            mlp(0)
            for n in range(N_KV, N_WO + 2):
                load(n, *chunk_source(n))
            mlp(1)
            for n in range(N_IN, N_WOUT + 2):
                load(n, *chunk_source(n))

            gate = a["w_exp_gate_2"][0].rearrange("g e (p k) f -> p (g e) (k f)", k=KD)
            up = a["w_exp_up_2"][0].rearrange("g e (p k) f -> p (g e) (k f)", k=KD)
            down = a["w_exp_down_2"][0].rearrange("g e (m p) d -> m p (g e) d", p=P)

            def experts(g2, i2, first=False):
                for u in range(MOE_UNROLL):
                    g = g2 * MOE_UNROLL + u
                    for c in range(CPB):
                        m = u * CPB + c
                        if not first or m >= MOE_RING:
                            sp.wait_ge(chunks_used, i2 * (MOE_UNROLL * CPB) + (m - MOE_RING + 1))
                        elif m < RING:
                            sp.wait_ge(lo_ready, 4 * (N_MOE - RING + m))
                        elif m < MOE_RING - 1:
                            sp.wait_ge(quarters_used, 4 * N_MOE)
                        else:
                            sp.wait_ge(lg_done, 1)
                        dst = moe_slot(m).rearrange("p (j w) -> p j w", j=BATCH)
                        if c < 8:
                            w = gate if c < 4 else up
                            src = w[:, bass.ds(g * BATCH, BATCH), (c % 4) * 1024:(c % 4) * 1024 + 1024]
                        else:
                            src = down[c - 8][:, bass.ds(g * BATCH, BATCH), :]
                        sp.dma_start(dst, src).then_inc(slot_loaded[MOE_SLOTS[m % MOE_RING]], 16)

            ITERS = GROUPS // MOE_UNROLL
            experts(0, 0, True)
            with sp.Fori(1, ITERS) as g2:
                experts(g2, g2)
            sp.wait_ge(most_ready, 1)
            n_most = sp.value_load(most[0:1, 0:1], min_val=0, max_val=T)
            with sp.Fori(1, PASSES) as b:
                with sp.If(n_most > b * SLOTS):
                    with sp.Fori(0, ITERS) as g2:
                        experts(g2, b * ITERS + g2)

            sp.wait_ge(out_lo, 1)
            sp.dma_start(out[0, 0:P, :], outsb[:, 0, :]).then_inc(stored, 16)
            sp.wait_ge(out_hi, 1)
            sp.dma_start(out[0, P:T, :], outsb[:, 1, :]).then_inc(stored, 16)
            sp.wait_ge(stored, 32)

        @block.gpsimd
        def _(pool):
            def every(src):
                return src.partition_broadcast(P)

            nd = 0
            with nc.allow_non_contiguous_dma(reason="small gain vectors"):
                pool.dma_start(poolg[:, :], a["mix_pre_g"][0].rearrange("(k p) -> p k", p=P)).then_inc(early_rows, 16)
                pool.dma_start(scale_row[:, :], every(a["pool_scale"][0])).then_inc(early_rows, 16)
                pool.dma_start(row[:, :], every(a["mix_post_g"][0])).then_inc(early_rows, 16)
                for i, src in enumerate((a["mlp_pre_g"][0], a["kv_norm_g"], a["mix_pre_g"][1], a["mlp_pre_g"][1],
                                         a["attn_norm_g_2"][0], a["ffn_norm_g_2"][0])):
                    pool.dma_start(gains[:, i, :], src.rearrange("(p k) -> p k", k=KD)).then_inc(late_loaded, 16)
                    nd += 1
                for i, src in ((0, a["q_norm_g_2"]), (1, a["k_norm_g_2"])):
                    for c in range(2):
                        pool.dma_start(qkg[64 * c:64 * c + 64, i:i + 1], src.rearrange("a d -> d a")).then_inc(late_loaded, 16)
                        nd += 1
                for i in range(3):
                    pool.dma_start(convw[:, i, :], a["conv_w_2"][0, i].rearrange("(m p) -> p m", p=P)).then_inc(late_loaded, 16)
                    nd += 1
                pool.dma_start(convg[:, :], a["conv_out_g_2"][0].rearrange("(m p) -> p m", p=P)).then_inc(late_loaded, 16)
                pool.dma_start(subg[:, :], every(a["attn_subln_g_2"][0])).then_inc(late_loaded, 16)
                nd += 2
                for i, nm in enumerate(("lambda_q1_2", "lambda_k1_2", "lambda_q2_2", "lambda_k2_2")):
                    pool.dma_start(lamv[:, i, :], every(a[nm][0])).then_inc(late_loaded, 16)
                    nd += 1
                pool.dma_start(wr[:, :, 0:NG], kd_rows(a["w_router_group_2"][0])).then_inc(late_loaded, 16)
                pool.dma_start(wr[:, :, NG:], kd_rows(a["w_router_expert_2"][0])).then_inc(late_loaded, 16)
                nd += 2
            assert nd == N_LATE
            for i, src in enumerate((a["mlp_post_g"][0], a["mix_post_g"][1], a["mlp_post_g"][1])):
                pool.wait_ge(x_ready, 2 * i + 2)
                pool.dma_start(row[:, :], every(src)).then_inc(row_loaded, 16)


        def mean_squares(pe, mm, i, bank):
            pe.wait_ge(sq2_ready, i + 1)
            for b in range(2):
                last = mm(ps[:, bank + b, :], blockmean, sq2[:, b * COLS:(b + 1) * COLS], start=True, stop=True)
            last.then_inc(ms2_done, 1)

        @block.tensor
        def _(pe):
            mm = nc.tensor.matmul

            def mm3(out, lhs, rhs, start, stop, **kw):
                (a_hi, a_lo), (b_hi, b_lo) = lhs, rhs
                mm(out, a_hi, b_hi, start=start, stop=False, skip_group_check=True)
                mm(out, a_hi, b_lo, start=False, stop=False, skip_group_check=True)
                return mm(out, a_lo, b_hi, start=False, stop=stop, skip_group_check=True)

            def arrived(n):
                pe.wait_ge(slot_loaded[n % RING], 16 * (n // RING + 1))

            def split(n, f, i=0):
                pe.wait_ge(lo_ready, i * QI + (4 * (n - 1) + f + 1))

            def transposes(turn):
                pe.wait_ge(h_ready, 2 * turn + 4)
                for b in range(4):
                    for k in (2 * b, 2 * b + 1):
                        for s in range(TT):
                            c = (k % 2) * T + s * P
                            last = nc.tensor.transpose(wk(b)[:, c:c + P], h[:, s, k:D:KD], ident)
                    last.then_inc(hT_banks, 1)

            def channel_major(out, n, f, ops, i=0, ready=None):
                split(n, f, i)
                w = [q[:, f, :].rearrange("p (k w) -> p k w", k=KD) for q in (w_hi, w_lo)]
                for k in range(KD):
                    if ready is not None:
                        ready(k)
                    last = mm3(out, [q[:, k, :] for q in w], [q[:, k, :] for q in ops], k == 0, k == KD - 1)
                last.then_inc(quarters_used, 1)

            def token_major(outs, n):
                for f in range(4):
                    split(n, f)
                    for kk in range(2):
                        k = 2 * f + kk
                        for s in range(TT):
                            last = mm3(outs[s], [q[:, k, s * P:(s + 1) * P] for q in (hT_hi, hT_lo)],
                                       [q[:, f, kk * COLS:(kk + 1) * COLS] for q in (w_hi, w_lo)], k == 0, k == KD - 1)
                    last.then_inc(quarters_used, 1)

            def hT_tile(turn):
                return lambda k: pe.wait_ge(hT_lo_ready, 4 * turn + k // 2 + 1) if k % 2 == 0 else None

            pe.wait_ge(early_loaded, EARLY)
            pe.wait_ge(h_ready, 2)
            for b in range(4):
                for k in (2 * b, 2 * b + 1):
                    for s in range(TT):
                        last = mm(wk(b)[:, (k % 2) * T:(k % 2) * T + T], h[:, s, k * P:(k + 1) * P], poolm[:, k // 2, s, :],
                                  start=(s == 0), stop=(s == TT - 1))
                last.then_inc(yT_banks, 1)
            arrived(N_POOL)
            pe.wait_ge(yT_lo, 1)
            pe.wait_ge(yT_hi, 1)
            pw = slot(N_POOL)[:, 0:2048].rearrange("p (m w) -> p m w", m=8)
            for s in range(TT):
                for g in range(4):
                    for c in range(2):
                        last = mm(acc[:, s, 256 * g:256 * g + 256], yT[:, 2 * g + c, s * P:(s + 1) * P], pw[:, 2 * g + c, :],
                                  start=(c == 0), stop=(c == 1))
                    if g % 2:
                        last.then_inc(quarters_used, 1)

            def mlp(layer, turn):
                for s in range(TT):
                    for half in range(2):
                        mm(acc[:, s, half * COLS:(half + 1) * COLS], zero_t[:, 0:P], zero_t[:, 0:COLS],
                           start=True, stop=True)
                transposes(turn)
                pe.wait_ge(hT_lo_ready, 4 * turn + 4)
                n0 = N_MLP[layer]
                with pe.Fori(0, PAIR_ITERS) as i:
                    for j in range(PAIRS):
                        n = n0 + 2 * j
                        for f in range(4):
                            channel_major(wk(f)[:, 0:T], n, f, (hT_hi, hT_lo), i)
                        for f in range(4):
                            split(n + 1, f, i)
                            pe.wait_ge(sq_ready, i * (4 * PAIRS) + (32 * layer + 4 * j + f + 1))
                            for s in range(TT):
                                for half in range(2):
                                    last = mm3(acc[:, s, half * COLS:(half + 1) * COLS],
                                               [q[:, f, s * P:(s + 1) * P] for q in (aT_hi, aT_lo)],
                                               [q[:, f, half * COLS:(half + 1) * COLS] for q in (w_hi, w_lo)], False, False)
                            last.then_inc(quarters_used, 1)

            pe.wait_ge(x_ready, 2)
            pe.wait_ge(zero_ready, 1)
            mlp(0, 0)

            transposes(1)
            for t in range(16):
                n, f = N_KV + t // 4, t % 4
                if 4 <= t < 8 or t >= 12:
                    pe.wait_ge(proj_taken, t - 3)
                if t < 8:
                    channel_major(ps[:, f, 0:T], n, f, (hT_hi, hT_lo), ready=hT_tile(1) if t == 0 else None)
                else:
                    if t == 8:
                        pe.wait_ge(q_lo, 4)
                    channel_major(wk(f)[:, 0:T], n, f, (mixT_hi, mixT_lo))
            pe.wait_ge(proj_taken, 8)
            for i in range(2):
                token_major([acc[:, s, i * COLS:(i + 1) * COLS] for s in range(TT)], N_KV + 4 + i)

            def zbank(i):
                return ps[:, i % 6, :]

            def scores(i):
                r, m = 64 * (i % 2), i // 2
                z = zbank(i)
                mm(z[:, 0:T], kT[r:r + 64, m, 0:P], qT[r:r + 64, m, :], start=True, stop=False, skip_group_check=True)
                mm(z[:, 0:P], identr[:, :], strictr[:, :], start=False, stop=False, skip_group_check=True)
                mm(z[:, T:T + P], kT[r:r + 64, m, P:T], qT[r:r + 64, m, P:T], start=False, stop=False, skip_group_check=True)
                mm(z[:, T:T + P], identr[:, :], strictr[:, :], start=False, stop=True, skip_group_check=True)\
                    .then_inc(z_done, 1)

            def args(i):
                z, lp = zbank(i), att[:, 2, i % 3, :]
                pe.wait_ge(lp_ready, i + 1)
                mm(z[:, 0:T], ntri, lp[:, 0:T], start=False, stop=False, skip_group_check=True)
                mm(z[:, P:T], nones, lp[:, T:T + P], start=False, stop=False, skip_group_check=True)
                mm(z[:, T:T + P], ntri, lp[:, T:T + P], start=False, stop=True, skip_group_check=True).then_inc(arg_done, 1)

            def weighted(i):
                r, m = 64 * (i % 2), i // 2
                p = att[:, 3, i % 3, :]
                o = wk(2 + m % 2)[r:r + 64, 0:T]
                pe.wait_ge(prob_ready, i + 1)
                if m >= 2 and i % 2 == 0:
                    pe.wait_ge(oT_ready, m - 1)
                mm(o, v[:, 0, i * DH:(i + 1) * DH], p[:, 0:T], start=True, stop=False, skip_group_check=True)
                last = mm(o[:, P:T], v[:, 1, i * DH:(i + 1) * DH], p[:, T:T + P], start=False, stop=True, skip_group_check=True)
                if i % 2:
                    last.then_inc(o_done, 1)

            pe.wait_ge(maskr_ready, 2)
            pe.wait_ge(proj_taken, 16)
            pe.wait_ge(v_taken, 4)
            for i in range(HEADS + 3):
                if i < HEADS:
                    if i >= 6:
                        pe.wait_ge(prob_ready, i - 5)
                    scores(i)
                if 2 <= i < HEADS + 2:
                    args(i - 2)
                if i >= 3:
                    weighted(i - 3)

            def project(n0):
                for m in range(KD):
                    split(n0 + m // 4, m % 4)
                    for s in range(TT):
                        for half in range(2):
                            last = mm3(acc[:, s, half * COLS:(half + 1) * COLS],
                                       [q[:, m, s * P:(s + 1) * P] for q in (mixT_hi, mixT_lo)],
                                       [q[:, m % 4, half * COLS:(half + 1) * COLS] for q in (w_hi, w_lo)],
                                       m == 0, m == KD - 1)
                    last.then_inc(quarters_used, 1)

            pe.wait_ge(oT_ready, 8)
            project(N_WO)
            pe.wait_ge(x_ready, 6)
            mlp(1, 2)

            transposes(3)
            for i in range(5):
                b0 = IN_BANKS[i]
                if i == 0:
                    pe.wait_ge(hT_lo_ready, 16)
                if i == 3:
                    pe.wait_ge(n2_ready, 1)
                if i == 4:
                    pe.wait_ge(n2_ready, 2)
                for f in range(4):
                    channel_major(ps[:, b0 + f // 2, (f % 2) * T:(f % 2) * T + T], N_IN + i, f, (hT_hi, hT_lo))
                if 1 <= i <= 2:
                    mean_squares(pe, mm, i - 1, 4 + 2 * (i - 1))
            token_major([ps[:, s, :] for s in range(TT)], N_IN + 5)
            mean_squares(pe, mm, 2, 2)

            def scores2(u):
                s, hd = u // 4, u % 4
                nk = (s + 1) * P
                for c in range(2):
                    mm(wk(2 * (u % 2) + c)[:, 0:nk], q2n[64 * c:64 * c + 64, hd, s * P:(s + 1) * P],
                       k2n[64 * c:64 * c + 64, hd, 0:nk], start=True, stop=False)
                for c in range(2):
                    last = mm(wk(2 * (u % 2) + c)[:, s * P:nk], ident, causal, start=False, stop=True)
                last.then_inc(s2_done, 1)

            def turn2(u):
                s = u // 4
                pe.wait_ge(a2_ready, u + 1)
                if u >= 2:
                    pe.wait_ge(a2T_ready, u - 1)
                for b in range(s + 1):
                    last = nc.tensor.transpose(ps[:, 2 + u % 2, b * P:(b + 1) * P], a2[:, u % 2, b * P:(b + 1) * P], ident)
                last.then_inc(a2T_done, 1)

            def out2(u):
                s, hd = u // 4, u % 4
                pe.wait_ge(a2T_ready, u + 1)
                for b in range(s + 1):
                    last = mm(ps[:, s, hd * VD:(hd + 1) * VD], a2T[:, u % 2, b * P:(b + 1) * P],
                              v2[:, b, hd * VD:(hd + 1) * VD], start=(b == 0), stop=(b == s))
                if hd == 3:
                    last.then_inc(o2_done, 1)

            pe.wait_ge(conv_gated, 1)
            pe.wait_ge(v2_ready, 2)
            pe.wait_ge(ms2_ready, 3)
            for u in range(8 + 2):
                if u < 8:
                    if u >= 2:
                        pe.wait_ge(e2_ready, 2 * (u - 1))
                    scores2(u)
                if 1 <= u < 9:
                    turn2(u - 1)
                if u >= 2:
                    out2(u - 2)
            for s in range(TT):
                pe.wait_ge(o2n_ready, s + 1)
                for hd in range(4):
                    last = nc.tensor.transpose(wk(s)[:, hd * P:(hd + 1) * P], o2[:, s, hd * VD:(hd + 1) * VD], ident)
                last.then_inc(o2T_done, 1)
            pe.wait_ge(o2T_ready, 2)
            pe.wait_ge(cT_ready, 1)
            project(N_WOUT)

            transposes(4)
            pe.wait_ge(hT_lo_ready, 20)
            pe.wait_ge(wr_ready, 1)
            for s in range(TT):
                for k in range(KD):
                    last = mm3(wk(0)[:, 64 * s:64 * s + 36], [q[:, k, s * P:(s + 1) * P] for q in (hT_hi, hT_lo)],
                               [q[:, k, :] for q in (wr_hi, wr_lo)], k == 0, k == KD - 1)
            last.then_inc(lg_done, 1)
            for s in range(TT):
                for half in range(2):
                    mm(acc[:, s, half * COLS:(half + 1) * COLS], ident, x[:, s, half * COLS:(half + 1) * COLS],
                       start=True, stop=True)
            pe.wait_ge(ind_ready, 1)
            mm(wk(1)[:, 0:32], before, ind[:, 0, :], start=True, stop=True)
            mm(wk(1)[:, 64:96], ones, ind[:, 0, :], start=True, stop=False)
            mm(wk(1)[:, 64:96], before, ind[:, 1, :], start=False, stop=True)
            mm(wk(1)[:, 128:160], ones, ind[:, 0, :], start=True, stop=False)
            mm(wk(1)[:, 128:160], ones, ind[:, 1, :], start=False, stop=True).then_inc(pos_done, 1)

            def experts(it, i2, u):

                def chunk(c):
                    m = u * CPB + c
                    q = MOE_SLOTS[m % MOE_RING]
                    pe.wait_ge(slot_loaded[q], i2 * (16 * MOE_UNROLL * CPB // MOE_RING) + 16 * (MOE_FRONT[q] + m // MOE_RING + 1))
                    return moe_slot(m)

                pe.wait_ge(G_ready, it + 1)
                for k in range(KD):
                    for s in range(TT):
                        last = mm(wk(2 + k // 4)[:, (k % 4) * P:(k % 4 + 1) * P], h[:, s, k:D:KD], G[:, s, :],
                                  start=(s == 0), stop=(s == TT - 1))
                    if k % 4 == 3:
                        last.then_inc(xg_done, 1)
                for s in range(TT):
                    last = nc.tensor.transpose(wk(0)[:, s * P:(s + 1) * P], Gw[:, s, :], ident)
                last.then_inc(S_done, 1)
                pe.wait_ge(xg_lo, it + 1)
                pe.wait_ge(xg_hi, it + 1)
                pe.wait_ge(S_ready, it + 1)
                for c in range(8):
                    w = chunk(c).rearrange("p (j k f) -> p j k f", j=BATCH, k=2)
                    for kk in range(2):
                        k = 2 * (c % 4) + kk
                        for j in range(BATCH):
                            q = slice(SLOTS * j, SLOTS * (j + 1))
                            last = mm(wk(c // 4)[q, :], xgT[:, k, q], w[:, j, kk, :], start=(k == 0), stop=(k == KD - 1))
                    last.then_inc(chunks_used, 1)
                pe.wait_ge(act_ready, it + 1)
                for f in range(4):
                    last = nc.tensor.transpose(wk(1)[:, f * P:(f + 1) * P], act_s[:, f * P:(f + 1) * P], ident)
                last.then_inc(actT_done, 1)
                pe.wait_ge(actT_ready, it + 1)
                for f in range(4):
                    w = chunk(8 + f).rearrange("p (j d) -> p j d", j=BATCH)
                    for half in range(2):
                        for j in range(BATCH):
                            q = slice(SLOTS * j, SLOTS * (j + 1))
                            last = mm(wk(2 + half)[q, :], actT[:, f, q], w[:, j, half * COLS:(half + 1) * COLS],
                                      start=(f == 0), stop=(f == 3))
                    last.then_inc(chunks_used, 1)
                pe.wait_ge(y_lo, it + 1)
                pe.wait_ge(y_hi, it + 1)
                for s in range(TT):
                    for half in range(2):
                        mm(acc[:, s, half * COLS:(half + 1) * COLS], S[:, s * P:(s + 1) * P],
                           ysb[:, half * COLS:(half + 1) * COLS], start=False, stop=False, skip_group_check=True)

            pe.wait_ge(most_ready, 1)
            n_most = pe.value_load(most[0:1, 0:1], min_val=0, max_val=T)
            ITERS = GROUPS // MOE_UNROLL
            with pe.Fori(0, ITERS) as g2:
                for u in range(MOE_UNROLL):
                    experts(g2 * MOE_UNROLL + u, g2, u)
            with pe.Fori(1, PASSES) as b:
                with pe.If(n_most > b * SLOTS):
                    with pe.Fori(0, ITERS) as g2:
                        for u in range(MOE_UNROLL):
                            experts((b * ITERS + g2) * MOE_UNROLL + u, b * ITERS + g2, u)
            mm(acc[:, 1, COLS:D], zero_t[:, 0:P], zero_t[:, 0:COLS], start=False, stop=True,
               skip_group_check=True).then_inc(moe_done, 1)

        @block.scalar
        def _(act):
            order = Order(act, act_order)
            fn = nc.scalar.activation

            turns = [0]

            def sum_squares(src, s):
                fn(h[:, s, :], src, ACT.Square, accum_out=ss[:, s:s + 1]).then_inc(ss_ready, 1)

            def rsqrt():
                act.wait_ge(ms_ready, turns[0] + 1)
                order(fn(lnv[:, :], ms[:, :], ACT.Ln))
                fn(r0[:, :], lnv[:, :], ACT.Exp, scale=-0.5).then_inc(r0_ready, 1)
                turns[0] += 1

            def pre_norm(x_count):
                for s in range(TT):
                    act.wait_ge(x_ready, x_count - 1 + s) if x_count else act.wait_ge(x_loaded, 16)
                    sum_squares(x[:, s, :], s)
                rsqrt()

            def post_norm(chunks):
                act.wait_ge(quarters_used, 4 * chunks)
                for s in range(TT):
                    sum_squares(acc[:, s, :], s)
                rsqrt()

            def take_hT(turn, gain, dst, ready, again=False):
                for b in range(4):
                    act.wait_ge(hT_banks, 4 * turn + b + 1)
                    if again:
                        act.wait_ge(hT_lo_ready, 4 * turn + b + 1)
                    for k in (2 * b, 2 * b + 1):
                        last = fn(dst[:, k, :], wk(b)[:, (k % 2) * T:(k % 2) * T + T], ACT.Copy, scale=gains[:, gain, k:k + 1])
                    last.then_inc(ready, 1)

            def split(n, f, src, i=0):
                if f == 0:
                    act.wait_ge(slot_loaded[n % RING], i * 16 + 16 * (n // RING + 1))
                act.wait_ge(quarters_used, i * QI + (4 * n + f - 3))
                fn(w_hi[:, f, :].rearrange("p (k w) -> p k w", k=KD), src, ACT.Copy).then_inc(hi_ready, 1)

            def ahead(n, f):
                n, f = ahead_of(n, f)
                if n < N_MOE:
                    split(n, f, quarter(n, f))

            act.preload_act_table_set("natural_log_exp_and_others")
            pre_norm(0)
            act.wait_ge(early_loaded, EARLY)
            act.wait_ge(early_rows, EARLY_ROWS)
            fn(identr[:, :], ident, ACT.Copy).then_inc(maskr_ready, 1)
            fn(strictr[:, :], strict, ACT.Copy).then_inc(maskr_ready, 1)
            for k in range(4):
                if k % 2 == 0:
                    act.wait_ge(yT_banks, k // 2 + 1)
                last = fn(yT[:, k, :], wk(k // 2)[:, (k % 2) * T:(k % 2) * T + T], ACT.Copy, scale=poolg[:, k:k + 1])
            last.then_inc(yT_lo, 1)
            for f in range(AHEAD):
                split(1, f, quarter(1, f))
            for s in range(TT):
                act.wait_ge(scaled, s + 1)
                sum_squares(mg[:, s, :], s)
            rsqrt()
            act.wait_ge(late_loaded, LATE)

            def mlp(layer, turn, x_count):
                pre_norm(x_count)
                take_hT(turn, 0 if layer == 0 else 3, hT_hi, hT_hi_ready)
                n0 = N_MLP[layer]
                with act.Fori(0, PAIR_ITERS) as i:
                    for j in range(2 * PAIRS):
                        for f in range(4):
                            n = n0 + j
                            n2, f2 = ahead_of(n, f)
                            split(n2, f2, mlp_quarter(n2, n2 - n0, f2), i)
                            if j % 2 == 0:
                                act.wait_ge(quarters_used, i * QI + (4 * n + f + 1))
                                fn(rT[:, f, :], wk(f)[:, 0:T], ACT.Relu).then_inc(relu_ready, 1)
                                act.wait_ge(relu_ready, i * (4 * PAIRS) + (32 * layer + 4 * (j // 2) + f + 1))
                                fn(aT_hi[:, f, :], rT[:, f, :], ACT.Square).then_inc(sq_hi, 1)
                post_norm(n0 + 16)

            mlp(0, 0, 2)

            pre_norm(4)
            take_hT(1, 1, hT_hi, hT_hi_ready)
            take_hT(1, 2, mixT_hi, q_hi, again=True)
            for t in range(16):
                n, f = N_KV + t // 4, t % 4
                ahead(n, f)
                act.wait_ge(quarters_used, 4 * n + f + 1)
                if t < 8:
                    fn(kT[:, t, :], ps[:, f, 0:T], ACT.Copy).then_inc(proj_taken, 1)
                else:
                    fn(qT[:, t - 8, :], wk(f)[:, 0:T], ACT.Copy, scale=DH ** -0.5).then_inc(proj_taken, 1)
            for n in (N_KV + 4, N_KV + 5):
                for f in range(4):
                    ahead(n, f)

            for i in range(HEADS + 4):
                if i < HEADS:
                    act.wait_ge(absz_ready, i + 1)
                    order(fn(att[:, 1, i % 3, :], att[:, 0, i % 3, :], ACT.Exp))
                    fn(att[:, 1, i % 3, :], att[:, 1, i % 3, :], ACT.Ln, bias=1.0).then_inc(log_ready, 1)
                if 2 <= i < HEADS + 2:
                    act.wait_ge(arg_done, i - 1)
                    fn(att[:, 3, (i - 2) % 3, :], ps[:, (i - 2) % 6, 0:384], ACT.Exp).then_inc(prob_ready, 1)
                if i >= 4 and i % 2 == 0:
                    m = (i - 4) // 2
                    act.wait_ge(o_done, m + 1)
                    fn(mixT_hi[:, m, :], wk(2 + m % 2)[:, 0:T], ACT.Copy).then_inc(oT_hi, 1)
            for n in (N_WO, N_WO + 1):
                for f in range(4):
                    ahead(n, f)
            post_norm(N_WO + 2)
            mlp(1, 2, 6)

            pre_norm(8)
            take_hT(3, 4, hT_hi, hT_hi_ready)
            act.wait_ge(lam_dots, 1)
            fn(lam[:, 2:4], lam[:, 0:2], ACT.Exp).then_inc(lam_exp, 1)
            fn(wr_hi[:, :, :], wr[:, :, :], ACT.Copy).then_inc(wr_hi_ready, 1)

            def wide_rsqrt(i):
                act.wait_ge(ms2_ready, i + 1)
                order(fn(wr0, wms, ACT.Ln))
                fn(wr0, wr0, ACT.Exp, scale=-0.5).then_inc(rw_ready, 1)

            def squares(i):
                act.wait_ge(raw_ready, i + 1)
                fn(sq2, (q2, k2)[i], ACT.Square).then_inc(sq2_ready, 1)

            def take_xc():
                act.wait_ge(quarters_used, 4 * (N_IN + 3))
                fn(xc.rearrange("p k t -> p (k t)"), ps[:, 2:4, :].rearrange("p b c -> p (b c)"), ACT.Copy).then_inc(xc_ready, 1)

            def conv_squares():
                act.wait_ge(conv_gated, 1)
                fn(sq2, convy[:, :, :].rearrange("p k t -> p (k t)"), ACT.Square).then_inc(sq2_ready, 1)

            tasks = {(1, 1): lambda: squares(0), (2, 1): lambda: wide_rsqrt(0), (2, 3): lambda: squares(1),
                     (3, 0): take_xc, (3, 1): lambda: wide_rsqrt(1), (5, 2): conv_squares}
            for c in range(6):
                for f in range(4):
                    ahead(N_IN + c, f)
                    if (c, f) in tasks:
                        tasks[c, f]()
            for s in range(TT):
                act.wait_ge(quarters_used, 4 * (N_IN + 6))
                fn(v2[:, s, :], ps[:, s, :], ACT.Copy).then_inc(v2_ready, 1)
            wide_rsqrt(2)

            for u in range(8 + 1):
                if u < 8:
                    s = u // 4
                    nk = (s + 1) * P
                    act.wait_ge(nm_ready, u + 1)
                    for c in range(2):
                        fn(e2[:, u % 2, c, 0:nk], wk(2 * (u % 2) + c)[:, 0:nk], ACT.Exp, bias=st2[:, u % 2, c:c + 1],
                           accum_out=st2[:, u % 2, 2 + c:3 + c]).then_inc(e2_ready, 1)
                if u >= 1:
                    s = (u - 1) // 4
                    act.wait_ge(a2T_done, u)
                    fn(a2T[:, (u - 1) % 2, 0:(s + 1) * P], ps[:, 2 + (u - 1) % 2, 0:(s + 1) * P], ACT.Copy).then_inc(a2T_ready, 1)
            for s in range(TT):
                act.wait_ge(o2_done, s + 1)
                fn(sq2[:, s * COLS:(s + 1) * COLS], ps[:, s, :], ACT.Square).then_inc(o2sq_ready, 1)
            act.wait_ge(subms_ready, 1)
            order(fn(sub[:, 2, :], sub[:, 1, :], ACT.Ln))
            fn(sub[:, 3, :], sub[:, 2, :], ACT.Exp, scale=-0.5).then_inc(subr_ready, 1)
            act.wait_ge(n2_ready, 3)
            fn(mixT_hi[:, 0:4, :], convy[:, :, :], ACT.Copy).then_inc(cT_hi, 1)
            for s in range(TT):
                act.wait_ge(o2T_done, s + 1)
                fn(mixT_hi[:, 4:8, s * P:(s + 1) * P], wk(s).rearrange("p (m t) -> p m t", m=4), ACT.Copy).then_inc(o2T_hi, 1)
            for n in (N_WOUT, N_WOUT + 1):
                for f in range(4):
                    ahead(n, f)

            pre_norm(10)
            take_hT(4, 5, hT_hi, hT_hi_ready)
            act.wait_ge(gd_ready, 1)
            fn(small[:, 16:24], small[:, 8:16], ACT.Exp).then_inc(ge_ready, 1)
            act.wait_ge(dd_ready, 1)
            fn(small[:, 26:28], small[:, 24:26], ACT.Exp).then_inc(de_ready, 1)

            def experts(it):
                act.wait_ge(xg_done, it * 2 + 1)
                for k in range(4):
                    last = fn(xgT[:, k, :], wk(2)[:, k * P:(k + 1) * P], ACT.Copy, scale=gains[:, 5, k:k + 1])
                last.then_inc(xg_lo, 1)
                act.wait_ge(S_done, it + 1)
                fn(S, wk(0)[:, 0:T], ACT.Copy).then_inc(S_ready, 1)
                act.wait_ge(chunks_used, it * CPB + (4))
                fn(act_e, wk(0), ACT.Exp, scale=-1.0).then_inc(ex_ready, 1)
                act.wait_ge(actT_done, it + 1)
                fn(actT.rearrange("p f c -> p (f c)"), wk(1), ACT.Copy).then_inc(actT_ready, 1)
                act.wait_ge(chunks_used, it * CPB + (12))
                fn(ysb[:, 0:COLS], wk(2), ACT.Copy).then_inc(y_lo, 1)

            act.wait_ge(most_ready, 1)
            n_most = act.value_load(most[0:1, 0:1], min_val=0, max_val=T)
            with act.Fori(0, GROUPS) as g:
                experts(g)
            with act.Fori(1, PASSES) as b:
                with act.If(n_most > b * SLOTS):
                    with act.Fori(0, GROUPS) as g:
                        experts(b * GROUPS + g)
            act.wait_ge(moe_done, 1)
            fn(outsb[:, 0, :], acc[:, 0, :], ACT.Copy).then_inc(out_lo, 1)

        @block.vector
        def _(dve):
            order = Order(dve, dve_order)
            ve = nc.vector
            turns = [0]
            xs = [0]

            def rsqrt():
                i = turns[0]
                dve.wait_ge(ss_ready, 2 * i + 2)
                ve.tensor_scalar(ms[:, :], ss[:, :], 1.0 / D, EPS, ALU.mult, ALU.add).then_inc(ms_ready, 1)
                dve.wait_ge(r0_ready, i + 1)
                order(ve.tensor_tensor(r1[:, :], r0[:, :], r0[:, :], ALU.mult))
                order(ve.scalar_tensor_tensor(r1[:, :], r1[:, :], -0.5, ms[:, :], ALU.mult, ALU.mult))
                order(ve.scalar_tensor_tensor(rstd[:, :], r1[:, :], 1.5, r0[:, :], ALU.add, ALU.mult))
                turns[0] += 1

            def normalise():
                rsqrt()
                for s in range(TT):
                    ve.tensor_scalar(h[:, s, :], x[:, s, :], rstd[:, s:s + 1], None, ALU.mult).then_inc(h_ready, 1)

            def add_to_x():
                rsqrt()
                for s in range(TT):
                    ve.scalar_tensor_tensor(x[:, s, :], mg[:, s, :], rstd[:, s:s + 1], x[:, s, :], ALU.mult, ALU.add)\
                      .then_inc(x_ready, 1)
                xs[0] += 2
                dve.wait_ge(x_ready, xs[0])

            def post_norm(turn):
                dve.wait_ge(row_loaded, 16 * turn)
                for s in range(TT):
                    dve.wait_ge(ss_ready, 2 * turns[0] + s + 1)
                    order(ve.tensor_tensor(mg[:, s, :], acc[:, s, :], row[:, :], ALU.mult))
                add_to_x()

            def lower(dst, src, gain, upper):
                return ve.scalar_tensor_tensor(dst, src, gain, upper.bitcast(F32), ALU.mult, ALU.subtract)

            def take_hT(base, gain, upper, dst, hi, ready):
                for b in range(4):
                    dve.wait_ge(hi, base + b + 1)
                    for k in (2 * b, 2 * b + 1):
                        last = lower(dst[:, k, :], wk(b)[:, (k % 2) * T:(k % 2) * T + T], gains[:, gain, k:k + 1], upper[:, k, :])
                    last.then_inc(ready, 1)

            def split(n, f, src, i=0):
                dve.wait_ge(hi_ready, i * QI + (4 * (n - 1) + f + 1))
                ve.tensor_tensor(w_lo[:, f, :].rearrange("p (k w) -> p k w", k=KD), src,
                                 w_hi[:, f, :].rearrange("p (k w) -> p k w", k=KD).bitcast(F32), ALU.subtract).then_inc(lo_ready, 1)

            def ahead(n, f):
                n, f = ahead_of(n, f)
                if n < N_MOE:
                    split(n, f, quarter(n, f))

            ve.memset(zero_t[:, :].bitcast(F32), 0.0).then_inc(zero_ready, 1)
            dve.wait_ge(x_loaded, 16)
            normalise()
            dve.wait_ge(early_loaded, EARLY)
            dve.wait_ge(early_rows, EARLY_ROWS)
            for k in range(4, 8):
                if k % 2 == 0:
                    dve.wait_ge(yT_banks, k // 2 + 1)
                last = ve.tensor_scalar(yT[:, k, :], wk(k // 2)[:, (k % 2) * T:(k % 2) * T + T], poolg[:, k:k + 1], None, ALU.mult)
            last.then_inc(yT_hi, 1)
            for f in range(AHEAD):
                split(1, f, quarter(1, f))
            for s in range(TT):
                dve.wait_ge(quarters_used, 2 * s + 2)
                ve.tensor_tensor(mg[:, s, :], acc[:, s, :], scale_row[:, :], ALU.mult).then_inc(scaled, 1)
            for s in range(TT):
                dve.wait_ge(ss_ready, 2 * turns[0] + s + 1)
                order(ve.tensor_tensor(mg[:, s, :], mg[:, s, :], row[:, :], ALU.mult))
            add_to_x()
            dve.wait_ge(late_loaded, LATE)

            def mlp(layer, turn):
                normalise()
                take_hT(4 * turn, 0 if layer == 0 else 3, hT_hi, hT_lo, hT_hi_ready, hT_lo_ready)
                n0 = N_MLP[layer]
                with dve.Fori(0, PAIR_ITERS) as i:
                    for j in range(2 * PAIRS):
                        for f in range(4):
                            n2, f2 = ahead_of(n0 + j, f)
                            split(n2, f2, mlp_quarter(n2, n2 - n0, f2), i)
                            if j % 2 == 0:
                                done = 32 * layer + 4 * (j // 2) + f
                                dve.wait_ge(relu_ready, i * (4 * PAIRS) + (done + 1))
                                ve.tensor_tensor(aT[:, f, :], rT[:, f, :], rT[:, f, :], ALU.mult).then_inc(sq_full, 1)
                                dve.wait_ge(sq_full, i * (4 * PAIRS) + (done + 1))
                                dve.wait_ge(sq_hi, i * (4 * PAIRS) + (done + 1))
                                ve.tensor_tensor(aT_lo[:, f, :], aT[:, f, :], aT_hi[:, f, :].bitcast(F32), ALU.subtract)\
                                  .then_inc(sq_ready, 1)
                post_norm(1 if layer == 0 else 3)

            mlp(0, 0)

            normalise()
            take_hT(4, 1, hT_hi, hT_lo, hT_hi_ready, hT_lo_ready)
            take_hT(0, 2, mixT_hi, mixT_lo, q_hi, q_lo)
            for n in range(N_KV, N_KV + 6):
                for f in range(4):
                    ahead(n, f)
            for i in range(2):
                dve.wait_ge(quarters_used, 4 * (N_KV + 5 + i))
                for s in range(TT):
                    ve.tensor_copy(v[:, s, i * COLS:(i + 1) * COLS], acc[:, s, i * COLS:(i + 1) * COLS]).then_inc(v_taken, 1)

            for i in range(HEADS + 4):
                if i < HEADS:
                    dve.wait_ge(z_done, i + 1)
                    order(ve.tensor_scalar(att[:, 2, i % 3, :], ps[:, i % 6, 0:384], 0.0, None, ALU.max))
                    ve.scalar_tensor_tensor(att[:, 0, i % 3, :], att[:, 2, i % 3, :], -2.0, ps[:, i % 6, 0:384],
                                            ALU.mult, ALU.add).then_inc(absz_ready, 1)
                if 1 <= i <= HEADS:
                    dve.wait_ge(log_ready, i)
                    ve.tensor_tensor(att[:, 2, (i - 1) % 3, :], att[:, 2, (i - 1) % 3, :], att[:, 1, (i - 1) % 3, :],
                                     ALU.add).then_inc(lp_ready, 1)
                if i >= 4 and i % 2 == 0:
                    m = (i - 4) // 2
                    dve.wait_ge(oT_hi, m + 1)
                    ve.tensor_tensor(mixT_lo[:, m, :], wk(2 + m % 2)[:, 0:T], mixT_hi[:, m, :].bitcast(F32), ALU.subtract)\
                      .then_inc(oT_ready, 1)
            for n in (N_WO, N_WO + 1):
                for f in range(4):
                    ahead(n, f)
            post_norm(2)
            mlp(1, 2)

            normalise()
            take_hT(12, 4, hT_hi, hT_lo, hT_hi_ready, hT_lo_ready)
            for c in range(2):
                order(ve.tensor_tensor(lamv[:, 2 * c, :], lamv[:, 2 * c, :], lamv[:, 2 * c + 1, :], ALU.mult))
                order(ve.tensor_reduce(lam[:, c:c + 1], lamv[:, 2 * c, :], AX.X, ALU.add))
            order(ve.tensor_scalar(qg8[:, :], qkg[:, 0:1], DH ** -0.5, None, ALU.mult))
            order(ve.tensor_scalar(subg[:, :], subg[:, :], 1.0 - LAM_INIT, None, ALU.mult))
            ve.memset(convu[:, :, 0:2], 0.0).then_inc(lam_dots, 1)
            dve.wait_ge(lam_exp, 1)
            dve.wait_ge(lam_dots, 1)
            order(ve.tensor_tensor(lam[:, 4:5], lam[:, 3:4], lam[:, 2:3], ALU.subtract))
            order(ve.tensor_scalar(lam[:, 5:6], lam[:, 4:5], -LAM_INIT, None, ALU.add))
            dve.wait_ge(wr_hi_ready, 1)
            ve.tensor_tensor(wr_lo[:, :, :], wr[:, :, :], wr_hi[:, :, :].bitcast(F32), ALU.subtract).then_inc(wr_ready, 1)

            def mean_square(i, bank):
                dve.wait_ge(ms2_done, i + 1)
                ve.tensor_scalar(wms, ps[:, bank:bank + 2, :].rearrange("p b c -> p (b c)"), 1.0, EPS, ALU.mult, ALU.add)\
                  .then_inc(ms2_ready, 1)

            def wide_rsqrt(i):
                dve.wait_ge(ms2_ready, i + 1)
                dve.wait_ge(rw_ready, i + 1)
                order(ve.tensor_tensor(wr1, wr0, wr0, ALU.mult))
                order(ve.scalar_tensor_tensor(wr1, wr1, -0.5, wms, ALU.mult, ALU.mult))
                order(ve.scalar_tensor_tensor(wr1, wr1, 1.5, wr0, ALU.add, ALU.mult))

            def raw(i):
                dve.wait_ge(quarters_used, 4 * (N_IN + 1 + i))
                ve.tensor_copy((q2, k2)[i], ps[:, 4 + 2 * i:6 + 2 * i, :].rearrange("p b c -> p (b c)")).then_inc(raw_ready, 1)

            def normed(i):
                wide_rsqrt(i)
                q = (q2, k2)[i]
                ve.scalar_tensor_tensor(q, q, (qg8[:, :], qkg[:, 1:2])[i], wr1, ALU.mult, ALU.mult).then_inc(n2_ready, 1)

            def conv_input():
                dve.wait_ge(xc_ready, 1)
                dve.wait_ge(quarters_used, 4 * (N_IN + 4))
                order(ve.tensor_tensor(convu[:, :, 2:], ps[:, 4:6, :].rearrange("p b (k t) -> p (b k) t", k=2), xc, ALU.mult))

            def conv_tap(tap):
                for m in range(4):
                    u = convu[:, m, tap:tap + T]
                    if tap == 2:
                        last = ve.tensor_scalar(convy[:, m, :], u, convw[:, tap, m:m + 1], None, ALU.mult)
                    else:
                        last = ve.scalar_tensor_tensor(convy[:, m, :], u, convw[:, tap, m:m + 1], convy[:, m, :], ALU.mult, ALU.add)
                    last.then_inc(dve_order, 1)
                    order.n += 1
                dve.wait_ge(dve_order, order.n)

            def conv_gate():
                dve.wait_ge(quarters_used, 4 * (N_IN + 5))
                ve.tensor_tensor(convy[:, :, :], ps[:, 6:8, :].rearrange("p b (k t) -> p (b k) t", k=2), convy[:, :, :], ALU.mult)\
                  .then_inc(conv_gated, 1)
                dve.wait_ge(conv_gated, 1)

            tasks = {(1, 0): lambda: raw(0), (2, 0): lambda: mean_square(0, 4), (2, 1): lambda: normed(0),
                     (2, 3): lambda: raw(1), (3, 0): lambda: mean_square(1, 6), (3, 1): lambda: normed(1),
                     (4, 0): conv_input, (4, 1): lambda: conv_tap(2), (4, 2): lambda: conv_tap(1), (4, 3): lambda: conv_tap(0),
                     (5, 1): conv_gate}
            for c in range(6):
                for f in range(4):
                    ahead(N_IN + c, f)
                    if (c, f) in tasks:
                        tasks[c, f]()
            mean_square(2, 2)
            wide_rsqrt(2)
            for m in range(4):
                last = ve.scalar_tensor_tensor(convy[:, m, :], convy[:, m, :], convg[:, m:m + 1], wr1[:, m * T:(m + 1) * T],
                                               ALU.mult, ALU.mult)
            last.then_inc(n2_ready, 1)

            for u in range(8 + 1):
                if u < 8:
                    nk = (u // 4 + 1) * P
                    dve.wait_ge(s2_done, u + 1)
                    ve.tensor_reduce(st2[:, u % 2, 0:2], ps[:, 4 + 2 * (u % 2):6 + 2 * (u % 2), 0:nk], AX.X, ALU.max,
                                     negate=True).then_inc(nm_ready, 1)
                if u >= 1:
                    w = u - 1
                    b, nk = w % 2, (w // 4 + 1) * P
                    dve.wait_ge(e2_ready, 2 * w + 2)
                    order(ve.reciprocal(st2[:, b, 4:6], st2[:, b, 2:4]))
                    order(ve.tensor_tensor(st2[:, b, 6:7], st2[:, b, 5:6], lam[:, 5:6], ALU.mult))
                    order(ve.tensor_scalar(e2[:, b, 0, 0:nk], e2[:, b, 0, 0:nk], st2[:, b, 4:5], None, ALU.mult))
                    ve.scalar_tensor_tensor(a2[:, b, 0:nk], e2[:, b, 1, 0:nk], st2[:, b, 6:7], e2[:, b, 0, 0:nk],
                                            ALU.mult, ALU.add).then_inc(a2_ready, 1)
            for s in range(TT):
                dve.wait_ge(o2sq_ready, s + 1)
                order(ve.tensor_reduce(sub[:, 0, 4 * s:4 * s + 4], sq2[:, s * COLS:(s + 1) * COLS].rearrange("p (m d) -> p m d", m=4),
                                       AX.X, ALU.add))
            ve.tensor_scalar(sub[:, 1, :], sub[:, 0, :], 1.0 / VD, EPS, ALU.mult, ALU.add).then_inc(subms_ready, 1)
            dve.wait_ge(subr_ready, 1)
            order(ve.tensor_tensor(sub[:, 4, :], sub[:, 3, :], sub[:, 3, :], ALU.mult))
            order(ve.scalar_tensor_tensor(sub[:, 4, :], sub[:, 4, :], -0.5, sub[:, 1, :], ALU.mult, ALU.mult))
            order(ve.scalar_tensor_tensor(sub[:, 5, :], sub[:, 4, :], 1.5, sub[:, 3, :], ALU.add, ALU.mult))
            for s in range(TT):
                for m in range(4):
                    last = ve.scalar_tensor_tensor(o2[:, s, m * VD:(m + 1) * VD], ps[:, s, m * VD:(m + 1) * VD],
                                                   sub[:, 5, 4 * s + m:4 * s + m + 1], subg[:, :], ALU.mult, ALU.mult)
                last.then_inc(o2n_ready, 1)
            dve.wait_ge(n2_ready, 3)
            dve.wait_ge(cT_hi, 1)
            ve.tensor_tensor(mixT_lo[:, 0:4, :], convy[:, :, :], mixT_hi[:, 0:4, :].bitcast(F32), ALU.subtract).then_inc(cT_ready, 1)
            for s in range(TT):
                dve.wait_ge(o2T_hi, s + 1)
                ve.tensor_tensor(mixT_lo[:, 4:8, s * P:(s + 1) * P], wk(s).rearrange("p (m t) -> p m t", m=4),
                                 mixT_hi[:, 4:8, s * P:(s + 1) * P].bitcast(F32), ALU.subtract).then_inc(o2T_ready, 1)
            for n in (N_WOUT, N_WOUT + 1):
                for f in range(4):
                    ahead(n, f)
            dve.wait_ge(quarters_used, 4 * N_MOE)
            for s in range(TT):
                ve.tensor_tensor(x[:, s, :], x[:, s, :], acc[:, s, :], ALU.add).then_inc(x_ready, 1)
            xs[0] += 2
            dve.wait_ge(x_ready, xs[0])

            normalise()
            take_hT(16, 5, hT_hi, hT_lo, hT_hi_ready, hT_lo_ready)

            def piece(c, n, *shape):
                ap = small[:, c:c + n]
                if len(shape) == 2:
                    return ap.rearrange("p (a b) -> p a b", a=shape[0])
                if len(shape) == 3:
                    return ap.rearrange("p (a b c) -> p a b c", a=shape[0], b=shape[1])
                return ap

            def over(ap, n):
                return ap.unsqueeze(2).to_broadcast([P, ap.shape[1], n])

            LG = piece(64, 72, TT, 36)
            dve.wait_ge(lg_done, 1)
            order(ve.tensor_copy(LG, wk(0)[:, 0:128].rearrange("p (s c) -> p s c", s=TT)[:, :, 0:36]))
            lgg = LG[:, :, 0:NG]
            gmax, gsum, ggate, gr = piece(0, 2), piece(2, 2), piece(4, 2), piece(6, 2)
            gd, ge = piece(8, 8, TT, NG), piece(16, 8, TT, NG)
            dd, de, w1, w2 = piece(24, 2), piece(26, 2), piece(28, 2), piece(30, 2)
            m1, m2, rr = piece(32, 2), piece(34, 2), piece(36, 2)
            goh = piece(40, 8, TT, NG)
            sel, oh1, oh2, t8, cw, o12 = (piece(140 + 16 * i, 16, TT, NE) for i in range(6))
            prod = piece(256, 64, TT, NG, NE)
            order(ve.tensor_reduce(gmax, lgg, AX.X, ALU.max))
            ve.tensor_tensor(gd, lgg, over(gmax, NG), ALU.subtract).then_inc(gd_ready, 1)
            dve.wait_ge(ge_ready, 1)
            order(ve.tensor_reduce(gsum, ge, AX.X, ALU.add))
            order(ve.reciprocal(ggate, gsum))

            def first_max(dst, src, top, n):
                order(ve.tensor_tensor(dst, src, over(top, n), ALU.is_ge))
                r = rank[:, NE - n:NE].unsqueeze(1).to_broadcast([P, TT, n])
                order(ve.tensor_tensor(dst, dst, r, ALU.mult))
                order(ve.tensor_reduce(rr, dst, AX.X, ALU.max))
                order(ve.tensor_tensor(dst, dst, over(rr, n), ALU.is_equal))

            first_max(goh, lgg, gmax, NG)
            gohb = goh.unsqueeze(3).to_broadcast([P, TT, NG, NE])
            for s in range(TT):
                order(ve.tensor_tensor(prod[:, s], LG[:, s, NG:].rearrange("p (g e) -> p g e", g=NG), gohb[:, s], ALU.mult))
            for s in range(TT):
                order(ve.tensor_reduce(sel[:, s, :], prod[:, s].rearrange("p g e -> p e g"), AX.X, ALU.add))
            order(ve.tensor_reduce(m1, sel, AX.X, ALU.max))
            first_max(oh1, sel, m1, NE)
            order(ve.scalar_tensor_tensor(t8, oh1, NEG, sel, ALU.mult, ALU.add))
            order(ve.tensor_reduce(m2, t8, AX.X, ALU.max))
            first_max(oh2, t8, m2, NE)
            ve.tensor_tensor(dd, m2, m1, ALU.subtract).then_inc(dd_ready, 1)
            order(ve.tensor_tensor(o12, oh1, oh2, ALU.add))
            for s in range(TT):
                order(ve.tensor_tensor(ind[:, s, :].rearrange("p (g e) -> p g e", g=NG), gohb[:, s],
                                       o12[:, s, :].unsqueeze(1).to_broadcast([P, NG, NE]), ALU.mult))
            ve.tensor_copy(ind[:, 0, :], ind[:, 0, :]).then_inc(ind_ready, 1)
            dve.wait_ge(de_ready, 1)
            order(ve.tensor_scalar(w2, de, 1.0, None, ALU.add))
            order(ve.reciprocal(w1, w2))
            order(ve.tensor_tensor(w1, w1, ggate, ALU.mult))
            order(ve.tensor_tensor(w2, w1, de, ALU.mult))
            order(ve.tensor_tensor(oh1, oh1, over(w1, NE), ALU.mult))
            order(ve.tensor_tensor(oh2, oh2, over(w2, NE), ALU.mult))
            order(ve.tensor_tensor(cw, oh1, oh2, ALU.add))
            for s in range(TT):
                order(ve.tensor_tensor(comb[:, s, :].rearrange("p (g e) -> p g e", g=NG), gohb[:, s],
                                       cw[:, s, :].unsqueeze(1).to_broadcast([P, NG, NE]), ALU.mult))
            dve.wait_ge(pos_done, 1)
            pos = wk(1)[:, 0:128].rearrange("p (s e) -> p s e", s=TT)[:, :, 0:NG * NE]
            order(ve.scalar_tensor_tensor(posm[:, :, :], pos, 1.0, ind[:, :, :], ALU.add, ALU.mult))
            order(ve.tensor_scalar(posm[:, :, :], posm[:, :, :], -1.0, None, ALU.add))
            order(ve.tensor_reduce(mostf[:, :], wk(1)[:, 128:160], AX.X, ALU.max))
            ve.tensor_copy(most[:, :], mostf[:, :]).then_inc(most_ready, 1)

            order_base = order.n

            def experts(g, it):
                for s in range(TT):
                    slots = slot_ids.unsqueeze(1).to_broadcast([P, BATCH, SLOTS])
                    e4 = posm[:, s, bass.ds(g * BATCH, BATCH)].unsqueeze(2).to_broadcast([P, BATCH, SLOTS])
                    w4 = comb[:, s, bass.ds(g * BATCH, BATCH)].unsqueeze(2).to_broadcast([P, BATCH, SLOTS])
                    g4 = G[:, s, :].rearrange("p (j c) -> p j c", j=BATCH)
                    order(ve.tensor_tensor(g4, slots, e4, ALU.is_equal))
                    last = ve.tensor_tensor(Gw[:, s, :].rearrange("p (j c) -> p j c", j=BATCH), g4, w4, ALU.mult)
                last.then_inc(G_ready, 1)
                dve.wait_ge(xg_done, it * 2 + 2)
                for k in range(4, 8):
                    last = ve.tensor_scalar(xgT[:, k, :], wk(3)[:, (k - 4) * P:(k - 3) * P], gains[:, 5, k:k + 1], None, ALU.mult)
                last.then_inc(xg_hi, 1)
                dve.wait_ge(ex_ready, it + 1)
                order(ve.tensor_scalar(act_d, act_e, 1.0, None, ALU.add))
                order(ve.reciprocal(act_r, act_d))
                order(ve.tensor_tensor(act_t, wk(0), act_r, ALU.mult))
                dve.wait_ge(chunks_used, it * CPB + (8))
                ve.tensor_tensor(act_s, wk(1), act_t, ALU.mult).then_inc(act_ready, 1)
                dve.wait_ge(chunks_used, it * CPB + (12))
                ve.tensor_copy(ysb[:, COLS:D], wk(3)).then_inc(y_hi, 1)

            PER = 5
            dve.wait_ge(most_ready, 1)
            n_most = dve.value_load(most[0:1, 0:1], min_val=0, max_val=T)
            with dve.Fori(0, GROUPS) as g:
                order.base, order.n = g * PER + order_base, 0
                experts(g, g)
                assert order.n == PER
            with dve.Fori(1, PASSES) as b:
                with dve.If(n_most > b * SLOTS):
                    ve.tensor_scalar(slot_ids, slot_ids, float(SLOTS), None, ALU.add).then_inc(slots_moved, 1)
                    with dve.Fori(0, GROUPS) as g:
                        order.base, order.n = (b * GROUPS + g) * PER + order_base, 0
                        dve.wait_ge(slots_moved, b)
                        experts(g, b * GROUPS + g)
            dve.wait_ge(moe_done, 1)
            ve.tensor_copy(outsb[:, 1, :], acc[:, 1, :]).then_inc(out_hi, 1)


_INS = ['x', 'pool_w', 'pool_scale', 'w_q', 'w_kv', 'kv_norm_g', 'w_o', 'w_up', 'w_down', 'mix_pre_g', 'mix_post_g',
        'mlp_pre_g', 'mlp_post_g', 'attn_norm_g_2', 'w_in_2', 'conv_w_2', 'conv_out_g_2', 'q_norm_g_2', 'k_norm_g_2',
        'lambda_q1_2', 'lambda_k1_2', 'lambda_q2_2', 'lambda_k2_2', 'attn_subln_g_2', 'w_out_2', 'ffn_norm_g_2',
        'w_router_group_2', 'w_router_expert_2', 'w_exp_gate_2', 'w_exp_up_2', 'w_exp_down_2']


def kernel(**inputs):
    import concourse.bacc as bacc
    from concourse.bass_utils import run_bass_kernel_spmd

    nc = bacc.Bacc("TRN2", target_bir_lowering=False, num_devices=1)
    consts, poolm = shape_constants()
    given = {name: np.ascontiguousarray(inputs[name]) for name in _INS}
    given["consts"], given["poolm"] = consts, poolm
    arrays, args = {}, {}
    for name, arr in given.items():
        arrays[f"in_{name}"] = arr
        args[name] = nc.dram_tensor(f"in_{name}", arr.shape, mybir.dt.from_np(arr.dtype), kind="ExternalInput").ap()
    out = nc.dram_tensor("out_0", (1, T, D), F32, kind="ExternalOutput").ap()
    build(nc, args, out)
    r = run_bass_kernel_spmd(nc, [arrays], core_ids=[0])
    return r.results[0]["out_0"]
```

```python
from contextlib import ExitStack

import concourse.bass as bass
import numpy as np
from concourse import mybir

P = 128
D = 1024
T = 256
TT = T // P
KD = D // P
FF = 4096
COLS = 512
EPS = 1e-6
NEG = -1e30
HEADS, DH = 16, 64
WINDOWS = (2, 4, 8, 16)
HEADS2, VD = 4, 128
LAM_INIT = 0.2
NG, NE = 4, 8
FE = 512
SLOTS = 32
BATCH = P // SLOTS
GROUPS = NG * NE // BATCH
PASSES = T // SLOTS

RING = 4
CHUNK = 4096
CPB = 12

ALU = mybir.AluOpType
ACT = mybir.ActivationFunctionType
F32 = mybir.dt.float32
F32R = mybir.dt.float32r
I32 = mybir.dt.int32
AX = mybir.AxisListType

C_IDENT, C_NTRI, C_NONE, C_STRICT, C_CAUSAL, C_BEFORE, C_ONES, C_BLOCK, C_IOTA, C_RANK, C_END = (
    0, 128, 256, 384, 512, 640, 768, 896, 1024, 1056, 1064)


def shape_constants():
    i = np.arange(P)
    row, col = i[:, None], i[None, :]
    c = np.zeros((P, C_END), np.float32)
    c[:, C_IDENT:C_IDENT + P] = row == col
    c[:, C_NTRI:C_NTRI + P] = -1.0 * (row >= col)
    c[:, C_NONE:C_NONE + P] = -1.0
    c[:, C_STRICT:C_STRICT + P] = np.where(row >= col, NEG, 0.0)
    c[:, C_CAUSAL:C_CAUSAL + P] = np.where(col > row, NEG, 0.0)
    c[:, C_BEFORE:C_BEFORE + P] = row < col
    c[:, C_ONES:C_ONES + P] = 1.0
    c[:, C_BLOCK:C_BLOCK + P] = (row // 64 == col // 64) / 64.0
    c[:, C_IOTA:C_IOTA + SLOTS] = np.arange(SLOTS)[None, :]
    c[:, C_RANK:C_RANK + NE] = (NE - np.arange(NE))[None, :]
    t = np.arange(T)
    pool = np.zeros((P, len(WINDOWS), TT, T), np.float32)
    for w, win in enumerate(WINDOWS):
        m = ((t[:, None] <= t[None, :]) & (t[:, None] > t[None, :] - win)) / np.minimum(t + 1, win)[None, :]
        m = m - np.eye(T)
        pool[:, w] = m.reshape(TT, P, T).transpose(1, 0, 2)
    return c, pool.reshape(P, -1)


S_GAINS, S_POOLG, S_QKG, S_CONVW, S_CONVG, S_SUBG, S_LAM, S_ROUTER, SMALL_END = (
    0, 48, 56, 58, 70, 74, 202, 458, 458 + KD * (NG + NG * NE))


def pack_small(a):
    def every(v):
        return np.broadcast_to(v.reshape(1, -1), (P, v.size))

    pieces = [a[n][i].reshape(P, KD) for n, i in (("mlp_pre_g", 0), ("kv_norm_g", slice(None)), ("mix_pre_g", 1), ("mlp_pre_g", 1),
                                                  ("attn_norm_g_2", 0), ("ffn_norm_g_2", 0))]
    pieces.append(a["mix_pre_g"][0].reshape(KD, P).T)
    pieces += [np.tile(a[n][0], 2).reshape(P, 1) for n in ("q_norm_g_2", "k_norm_g_2")]
    pieces += [a["conv_w_2"][0, i].reshape(4, P).T for i in range(3)]
    pieces.append(a["conv_out_g_2"][0].reshape(4, P).T)
    pieces.append(every(a["attn_subln_g_2"][0]))
    pieces += [every(a[n][0]) for n in ("lambda_q1_2", "lambda_k1_2", "lambda_q2_2", "lambda_k2_2")]
    pieces.append(np.concatenate([a["w_router_group_2"][0].reshape(P, KD, NG), a["w_router_expert_2"][0].reshape(P, KD, NG * NE)],
                                 axis=2).reshape(P, -1))
    return np.ascontiguousarray(np.concatenate(pieces, axis=1))


N_POOL = 0
N_MLP = (1, 25)
N_KV = 17
N_WO = 23
N_IN = 41
N_WOUT = 47
N_MOE = 49
ROW_CHUNKS = {N_KV + 4, N_KV + 5, N_WO, N_WO + 1, N_IN + 2, N_WOUT, N_WOUT + 1}
PAIRS = RING // 2
PAIR_ITERS = FF // COLS // PAIRS
QI = 4 * RING
AHEAD = 2

GATED = 12
OUT = 24
STEPS = 32
UNITS = TT * HEADS2
UNIT_STEP = {GATED + 3 * (u // 2) + u % 2: u for u in range(UNITS)}


def step_quarter(p):
    if p < GATED:
        return N_IN + p // 4, p % 4
    if p < OUT:
        return N_IN + 3 + (p - GATED) % 3, (p - GATED) // 3
    return N_WOUT + (p - OUT) // 4, p % 4


def split_count(n):
    if N_IN + 3 <= n < N_IN + 6:
        return 4 * (N_IN - 1) + GATED + 9 + (n - N_IN - 3) + 1
    return 4 * n

MOE_RING = 2 * RING
MOE_SLOTS = (1, 2, 3, 0, 4, 5, 6, 7)
MOE_UNROLL = 2
MOE_FRONT = [len(range(q, N_MOE, RING)) for q in range(RING)] + [0] * RING


def build(nc, a, out):
    ctx = ExitStack()
    with ctx:
        def sem(name):
            return ctx.enter_context(nc.semaphore(name))

        top = [-(-nc.sbuf_base // 64) * 64]

        def at(name, shape, offset, dt=F32):
            return nc.alloc_sbuf_tensor_at(name, shape, dt, offset=offset)

        def region(nbytes):
            base = top[0]
            top[0] += -(-nbytes // 64) * 64
            return base

        def sb(name, shape, dt=F32):
            return at(name, shape, region(4 * int(np.prod(shape[1:]))), dt)

        K = 1024
        consts = sb("consts", [P, C_END])
        identr = sb("identr", [P, P], F32R)
        strictr = sb("strictr", [P, P], F32R)
        x = sb("x", [P, TT, D])
        h = sb("h", [P, TT, D])
        packed = sb("packed", [P, SMALL_END])
        gains = packed[:, S_GAINS:S_POOLG].rearrange("p (g k) -> p g k", k=KD)
        poolg = packed[:, S_POOLG:S_QKG]
        qkg = packed[:, S_QKG:S_CONVW]
        convw = packed[:, S_CONVW:S_CONVG].rearrange("p (i m) -> p i m", m=4)
        convg = packed[:, S_CONVG:S_SUBG]
        subg = packed[:, S_SUBG:S_LAM]
        lamv = packed[:, S_LAM:S_ROUTER].rearrange("p (i d) -> p i d", d=64)
        wr = packed[:, S_ROUTER:SMALL_END].rearrange("p (k e) -> p k e", k=KD)
        row = sb("row", [P, D])
        qg8 = sb("qg8", [P, 1])
        lam = sb("lam", [P, 8])
        wr_hi = sb("wr_hi", [P, KD, NG + NG * NE], F32R)
        wr_lo = sb("wr_lo", [P, KD, NG + NG * NE], F32R)
        ss = sb("ss", [P, 2])
        ms = sb("ms", [P, 2])
        lnv = sb("lnv", [P, 2])
        r0 = sb("r0", [P, 2])
        r1 = sb("r1", [P, 2])
        rstd = sb("rstd", [P, 2])
        rstd2 = sb("rstd2", [P, 2])
        st2 = sb("st2", [P, 2, 8])
        inv_sum = sb("inv_sum", [P, UNITS])
        sub = sb("sub", [P, 6, 8])
        small = sb("small", [P, 320])
        posm = sb("posm", [P, TT, NG * NE])
        comb = sb("comb", [P, TT, NG * NE])
        ind = sb("ind", [P, TT, NG * NE])
        most = sb("most", [P, 1], I32)
        mostf = sb("mostf", [P, 1])

        ring = sb("ring", [P, RING, CHUNK])
        w_base = region(64 * K)
        w_hi = at("w_hi", [P, 4, 1024], w_base, F32R)
        w_lo = at("w_lo", [P, 4, 1024], w_base + 16 * K, F32R)
        mixT_hi = at("mixT_hi", [P, KD, T], w_base + 32 * K, F32R)
        mixT_lo = at("mixT_lo", [P, KD, T], w_base + 40 * K, F32R)
        hT_hi = at("hT_hi", [P, KD, T], w_base + 48 * K, F32R)
        hT_lo = at("hT_lo", [P, KD, T], w_base + 56 * K, F32R)
        ring2 = at("ring2", [P, RING, CHUNK], w_base)
        yT = at("yT", [P, KD, T], w_base + 32 * K)

        kqv = region(24 * K)
        kbuf = at("kbuf", [P, KD * T], kqv)
        qbuf = at("qbuf", [P, KD * T], kqv + 8 * K)
        vbuf = at("vbuf", [P, TT * D], kqv + 16 * K)
        aT_hi = at("aT_hi", [P, 4, T], kqv + 8 * K, F32R)
        aT_lo = at("aT_lo", [P, 4, T], kqv + 12 * K, F32R)
        rT = at("rT", [P, 4, T], kqv + 16 * K)
        aT = at("aT", [P, 4, T], kqv + 20 * K)

        scratch = region(20 * K + 64)
        mg = at("mg", [P, TT, D], scratch)
        scale_row = at("scale_row", [P, D], scratch + 8 * K)
        att = at("att", [P, 4, 3, 384], scratch)
        convu = at("convu", [P, 4, T + 2], scratch + 8 * K)
        convy = at("convy", [P, 4, T], scratch + 12 * K + 64)
        e2 = at("e2", [P, 2, 2, T], scratch + 16 * K + 64)
        zero_t = sb("zero_t", [P, COLS], F32R)
        assert top[0] <= nc.sbuf_usable_end, (top[0], nc.sbuf_usable_end)

        ps = ctx.enter_context(nc.psum_tensor("ps", [P, 8, COLS], F32))
        acc = ps[:, 0:4, :].rearrange("p (t b) c -> p t (b c)", t=TT)

        def wk(b):
            return ps[:, 4 + b, :]

        ident = consts[:, C_IDENT:C_IDENT + P]
        ntri = consts[:, C_NTRI:C_NTRI + P]
        nones = consts[:, C_NONE:C_NONE + P]
        strict = consts[:, C_STRICT:C_STRICT + P]
        causal = consts[:, C_CAUSAL:C_CAUSAL + P]
        before = consts[:, C_BEFORE:C_BEFORE + P]
        ones = consts[:, C_ONES:C_ONES + P]
        blockmean = consts[:, C_BLOCK:C_BLOCK + P]
        slot_ids = consts[:, C_IOTA:C_IOTA + SLOTS]
        rank = consts[:, C_RANK:C_RANK + NE]

        poolm = kbuf[:, :].rearrange("p (w s t) -> p w s t", w=4, s=TT)
        kT = kbuf[:, :].rearrange("p (k t) -> p k t", k=KD)
        qT = qbuf[:, :].rearrange("p (k t) -> p k t", k=KD)
        v = vbuf[:, :].rearrange("p (s d) -> p s d", s=TT)
        q2 = qbuf[:, 0:1024]
        q2n = q2.rearrange("p (m t) -> p m t", m=4)
        k2 = qbuf[:, 1024:2048]
        k2n = k2.rearrange("p (m t) -> p m t", m=4)
        sq2 = kbuf[:, 0:1024]
        wms = kbuf[:, 1024:2048]
        wr0 = mg[:, 0, :]
        wr1 = mg[:, 1, :]
        v2 = vbuf[:, 0:1024].rearrange("p (s d) -> p s d", s=TT)
        xc = vbuf[:, 1024:2048].rearrange("p (k t) -> p k t", k=4)
        o2 = h[:, :, 0:COLS]
        a2 = h[:, 0, COLS:D].rearrange("p (b t) -> p b t", b=2)
        a2T = h[:, 1, COLS:D].rearrange("p (b t) -> p b t", b=2)
        G = kbuf[:, 0:256].rearrange("p (s c) -> p s c", s=TT)
        Gw = kbuf[:, 256:512].rearrange("p (s c) -> p s c", s=TT)
        S = kbuf[:, 512:768]
        actT = kbuf[:, 1024:1536].rearrange("p (f c) -> p f c", f=4)
        act_e = qbuf[:, 0:512]
        act_d = qbuf[:, 512:1024]
        act_r = qbuf[:, 1024:1536]
        act_t = qbuf[:, 1536:2048]
        xgT = vbuf[:, 0:1024].rearrange("p (k c) -> p k c", k=KD)
        ysb = vbuf[:, 1024:2048]
        act_s = kbuf[:, 1536:2048]
        outsb = mg

        x_loaded = sem("x_loaded")
        poolm_loaded = sem("poolm_loaded")
        packed_loaded = sem("packed_loaded")
        consts_loaded = sem("consts_loaded")
        scale_loaded = sem("scale_loaded")
        slot_loaded = [sem(f"slot_loaded{i}") for i in range(MOE_RING)]
        hi_ready = sem("hi_ready")
        lo_ready = sem("lo_ready")
        quarters_used = sem("quarters_used")
        chunks_used = sem("chunks_used")
        row_loaded = sem("row_loaded")
        q_hi = sem("q_hi")
        q_lo = sem("q_lo")
        oT_hi = sem("oT_hi")
        cT_ready = sem("cT_ready")
        cT_hi = sem("cT_hi")
        o2T_hi = sem("o2T_hi")
        wr_hi_ready = sem("wr_hi_ready")
        wr_ready = sem("wr_ready")
        maskr_ready = sem("maskr_ready")
        act_order = sem("act_order")
        dve_order = sem("dve_order")
        pe_order = sem("pe_order")
        x_ready = sem("x_ready")
        ss_ready = sem("ss_ready")
        ms_ready = sem("ms_ready")
        r0_ready = sem("r0_ready")
        h_ready = sem("h_ready")
        hT_banks = sem("hT_banks")
        hT_hi_ready = sem("hT_hi_ready")
        hT_lo_ready = sem("hT_lo_ready")
        m_ready = sem("m_ready")
        yT_banks = sem("yT_banks")
        yT_lo = sem("yT_lo")
        yT_hi = sem("yT_hi")
        mg_ready = sem("mg_ready")
        r2_ready = sem("r2_ready")
        scaled = sem("scaled")
        relu_ready = sem("relu_ready")
        sq_hi = sem("sq_hi")
        sq_full = sem("sq_full")
        sq_ready = sem("sq_ready")
        proj_done = sem("proj_done")
        proj_taken = sem("proj_taken")
        v_taken = sem("v_taken")
        z_done = sem("z_done")
        absz_ready = sem("absz_ready")
        log_ready = sem("log_ready")
        lp_ready = sem("lp_ready")
        arg_done = sem("arg_done")
        prob_ready = sem("prob_ready")
        o_done = sem("o_done")
        oT_ready = sem("oT_ready")
        in_done = sem("in_done")
        raw_ready = sem("raw_ready")
        sq2_ready = sem("sq2_ready")
        ms2_done = sem("ms2_done")
        ms2_ready = sem("ms2_ready")
        rw_ready = sem("rw_ready")
        n2_ready = sem("n2_ready")
        xc_ready = sem("xc_ready")
        v2_ready = sem("v2_ready")
        s2_done = sem("s2_done")
        nm_ready = sem("nm_ready")
        e2_ready = sem("e2_ready")
        a2_ready = sem("a2_ready")
        a2T_done = sem("a2T_done")
        a2T_ready = sem("a2T_ready")
        o2_done = sem("o2_done")
        lam_dots = sem("lam_dots")
        lam_exp = sem("lam_exp")
        o2sq_ready = sem("o2sq_ready")
        subms_ready = sem("subms_ready")
        subr_ready = sem("subr_ready")
        o2n_ready = sem("o2n_ready")
        o2T_done = sem("o2T_done")
        o2T_ready = sem("o2T_ready")
        lg_done = sem("lg_done")
        gd_ready = sem("gd_ready")
        ge_ready = sem("ge_ready")
        dd_ready = sem("dd_ready")
        de_ready = sem("de_ready")
        ind_ready = sem("ind_ready")
        pos_done = sem("pos_done")
        most_ready = sem("most_ready")
        seeded = sem("seeded")
        G_ready = sem("G_ready")
        xg_done = sem("xg_done")
        S_done = sem("S_done")
        S_ready = sem("S_ready")
        xg_lo = sem("xg_lo")
        xg_hi = sem("xg_hi")
        ex_ready = sem("ex_ready")
        act_ready = sem("act_ready")
        actT_done = sem("actT_done")
        actT_ready = sem("actT_ready")
        y_lo = sem("y_lo")
        y_hi = sem("y_hi")
        moe_done = sem("moe_done")
        out_lo = sem("out_lo")
        out_hi = sem("out_hi")
        stored = sem("stored")
        zero_ready = sem("zero_ready")
        cu_ready = sem("cu_ready")
        conv_gated = sem("conv_gated")
        slots_moved = sem("slots_moved")

        block = ctx.enter_context(nc.Block())

        class Order:

            def __init__(self, eng, s):
                self.eng, self.s, self.base, self.n = eng, s, 0, 0

            def __call__(self, ins):
                self.n += 1
                ins.then_inc(self.s, 1)
                self.eng.wait_ge(self.s, self.base + self.n)

        def slot(n):
            return ring[:, n % RING, :]

        def quarter(n, f):
            if n in ROW_CHUNKS:
                return slot(n)[:, 1024 * f:1024 * (f + 1)].rearrange("p (k w) -> p k w", k=KD)
            return slot(n).rearrange("p (k w) -> p k w", k=KD)[:, :, f * P:(f + 1) * P]

        def mlp_quarter(n, j, f):
            if j % 2:
                return slot(n)[:, 1024 * f:1024 * (f + 1)].rearrange("p (k w) -> p k w", k=KD)
            return slot(n).rearrange("p (k w) -> p k w", k=KD)[:, :, f * P:(f + 1) * P]

        def ahead_of(n, f):
            return n + (f + AHEAD) // 4, (f + AHEAD) % 4

        def moe_slot(c):
            q = MOE_SLOTS[c % MOE_RING]
            return ring[:, q, :] if q < RING else ring2[:, q - RING, :]

        def kd_rows(w):
            return w.rearrange("(p k) n -> p k n", k=KD)

        def std_rows(w):
            return w.rearrange("(m p) n -> p m n", p=P)

        def chunk_source(n):
            if n == N_POOL:
                return a["pool_w"][0].rearrange("g (c p) d -> p (g c) d", p=P), 8, 256
            if N_KV <= n < N_KV + 6:
                w, c = [("w_kv", 0), ("w_kv", 1), ("w_q", 0), ("w_q", 1), ("w_kv", 2), ("w_kv", 3)][n - N_KV]
                src = a[w] if w == "w_kv" else a[w][0]
                return kd_rows(src)[:, :, c * COLS:(c + 1) * COLS], KD, COLS
            if N_WO <= n < N_WO + 2:
                return std_rows(a["w_o"][0])[:, 4 * (n - N_WO):4 * (n - N_WO) + 4, :], 4, D
            if N_IN <= n < N_IN + 6:
                c = [3, 4, 5, 0, 2, 1][n - N_IN]
                return kd_rows(a["w_in_2"][0])[:, :, c * COLS:(c + 1) * COLS], KD, COLS
            return std_rows(a["w_out_2"][0])[:, 4 * (n - N_WOUT):4 * (n - N_WOUT) + 4, :], 4, D

        @block.sync
        def _(sp):
            sp.dma_start(x[:, :, :], a["x"][0].rearrange("(s p) d -> p s d", p=P)).then_inc(x_loaded, 16)
            sp.dma_start(kbuf[:, :], a["poolm"]).then_inc(poolm_loaded, 16)
            sp.dma_start(packed[:, :], a["packed"]).then_inc(packed_loaded, 16)

            def load(n, src, m, w):
                if n == RING:
                    sp.wait_ge(quarters_used, 4)
                elif n > RING:
                    sp.wait_ge(lo_ready, split_count(n - RING))
                sp.dma_start(slot(n)[:, 0:m * w].rearrange("p (m w) -> p m w", m=m), src)\
                  .then_inc(slot_loaded[n % RING], 16)
                if n == 1:
                    sp.dma_start(consts[:, :], a["consts"]).then_inc(consts_loaded, 16)

            def mlp(layer):
                up, down = kd_rows(a["w_up"][layer]), std_rows(a["w_down"][layer])
                n0 = N_MLP[layer]
                for j in range(2 * PAIRS):
                    n = n0 + j
                    if j % 2 == 0:
                        load(n, up[:, :, j // 2 * COLS:(j // 2 + 1) * COLS], KD, COLS)
                    else:
                        load(n, down[:, j // 2 * 4:j // 2 * 4 + 4, :], 4, D)
                with sp.Fori(1, PAIR_ITERS) as i:
                    for j in range(2 * PAIRS):
                        n = n0 + j
                        sp.wait_ge(lo_ready, i * QI + 4 * (n - RING))
                        if j % 2 == 0:
                            dst = slot(n).rearrange("p (m w) -> p m w", m=KD)
                            src = up[:, :, bass.ds(i * (PAIRS * COLS) + j // 2 * COLS, COLS)]
                        else:
                            dst = slot(n).rearrange("p (m w) -> p m w", m=4)
                            src = down[:, bass.ds(i * (PAIRS * 4) + j // 2 * 4, 4), :]
                        sp.dma_start(dst, src).then_inc(slot_loaded[n % RING], 16)

            load(N_POOL, *chunk_source(N_POOL))
            sp.dma_start(scale_row[:, :], a["pool_scale"][0].partition_broadcast(P)).then_inc(scale_loaded, 16)
            sp.dma_start(row[:, :], a["mix_post_g"][0].partition_broadcast(P)).then_inc(scale_loaded, 16)
            mlp(0)
            for n in range(N_KV, N_WO + 2):
                load(n, *chunk_source(n))
            mlp(1)
            for n in range(N_IN, N_WOUT + 2):
                load(n, *chunk_source(n))

            gate = a["w_exp_gate_2"][0].rearrange("g e (p k) f -> p (g e) (k f)", k=KD)
            up = a["w_exp_up_2"][0].rearrange("g e (p k) f -> p (g e) (k f)", k=KD)
            down = a["w_exp_down_2"][0].rearrange("g e (m p) d -> m p (g e) d", p=P)

            def experts(g2, i2, first=False):
                for u in range(MOE_UNROLL):
                    g = g2 * MOE_UNROLL + u
                    for c in range(CPB):
                        m = u * CPB + c
                        if not first or m >= MOE_RING:
                            sp.wait_ge(chunks_used, i2 * (MOE_UNROLL * CPB) + (m - MOE_RING + 1))
                        elif m < RING:
                            sp.wait_ge(lo_ready, split_count(N_MOE - RING + m))
                        elif m < MOE_RING - 1:
                            sp.wait_ge(quarters_used, 4 * N_MOE)
                        else:
                            sp.wait_ge(lg_done, 1)
                        dst = moe_slot(m).rearrange("p (j w) -> p j w", j=BATCH)
                        if c < 8:
                            w = gate if c < 4 else up
                            src = w[:, bass.ds(g * BATCH, BATCH), (c % 4) * 1024:(c % 4) * 1024 + 1024]
                        else:
                            src = down[c - 8][:, bass.ds(g * BATCH, BATCH), :]
                        sp.dma_start(dst, src).then_inc(slot_loaded[MOE_SLOTS[m % MOE_RING]], 16)

            ITERS = GROUPS // MOE_UNROLL
            experts(0, 0, True)
            with sp.Fori(1, ITERS) as g2:
                experts(g2, g2)
            sp.wait_ge(most_ready, 1)
            n_most = sp.value_load(most[0:1, 0:1], min_val=0, max_val=T)
            with sp.Fori(1, PASSES) as b:
                with sp.If(n_most > b * SLOTS):
                    with sp.Fori(0, ITERS) as g2:
                        experts(g2, b * ITERS + g2)

            sp.wait_ge(out_lo, 1)
            sp.dma_start(out[0, 0:P, :], outsb[:, 0, :]).then_inc(stored, 16)
            sp.wait_ge(out_hi, 1)
            sp.dma_start(out[0, P:T, :], outsb[:, 1, :]).then_inc(stored, 16)
            sp.wait_ge(stored, 32)

        @block.gpsimd
        def _(pool):
            def every(src):
                return src.partition_broadcast(P)

            for i, src in enumerate((a["mlp_post_g"][0], a["mix_post_g"][1], a["mlp_post_g"][1])):
                pool.wait_ge(x_ready, 2 * i + 2)
                pool.dma_start(row[:, :], every(src)).then_inc(row_loaded, 16)


        @block.tensor
        def _(pe):
            mm = nc.tensor.matmul

            def mm3(out, lhs, rhs, start, stop, **kw):
                (a_hi, a_lo), (b_hi, b_lo) = lhs, rhs
                mm(out, a_hi, b_hi, start=start, stop=False, skip_group_check=True)
                mm(out, a_hi, b_lo, start=False, stop=False, skip_group_check=True)
                return mm(out, a_lo, b_hi, start=False, stop=stop, skip_group_check=True)

            def arrived(n):
                pe.wait_ge(slot_loaded[n % RING], 16 * (n // RING + 1))

            def split(n, f, i=0):
                pe.wait_ge(lo_ready, i * QI + (4 * (n - 1) + f + 1))

            def transposes(src, ready, count):
                for s in range(TT):
                    pe.wait_ge(ready, count - 1 + s)
                    for k in range(KD):
                        c = (k % 2) * T + s * P
                        last = nc.tensor.transpose(wk(k // 2)[:, c:c + P], src[:, s, k:D:KD], ident)
                        if s == 1 and k % 2:
                            last.then_inc(hT_banks, 1)

            def channel_major(out, b, ops, ready=None):
                w = [q[:, b, :].rearrange("p (k w) -> p k w", k=KD) for q in (w_hi, w_lo)]
                for k in range(KD):
                    if ready is not None:
                        ready(k)
                    last = mm3(out, [q[:, k, :] for q in w], [q[:, k, :] for q in ops], k == 0, k == KD - 1)
                last.then_inc(quarters_used, 1)

            def token_major(outs, f):
                for kk in range(2):
                    k = 2 * f + kk
                    for s in range(TT):
                        last = mm3(outs[s], [q[:, k, s * P:(s + 1) * P] for q in (hT_hi, hT_lo)],
                                   [q[:, f, kk * COLS:(kk + 1) * COLS] for q in (w_hi, w_lo)], k == 0, k == KD - 1)
                last.then_inc(quarters_used, 1)

            def hT_tile(turn):
                return lambda k: pe.wait_ge(hT_lo_ready, 4 * turn + k // 2 + 1) if k % 2 == 0 else None

            pe.wait_ge(poolm_loaded, 16)
            pe.wait_ge(h_ready, 2)
            for b in range(4):
                for k in (2 * b, 2 * b + 1):
                    for s in range(TT):
                        last = mm(wk(b)[:, (k % 2) * T + s * P:(k % 2) * T + T], h[:, s, k * P:(k + 1) * P],
                                  poolm[:, k // 2, s, s * P:], start=(s == 0), stop=(s == TT - 1), skip_group_check=True)
                last.then_inc(yT_banks, 1)
            arrived(N_POOL)
            pe.wait_ge(yT_lo, 1)
            pe.wait_ge(yT_hi, 1)
            pw = slot(N_POOL)[:, 0:2048].rearrange("p (m w) -> p m w", m=8)
            for s in range(TT):
                for g in range(4):
                    for c in range(2):
                        last = mm(acc[:, s, 256 * g:256 * g + 256], yT[:, 2 * g + c, s * P:(s + 1) * P], pw[:, 2 * g + c, :],
                                  start=(c == 0), stop=(c == 1))
                    if g % 2:
                        last.then_inc(quarters_used, 1)

            def mlp(layer, turn, x_count):
                for s in range(TT):
                    for half in range(2):
                        mm(acc[:, s, half * COLS:(half + 1) * COLS], zero_t[:, 0:P], zero_t[:, 0:COLS],
                           start=True, stop=True)
                transposes(x, x_ready, x_count)
                pe.wait_ge(hT_lo_ready, 4 * turn + 4)
                n0 = N_MLP[layer]
                with pe.Fori(0, PAIR_ITERS) as i:
                    for j in range(PAIRS):
                        n = n0 + 2 * j
                        for f in range(4):
                            split(n, f, i)
                            channel_major(wk(f)[:, 0:T], f, (hT_hi, hT_lo))
                        for f in range(4):
                            split(n + 1, f, i)
                            pe.wait_ge(sq_ready, i * (4 * PAIRS) + (32 * layer + 4 * j + f + 1))
                            for s in range(TT):
                                for half in range(2):
                                    last = mm3(acc[:, s, half * COLS:(half + 1) * COLS],
                                               [q[:, f, s * P:(s + 1) * P] for q in (aT_hi, aT_lo)],
                                               [q[:, f, half * COLS:(half + 1) * COLS] for q in (w_hi, w_lo)], False, False)
                            last.then_inc(quarters_used, 1)

            pe.wait_ge(scaled, 2)
            pe.wait_ge(zero_ready, 1)
            pe.wait_ge(consts_loaded, 16)
            mlp(0, 0, 2)

            transposes(h, h_ready, 4)
            for t in range(16):
                n, f = N_KV + t // 4, t % 4
                if 4 <= t < 8 or t >= 12:
                    pe.wait_ge(proj_taken, t - 3)
                split(n, f)
                if t < 8:
                    channel_major(ps[:, f, 0:T], f, (hT_hi, hT_lo), ready=hT_tile(1) if t == 0 else None)
                else:
                    if t == 8:
                        pe.wait_ge(q_lo, 4)
                    channel_major(wk(f)[:, 0:T], f, (mixT_hi, mixT_lo))
            pe.wait_ge(proj_taken, 8)
            for i in range(2):
                for f in range(4):
                    split(N_KV + 4 + i, f)
                    token_major([acc[:, s, i * COLS:(i + 1) * COLS] for s in range(TT)], f)

            def zbank(i):
                return ps[:, i % 6, :]

            def scores(i):
                r, m = 64 * (i % 2), i // 2
                z = zbank(i)
                mm(z[:, 0:T], kT[r:r + 64, m, 0:P], qT[r:r + 64, m, :], start=True, stop=False, skip_group_check=True)
                mm(z[:, 0:P], identr[:, :], strictr[:, :], start=False, stop=False, skip_group_check=True)
                mm(z[:, T:T + P], kT[r:r + 64, m, P:T], qT[r:r + 64, m, P:T], start=False, stop=False, skip_group_check=True)
                mm(z[:, T:T + P], identr[:, :], strictr[:, :], start=False, stop=True, skip_group_check=True)\
                    .then_inc(z_done, 1)

            def args(i):
                z, lp = zbank(i), att[:, 2, i % 3, :]
                pe.wait_ge(lp_ready, i + 1)
                mm(z[:, 0:T], ntri, lp[:, 0:T], start=False, stop=False, skip_group_check=True)
                mm(z[:, P:T], nones, lp[:, T:T + P], start=False, stop=False, skip_group_check=True)
                mm(z[:, T:T + P], ntri, lp[:, T:T + P], start=False, stop=True, skip_group_check=True).then_inc(arg_done, 1)

            def weighted(i):
                r, m = 64 * (i % 2), i // 2
                p = att[:, 3, i % 3, :]
                o = wk(2 + m % 2)[r:r + 64, 0:T]
                pe.wait_ge(prob_ready, i + 1)
                if m >= 2 and i % 2 == 0:
                    pe.wait_ge(oT_ready, m - 1)
                mm(o, v[:, 0, i * DH:(i + 1) * DH], p[:, 0:T], start=True, stop=False, skip_group_check=True)
                last = mm(o[:, P:T], v[:, 1, i * DH:(i + 1) * DH], p[:, T:T + P], start=False, stop=True, skip_group_check=True)
                if i % 2:
                    last.then_inc(o_done, 1)

            pe.wait_ge(maskr_ready, 2)
            pe.wait_ge(proj_taken, 16)
            pe.wait_ge(v_taken, 4)
            for i in range(HEADS + 3):
                if i < HEADS:
                    if i >= 6:
                        pe.wait_ge(prob_ready, i - 5)
                    scores(i)
                if 2 <= i < HEADS + 2:
                    args(i - 2)
                if i >= 3:
                    weighted(i - 3)

            def project(m):
                for s in range(TT):
                    for half in range(2):
                        last = mm3(acc[:, s, half * COLS:(half + 1) * COLS],
                                   [q[:, m, s * P:(s + 1) * P] for q in (mixT_hi, mixT_lo)],
                                   [q[:, m % 4, half * COLS:(half + 1) * COLS] for q in (w_hi, w_lo)],
                                   m == 0, m == KD - 1)
                last.then_inc(quarters_used, 1)

            pe.wait_ge(prob_ready, HEADS)
            for m in range(KD):
                split(N_WO + m // 4, m % 4)
                if m % 2 == 0:
                    pe.wait_ge(oT_ready, m + 2)
                project(m)
            pe.wait_ge(mg_ready, 4)
            pe.wait_ge(ss_ready, 12)
            mlp(1, 2, 6)

            transposes(h, h_ready, 6)

            def mean_squares(i):
                pe.wait_ge(sq2_ready, i + 1)
                if i == 0:
                    mm(ps[:, 4, :], blockmean, sq2[:, 0:COLS], start=True, stop=True)
                    mm(ps[:, 5, :], blockmean, sq2[:, COLS:D], start=True, stop=True).then_inc(ms2_done, 1)
                elif i == 1:
                    pe.wait_ge(ms2_ready, 1)
                    mm(ps[:, 4, :], blockmean, sq2[:, 0:COLS], start=True, stop=True)
                    mm(ps[:, 5, :], blockmean, sq2[:, COLS:D], start=True, stop=True).then_inc(ms2_done, 1)
                else:
                    f = i - 2
                    pe.wait_ge(ms2_ready, i)
                    mm(ps[:, 5, 0:T], blockmean, sq2[:, f * T:(f + 1) * T], start=True, stop=True).then_inc(ms2_done, 1)

            def scores2(u):
                s, hd = u // 4, u % 4
                nk = (s + 1) * P
                if u == 0:
                    pe.wait_ge(n2_ready, 2)
                else:
                    pe.wait_ge(e2_ready, 2 * u)
                for c in range(2):
                    mm(ps[:, c, 0:nk], q2n[64 * c:64 * c + 64, hd, s * P:(s + 1) * P],
                       k2n[64 * c:64 * c + 64, hd, 0:nk], start=True, stop=False)
                for c in range(2):
                    last = mm(ps[:, c, s * P:nk], ident, causal, start=False, stop=True)
                last.then_inc(s2_done, 1)

            def turn2(u):
                s = u // 4
                pe.wait_ge(a2_ready, u + 1)
                if u >= 1:
                    pe.wait_ge(a2T_ready, u)
                for b in range(s + 1):
                    last = nc.tensor.transpose(ps[:, 2, b * P:(b + 1) * P], a2[:, u % 2, b * P:(b + 1) * P], ident)
                last.then_inc(a2T_done, 1)

            def out2(u):
                s, hd = u // 4, u % 4
                if u == 0:
                    pe.wait_ge(v2_ready, 2)
                pe.wait_ge(a2T_ready, u + 1)
                for b in range(s + 1):
                    last = mm(ps[:, 6 + s, hd * VD:(hd + 1) * VD], a2T[:, u % 2, b * P:(b + 1) * P],
                              v2[:, b, hd * VD:(hd + 1) * VD], start=(b == 0), stop=(b == s))
                if hd == 3:
                    last.then_inc(o2_done, 1)

            def turn_output(s):
                pe.wait_ge(o2n_ready, s + 1)
                pe.wait_ge(conv_gated, 4) if s == 0 else pe.wait_ge(ms2_ready, 6)
                for hd in range(4):
                    last = nc.tensor.transpose(ps[:, 4 + s, hd * P:(hd + 1) * P], o2[:, s, hd * VD:(hd + 1) * VD], ident)
                last.then_inc(o2T_done, 1)

            def bank_free(p):
                r, f = (p - 2 - GATED) % 3, (p - 2 - GATED) // 3
                return (xc_ready, cu_ready, conv_gated)[r], f + 1

            for p in range(STEPS):
                if p in UNIT_STEP:
                    scores2(UNIT_STEP[p])
                if p == OUT:
                    out2(UNITS - 1)
                    pe.wait_ge(cu_ready, 4)
                pe.wait_ge(lo_ready, 4 * (N_IN - 1) + p + 1)
                if p < 4:
                    channel_major(ps[:, p // 2, (p % 2) * T:(p % 2) * T + T], p % 4, (hT_hi, hT_lo),
                                  ready=hT_tile(3) if p == 0 else None)
                elif p < 8:
                    channel_major(ps[:, p // 2, (p % 2) * T:(p % 2) * T + T], p % 4, (hT_hi, hT_lo))
                elif p < GATED:
                    token_major([ps[:, 6 + s, :] for s in range(TT)], p - 8)
                elif p < OUT:
                    if p == GATED:
                        pe.wait_ge(raw_ready, 2)
                        pe.wait_ge(ms2_ready, 2)
                    elif p >= GATED + 2:
                        pe.wait_ge(*bank_free(p))
                    channel_major(ps[:, 3 + p % 2, 0:T], p % 4, (hT_hi, hT_lo))
                else:
                    m = p - OUT
                    if m < 4:
                        pe.wait_ge(cT_ready, m + 1)
                    elif m == 4:
                        pe.wait_ge(o2T_ready, 2)
                    project(m)
                if p - 2 in UNIT_STEP and p != OUT:
                    out2(UNIT_STEP[p - 2])
                if p - 1 in UNIT_STEP:
                    turn2(UNIT_STEP[p - 1])
                if p == 5 or p == 9:
                    mean_squares(p // 8)
                elif p >= GATED and p <= OUT and p % 3 == 0 and p > GATED:
                    mean_squares(2 + (p - GATED) // 3 - 1)
                if p == OUT + 1:
                    turn_output(0)
                if p == OUT + 2:
                    turn_output(1)

            transposes(h, h_ready, 8)
            pe.wait_ge(hT_lo_ready, 20)
            pe.wait_ge(wr_ready, 1)
            for s in range(TT):
                for k in range(KD):
                    last = mm3(wk(0)[:, 64 * s:64 * s + 36], [q[:, k, s * P:(s + 1) * P] for q in (hT_hi, hT_lo)],
                               [q[:, k, :] for q in (wr_hi, wr_lo)], k == 0, k == KD - 1)
            last.then_inc(lg_done, 1)
            for s in range(TT):
                for half in range(2):
                    mm(acc[:, s, half * COLS:(half + 1) * COLS], ident, x[:, s, half * COLS:(half + 1) * COLS],
                       start=True, stop=True)
            pe.wait_ge(ind_ready, 1)
            mm(wk(1)[:, 0:32], before, ind[:, 0, :], start=True, stop=True)
            mm(wk(1)[:, 64:96], ones, ind[:, 0, :], start=True, stop=False)
            mm(wk(1)[:, 64:96], before, ind[:, 1, :], start=False, stop=True)
            mm(wk(1)[:, 128:160], ones, ind[:, 0, :], start=True, stop=False)
            mm(wk(1)[:, 128:160], ones, ind[:, 1, :], start=False, stop=True).then_inc(pos_done, 1)

            def experts(it, i2, u):

                def chunk(c):
                    m = u * CPB + c
                    q = MOE_SLOTS[m % MOE_RING]
                    pe.wait_ge(slot_loaded[q], i2 * (16 * MOE_UNROLL * CPB // MOE_RING) + 16 * (MOE_FRONT[q] + m // MOE_RING + 1))
                    return moe_slot(m)

                pe.wait_ge(G_ready, it + 1)
                for k in range(KD):
                    for s in range(TT):
                        last = mm(wk(2 + k // 4)[:, (k % 4) * P:(k % 4 + 1) * P], h[:, s, k:D:KD], G[:, s, :],
                                  start=(s == 0), stop=(s == TT - 1))
                    if k % 4 == 3:
                        last.then_inc(xg_done, 1)
                for s in range(TT):
                    last = nc.tensor.transpose(wk(0)[:, s * P:(s + 1) * P], Gw[:, s, :], ident)
                last.then_inc(S_done, 1)
                pe.wait_ge(xg_lo, it + 1)
                pe.wait_ge(xg_hi, it + 1)
                pe.wait_ge(S_ready, it + 1)
                for c in range(8):
                    w = chunk(c).rearrange("p (j k f) -> p j k f", j=BATCH, k=2)
                    for kk in range(2):
                        k = 2 * (c % 4) + kk
                        for j in range(BATCH):
                            q = slice(SLOTS * j, SLOTS * (j + 1))
                            last = mm(wk(c // 4)[q, :], xgT[:, k, q], w[:, j, kk, :], start=(k == 0), stop=(k == KD - 1))
                    last.then_inc(chunks_used, 1)
                pe.wait_ge(act_ready, it + 1)
                for f in range(4):
                    last = nc.tensor.transpose(wk(1)[:, f * P:(f + 1) * P], act_s[:, f * P:(f + 1) * P], ident)
                last.then_inc(actT_done, 1)
                pe.wait_ge(actT_ready, it + 1)
                for f in range(4):
                    w = chunk(8 + f).rearrange("p (j d) -> p j d", j=BATCH)
                    for half in range(2):
                        for j in range(BATCH):
                            q = slice(SLOTS * j, SLOTS * (j + 1))
                            last = mm(wk(2 + half)[q, :], actT[:, f, q], w[:, j, half * COLS:(half + 1) * COLS],
                                      start=(f == 0), stop=(f == 3))
                    last.then_inc(chunks_used, 1)
                pe.wait_ge(y_lo, it + 1)
                pe.wait_ge(y_hi, it + 1)
                for s in range(TT):
                    for half in range(2):
                        mm(acc[:, s, half * COLS:(half + 1) * COLS], S[:, s * P:(s + 1) * P],
                           ysb[:, half * COLS:(half + 1) * COLS], start=False, stop=False, skip_group_check=True)

            pe.wait_ge(most_ready, 1)
            n_most = pe.value_load(most[0:1, 0:1], min_val=0, max_val=T)
            ITERS = GROUPS // MOE_UNROLL
            with pe.Fori(0, ITERS) as g2:
                for u in range(MOE_UNROLL):
                    experts(g2 * MOE_UNROLL + u, g2, u)
            with pe.Fori(1, PASSES) as b:
                with pe.If(n_most > b * SLOTS):
                    with pe.Fori(0, ITERS) as g2:
                        for u in range(MOE_UNROLL):
                            experts((b * ITERS + g2) * MOE_UNROLL + u, b * ITERS + g2, u)
            mm(acc[:, 1, COLS:D], zero_t[:, 0:P], zero_t[:, 0:COLS], start=False, stop=True,
               skip_group_check=True).then_inc(moe_done, 1)

        @block.scalar
        def _(act):
            order = Order(act, act_order)
            fn = nc.scalar.activation

            turns = [0]

            def sum_squares(src, s, scale=1.0):
                fn(h[:, s, :], src, ACT.Square, scale=scale, accum_out=ss[:, s:s + 1]).then_inc(ss_ready, 1)

            def rsqrt():
                act.wait_ge(ms_ready, turns[0] + 1)
                order(fn(lnv[:, :], ms[:, :], ACT.Ln))
                fn(r0[:, :], lnv[:, :], ACT.Exp, scale=-0.5).then_inc(r0_ready, 1)
                turns[0] += 1

            def pre_norm(x_count):
                for s in range(TT):
                    act.wait_ge(x_ready, x_count - 1 + s) if x_count else act.wait_ge(x_loaded, 16)
                    sum_squares(x[:, s, :], s)
                rsqrt()

            def post_norm(chunks, turn, pre_scale=None):
                act.wait_ge(quarters_used, 4 * chunks)
                for s in range(TT):
                    if s == 1:
                        act.wait_ge(mg_ready, 2 * turn - 1)
                    sum_squares(acc[:, s, :], s, 1.0 if pre_scale is None else pre_scale[:, s:s + 1])
                rsqrt()

            def take_hT(turn, gain, dst, ready, again=False):
                for b in range(4):
                    act.wait_ge(hT_banks, 4 * turn + b + 1)
                    if again:
                        act.wait_ge(hT_lo_ready, 4 * turn + b + 1)
                    for k in (2 * b, 2 * b + 1):
                        last = fn(dst[:, k, :], wk(b)[:, (k % 2) * T:(k % 2) * T + T], ACT.Copy, scale=gains[:, gain, k:k + 1])
                    last.then_inc(ready, 1)

            def split(n, f, src, i=0):
                if f == 0:
                    act.wait_ge(slot_loaded[n % RING], i * 16 + 16 * (n // RING + 1))
                act.wait_ge(quarters_used, i * QI + (4 * n + f - 3))
                fn(w_hi[:, f, :].rearrange("p (k w) -> p k w", k=KD), src, ACT.Copy).then_inc(hi_ready, 1)

            def ahead(n, f):
                n, f = ahead_of(n, f)
                if n < N_MOE:
                    split(n, f, quarter(n, f))

            def ahead_step(p):
                p += AHEAD
                if p < STEPS:
                    n, f = step_quarter(p)
                    if f == 0:
                        act.wait_ge(slot_loaded[n % RING], 16 * (n // RING + 1))
                    act.wait_ge(quarters_used, 4 * N_IN + p - 3)
                    fn(w_hi[:, p % 4, :].rearrange("p (k w) -> p k w", k=KD), quarter(n, f), ACT.Copy).then_inc(hi_ready, 1)

            act.preload_act_table_set("natural_log_exp_and_others")
            pre_norm(0)
            act.wait_ge(packed_loaded, 16)
            for k in range(4):
                if k % 2 == 0:
                    act.wait_ge(yT_banks, k // 2 + 1)
                last = fn(yT[:, k, :], wk(k // 2)[:, (k % 2) * T:(k % 2) * T + T], ACT.Copy, scale=poolg[:, k:k + 1])
            last.then_inc(yT_lo, 1)
            for f in range(AHEAD):
                split(1, f, quarter(1, f))
            for s in range(TT):
                act.wait_ge(scaled, s + 1)
                sum_squares(mg[:, s, :], s)
            rsqrt()
            act.wait_ge(consts_loaded, 16)
            fn(identr[:, :], ident, ACT.Copy).then_inc(maskr_ready, 1)
            fn(strictr[:, :], strict, ACT.Copy).then_inc(maskr_ready, 1)

            def mlp(layer, turn, x_count):
                take_hT(turn, 0 if layer == 0 else 3, hT_hi, hT_hi_ready)
                pre_norm(x_count)
                n0 = N_MLP[layer]
                with act.Fori(0, PAIR_ITERS) as i:
                    for j in range(2 * PAIRS):
                        for f in range(4):
                            n = n0 + j
                            n2, f2 = ahead_of(n, f)
                            split(n2, f2, mlp_quarter(n2, n2 - n0, f2), i)
                            if j % 2 == 0:
                                act.wait_ge(quarters_used, i * QI + (4 * n + f + 1))
                                fn(rT[:, f, :], wk(f)[:, 0:T], ACT.Relu).then_inc(relu_ready, 1)
                                act.wait_ge(relu_ready, i * (4 * PAIRS) + (32 * layer + 4 * (j // 2) + f + 1))
                                fn(aT_hi[:, f, :], rT[:, f, :], ACT.Square).then_inc(sq_hi, 1)
                act.wait_ge(r2_ready, layer + 1)
                post_norm(n0 + 16, 1 + 2 * layer, rstd2)

            mlp(0, 0, 2)

            pre_norm(4)
            take_hT(1, 1, hT_hi, hT_hi_ready)
            take_hT(1, 2, mixT_hi, q_hi, again=True)
            for t in range(16):
                n, f = N_KV + t // 4, t % 4
                ahead(n, f)
                act.wait_ge(quarters_used, 4 * n + f + 1)
                if t < 8:
                    fn(kT[:, t, :], ps[:, f, 0:T], ACT.Copy).then_inc(proj_taken, 1)
                else:
                    fn(qT[:, t - 8, :], wk(f)[:, 0:T], ACT.Copy, scale=DH ** -0.5).then_inc(proj_taken, 1)
            for n in (N_KV + 4, N_KV + 5):
                for f in range(4):
                    ahead(n, f)

            for i in range(HEADS + 4):
                if i < HEADS:
                    act.wait_ge(absz_ready, i + 1)
                    order(fn(att[:, 1, i % 3, :], att[:, 0, i % 3, :], ACT.Exp))
                    fn(att[:, 1, i % 3, :], att[:, 1, i % 3, :], ACT.Ln, bias=1.0).then_inc(log_ready, 1)
                if 2 <= i < HEADS + 2:
                    act.wait_ge(arg_done, i - 1)
                    fn(att[:, 3, (i - 2) % 3, :], ps[:, (i - 2) % 6, 0:384], ACT.Exp).then_inc(prob_ready, 1)
                if i >= 4 and i % 2 == 0:
                    m = (i - 4) // 2
                    act.wait_ge(o_done, m + 1)
                    fn(mixT_hi[:, m, :], wk(2 + m % 2)[:, 0:T], ACT.Copy).then_inc(oT_hi, 1)
            for n in (N_WO, N_WO + 1):
                for f in range(4):
                    ahead(n, f)
            post_norm(N_WO + 2, 2)
            mlp(1, 2, 6)

            pre_norm(8)
            take_hT(3, 4, hT_hi, hT_hi_ready)
            act.wait_ge(lam_dots, 1)
            fn(lam[:, 2:4], lam[:, 0:2], ACT.Exp).then_inc(lam_exp, 1)
            fn(wr_hi[:, :, :], wr[:, :, :], ACT.Copy).then_inc(wr_hi_ready, 1)

            def part(buf, i):
                return buf if i < 2 else buf[:, (i - 2) * T:(i - 1) * T]

            def wide_rsqrt(i):
                act.wait_ge(ms2_done, i + 1)
                src = ps[:, 4:6, :].rearrange("p b c -> p (b c)") if i < 2 else ps[:, 5, 0:T]
                fn(part(wms, i), src, ACT.Copy, bias=EPS).then_inc(ms2_ready, 1)
                act.wait_ge(ms2_ready, i + 1)
                order(fn(part(wr0, i), part(wms, i), ACT.Ln))
                fn(part(wr0, i), part(wr0, i), ACT.Exp, scale=-0.5).then_inc(rw_ready, 1)

            def squares(i):
                act.wait_ge(quarters_used, 4 * (N_IN + 1 + i))
                src = ps[:, 2 * i:2 * i + 2, :].rearrange("p b c -> p (b c)")
                fn(sq2, src, ACT.Square).then_inc(sq2_ready, 1)
                fn((q2, k2)[i], src, ACT.Copy).then_inc(raw_ready, 1)

            def conv_squares(f):
                act.wait_ge(conv_gated, f + 1)
                fn(sq2[:, f * T:(f + 1) * T], convy[:, f, :], ACT.Square).then_inc(sq2_ready, 1)

            def output_squares(s):
                act.wait_ge(o2_done, s + 1)
                fn(o2[:, s, :], ps[:, 6 + s, :], ACT.Square).then_inc(o2sq_ready, 1)

            def output_rsqrt(s):
                act.wait_ge(subms_ready, s + 1)
                order(fn(sub[:, 2, 4 * s:4 * s + 4], sub[:, 1, 4 * s:4 * s + 4], ACT.Ln))
                fn(sub[:, 3, 4 * s:4 * s + 4], sub[:, 2, 4 * s:4 * s + 4], ACT.Exp, scale=-0.5).then_inc(subr_ready, 1)

            for p in range(STEPS):
                if p in UNIT_STEP:
                    u = UNIT_STEP[p]
                    nk = (u // 4 + 1) * P
                    act.wait_ge(nm_ready, u + 1)
                    for c in range(2):
                        fn(e2[:, u % 2, c, 0:nk], ps[:, c, 0:nk], ACT.Exp, bias=st2[:, u % 2, c:c + 1],
                           accum_out=st2[:, u % 2, 2 + c:3 + c]).then_inc(e2_ready, 1)
                if p - 2 in UNIT_STEP:
                    u = UNIT_STEP[p - 2]
                    nk = (u // 4 + 1) * P
                    act.wait_ge(a2T_done, u + 1)
                    fn(a2T[:, u % 2, 0:nk], ps[:, 2, 0:nk], ACT.Copy).then_inc(a2T_ready, 1)
                if p == OUT + 1:
                    output_rsqrt(1)
                if p == 4 or p == 8:
                    squares(p // 8)
                ahead_step(p)
                if p == 6 or p == 10:
                    wide_rsqrt(p // 8)
                if p == GATED:
                    act.wait_ge(quarters_used, 4 * N_IN + GATED)
                    for s in range(TT):
                        fn(v2[:, s, :], ps[:, 6 + s, :], ACT.Copy).then_inc(v2_ready, 1)
                if GATED < p <= OUT:
                    r, f = (p - 1 - GATED) % 3, (p - 1 - GATED) // 3
                    if r == 0:
                        act.wait_ge(quarters_used, 4 * N_IN + p)
                        fn(xc[:, f, :], ps[:, 3 + (p - 1) % 2, 0:T], ACT.Copy).then_inc(xc_ready, 1)
                    elif r == 2:
                        conv_squares(f)
                if GATED + 4 <= p <= OUT + 1 and (p - GATED) % 3 == 1:
                    wide_rsqrt(2 + (p - GATED - 4) // 3)
                if GATED + 5 <= p <= OUT + 2 and (p - GATED) % 3 == 2:
                    f = (p - GATED - 5) // 3
                    act.wait_ge(n2_ready, 3 + f)
                    fn(mixT_hi[:, f, :], convy[:, f, :], ACT.Copy).then_inc(cT_hi, 1)
                if p == GATED + 8:
                    output_squares(0)
                if p == OUT:
                    output_squares(1)
                if p == GATED + 10:
                    output_rsqrt(0)
                if p == OUT + 2 or p == OUT + 3:
                    s = p - OUT - 2
                    act.wait_ge(o2T_done, s + 1)
                    fn(mixT_hi[:, 4:8, s * P:(s + 1) * P], ps[:, 4 + s, :].rearrange("p (m t) -> p m t", m=4), ACT.Copy)\
                        .then_inc(o2T_hi, 1)

            pre_norm(10)
            take_hT(4, 5, hT_hi, hT_hi_ready)
            act.wait_ge(gd_ready, 1)
            fn(small[:, 16:24], small[:, 8:16], ACT.Exp).then_inc(ge_ready, 1)
            act.wait_ge(dd_ready, 1)
            fn(small[:, 26:28], small[:, 24:26], ACT.Exp).then_inc(de_ready, 1)

            def experts(it):
                act.wait_ge(xg_done, it * 2 + 1)
                for k in range(4):
                    last = fn(xgT[:, k, :], wk(2)[:, k * P:(k + 1) * P], ACT.Copy, scale=gains[:, 5, k:k + 1])
                last.then_inc(xg_lo, 1)
                act.wait_ge(S_done, it + 1)
                fn(S, wk(0)[:, 0:T], ACT.Copy).then_inc(S_ready, 1)
                act.wait_ge(chunks_used, it * CPB + (4))
                fn(act_e, wk(0), ACT.Exp, scale=-1.0).then_inc(ex_ready, 1)
                act.wait_ge(actT_done, it + 1)
                fn(actT.rearrange("p f c -> p (f c)"), wk(1), ACT.Copy).then_inc(actT_ready, 1)
                act.wait_ge(chunks_used, it * CPB + (12))
                fn(ysb[:, 0:COLS], wk(2), ACT.Copy).then_inc(y_lo, 1)

            act.wait_ge(most_ready, 1)
            n_most = act.value_load(most[0:1, 0:1], min_val=0, max_val=T)
            with act.Fori(0, GROUPS) as g:
                experts(g)
            with act.Fori(1, PASSES) as b:
                with act.If(n_most > b * SLOTS):
                    with act.Fori(0, GROUPS) as g:
                        experts(b * GROUPS + g)
            act.wait_ge(moe_done, 1)
            fn(outsb[:, 0, :], acc[:, 0, :], ACT.Copy).then_inc(out_lo, 1)

        @block.vector
        def _(dve):
            order = Order(dve, dve_order)
            ve = nc.vector
            turns = [0]
            xs = [0]

            def rsqrt():
                i = turns[0]
                dve.wait_ge(ss_ready, 2 * i + 2)
                ve.tensor_scalar(ms[:, :], ss[:, :], 1.0 / D, EPS, ALU.mult, ALU.add).then_inc(ms_ready, 1)
                dve.wait_ge(r0_ready, i + 1)
                order(ve.tensor_tensor(r1[:, :], r0[:, :], r0[:, :], ALU.mult))
                order(ve.scalar_tensor_tensor(r1[:, :], r1[:, :], -0.5, ms[:, :], ALU.mult, ALU.mult))
                order(ve.scalar_tensor_tensor(rstd[:, :], r1[:, :], 1.5, r0[:, :], ALU.add, ALU.mult))
                turns[0] += 1

            def normalise():
                rsqrt()
                for s in range(TT):
                    ve.tensor_scalar(h[:, s, :], x[:, s, :], rstd[:, s:s + 1], None, ALU.mult).then_inc(h_ready, 1)

            def add_to_x():
                rsqrt()
                for s in range(TT):
                    ve.scalar_tensor_tensor(x[:, s, :], mg[:, s, :], rstd[:, s:s + 1], x[:, s, :], ALU.mult, ALU.add)\
                      .then_inc(x_ready, 1)
                xs[0] += 2
                dve.wait_ge(x_ready, xs[0])

            def post_norm(chunks, turn, pre_scale=None):
                dve.wait_ge(row_loaded, 16 * turn)
                dve.wait_ge(quarters_used, 4 * chunks)
                for s in (1, 0):
                    if s == 0:
                        dve.wait_ge(ss_ready, 2 * turns[0] + 1)
                    if pre_scale is None:
                        last = ve.tensor_tensor(mg[:, s, :], acc[:, s, :], row[:, :], ALU.mult)
                    else:
                        last = ve.scalar_tensor_tensor(mg[:, s, :], acc[:, s, :], pre_scale[:, s:s + 1], row[:, :], ALU.mult, ALU.mult)
                    last.then_inc(mg_ready, 1)
                dve.wait_ge(mg_ready, 2 * turn)
                add_to_x()

            def lower(dst, src, gain, upper):
                return ve.scalar_tensor_tensor(dst, src, gain, upper.bitcast(F32), ALU.mult, ALU.subtract)

            def take_hT(base, gain, upper, dst, hi, ready):
                for b in range(4):
                    dve.wait_ge(hi, base + b + 1)
                    for k in (2 * b, 2 * b + 1):
                        last = lower(dst[:, k, :], wk(b)[:, (k % 2) * T:(k % 2) * T + T], gains[:, gain, k:k + 1], upper[:, k, :])
                    last.then_inc(ready, 1)

            def split(n, f, src, i=0):
                dve.wait_ge(hi_ready, i * QI + (4 * (n - 1) + f + 1))
                ve.tensor_tensor(w_lo[:, f, :].rearrange("p (k w) -> p k w", k=KD), src,
                                 w_hi[:, f, :].rearrange("p (k w) -> p k w", k=KD).bitcast(F32), ALU.subtract).then_inc(lo_ready, 1)

            def ahead(n, f):
                n, f = ahead_of(n, f)
                if n < N_MOE:
                    split(n, f, quarter(n, f))

            def ahead_step(p):
                p += AHEAD
                if p < STEPS:
                    n, f = step_quarter(p)
                    dve.wait_ge(hi_ready, 4 * (N_IN - 1) + p + 1)
                    ve.tensor_tensor(w_lo[:, p % 4, :].rearrange("p (k w) -> p k w", k=KD), quarter(n, f),
                                     w_hi[:, p % 4, :].rearrange("p (k w) -> p k w", k=KD).bitcast(F32), ALU.subtract)\
                      .then_inc(lo_ready, 1)

            ve.memset(zero_t[:, :].bitcast(F32), 0.0).then_inc(zero_ready, 1)
            dve.wait_ge(x_loaded, 16)
            normalise()
            dve.wait_ge(packed_loaded, 16)
            for k in range(4, 8):
                if k % 2 == 0:
                    dve.wait_ge(yT_banks, k // 2 + 1)
                last = ve.tensor_scalar(yT[:, k, :], wk(k // 2)[:, (k % 2) * T:(k % 2) * T + T], poolg[:, k:k + 1], None, ALU.mult)
            last.then_inc(yT_hi, 1)
            for f in range(AHEAD):
                split(1, f, quarter(1, f))
            dve.wait_ge(scale_loaded, 32)
            for s in range(TT):
                dve.wait_ge(quarters_used, 2 * s + 2)
                ve.tensor_tensor(mg[:, s, :], acc[:, s, :], scale_row[:, :], ALU.mult).then_inc(scaled, 1)
            for s in range(TT):
                dve.wait_ge(ss_ready, 2 * turns[0] + s + 1)
                order(ve.tensor_tensor(mg[:, s, :], mg[:, s, :], row[:, :], ALU.mult))
            add_to_x()
            dve.wait_ge(consts_loaded, 16)

            def mlp(layer, turn):
                take_hT(4 * turn, 0 if layer == 0 else 3, hT_hi, hT_lo, hT_hi_ready, hT_lo_ready)
                rsqrt()
                ve.tensor_tensor(rstd2[:, :], rstd[:, :], rstd[:, :], ALU.mult).then_inc(r2_ready, 1)
                n0 = N_MLP[layer]
                with dve.Fori(0, PAIR_ITERS) as i:
                    for j in range(2 * PAIRS):
                        for f in range(4):
                            n2, f2 = ahead_of(n0 + j, f)
                            split(n2, f2, mlp_quarter(n2, n2 - n0, f2), i)
                            if j % 2 == 0:
                                done = 32 * layer + 4 * (j // 2) + f
                                dve.wait_ge(relu_ready, i * (4 * PAIRS) + (done + 1))
                                ve.tensor_tensor(aT[:, f, :], rT[:, f, :], rT[:, f, :], ALU.mult).then_inc(sq_full, 1)
                                dve.wait_ge(sq_full, i * (4 * PAIRS) + (done + 1))
                                dve.wait_ge(sq_hi, i * (4 * PAIRS) + (done + 1))
                                ve.tensor_tensor(aT_lo[:, f, :], aT[:, f, :], aT_hi[:, f, :].bitcast(F32), ALU.subtract)\
                                  .then_inc(sq_ready, 1)
                dve.wait_ge(r2_ready, layer + 1)
                post_norm(n0 + 16, 1 + 2 * layer, rstd2)

            mlp(0, 0)

            normalise()
            take_hT(4, 1, hT_hi, hT_lo, hT_hi_ready, hT_lo_ready)
            take_hT(0, 2, mixT_hi, mixT_lo, q_hi, q_lo)
            for n in range(N_KV, N_KV + 6):
                for f in range(4):
                    ahead(n, f)
            for i in range(2):
                dve.wait_ge(quarters_used, 4 * (N_KV + 5 + i))
                for s in range(TT):
                    ve.tensor_copy(v[:, s, i * COLS:(i + 1) * COLS], acc[:, s, i * COLS:(i + 1) * COLS]).then_inc(v_taken, 1)

            for i in range(HEADS + 4):
                if i < HEADS:
                    dve.wait_ge(z_done, i + 1)
                    order(ve.tensor_scalar(att[:, 2, i % 3, :], ps[:, i % 6, 0:384], 0.0, None, ALU.max))
                    ve.scalar_tensor_tensor(att[:, 0, i % 3, :], att[:, 2, i % 3, :], -2.0, ps[:, i % 6, 0:384],
                                            ALU.mult, ALU.add).then_inc(absz_ready, 1)
                if 1 <= i <= HEADS:
                    dve.wait_ge(log_ready, i)
                    ve.tensor_tensor(att[:, 2, (i - 1) % 3, :], att[:, 2, (i - 1) % 3, :], att[:, 1, (i - 1) % 3, :],
                                     ALU.add).then_inc(lp_ready, 1)
                if i >= 4 and i % 2 == 0:
                    m = (i - 4) // 2
                    dve.wait_ge(oT_hi, m + 1)
                    ve.tensor_tensor(mixT_lo[:, m, :], wk(2 + m % 2)[:, 0:T], mixT_hi[:, m, :].bitcast(F32), ALU.subtract)\
                      .then_inc(oT_ready, 1)
            for n in (N_WO, N_WO + 1):
                for f in range(4):
                    ahead(n, f)
            post_norm(N_WO + 2, 2)
            mlp(1, 2)

            normalise()
            take_hT(12, 4, hT_hi, hT_lo, hT_hi_ready, hT_lo_ready)
            for c in range(2):
                order(ve.tensor_tensor(lamv[:, 2 * c, :], lamv[:, 2 * c, :], lamv[:, 2 * c + 1, :], ALU.mult))
                order(ve.tensor_reduce(lam[:, c:c + 1], lamv[:, 2 * c, :], AX.X, ALU.add))
            order(ve.tensor_scalar(qg8[:, :], qkg[:, 0:1], DH ** -0.5, None, ALU.mult))
            order(ve.tensor_scalar(subg[:, :], subg[:, :], 1.0 - LAM_INIT, None, ALU.mult))
            ve.memset(convu[:, :, 0:2], 0.0).then_inc(lam_dots, 1)
            dve.wait_ge(lam_exp, 1)
            dve.wait_ge(lam_dots, 1)
            order(ve.tensor_tensor(lam[:, 4:5], lam[:, 3:4], lam[:, 2:3], ALU.subtract))
            order(ve.tensor_scalar(lam[:, 5:6], lam[:, 4:5], -LAM_INIT, None, ALU.add))
            dve.wait_ge(wr_hi_ready, 1)
            ve.tensor_tensor(wr_lo[:, :, :], wr[:, :, :], wr_hi[:, :, :].bitcast(F32), ALU.subtract).then_inc(wr_ready, 1)

            def part(buf, i):
                return buf if i < 2 else buf[:, (i - 2) * T:(i - 1) * T]

            def wide_rsqrt(i):
                dve.wait_ge(ms2_ready, i + 1)
                dve.wait_ge(rw_ready, i + 1)
                e, r, m = part(wr0, i), part(wr1, i), part(wms, i)
                order(ve.tensor_tensor(r, e, e, ALU.mult))
                order(ve.scalar_tensor_tensor(r, r, -0.5, m, ALU.mult, ALU.mult))
                order(ve.scalar_tensor_tensor(r, r, 1.5, e, ALU.add, ALU.mult))

            def normed(i):
                wide_rsqrt(i)
                q = (q2, k2)[i]
                dve.wait_ge(raw_ready, i + 1)
                ve.scalar_tensor_tensor(q, q, (qg8[:, :], qkg[:, 1:2])[i], wr1, ALU.mult, ALU.mult).then_inc(n2_ready, 1)

            def conv_input(f, p):
                dve.wait_ge(xc_ready, f + 1)
                dve.wait_ge(quarters_used, 4 * N_IN + p)
                ve.tensor_tensor(convu[:, f, 2:], ps[:, 3 + (p - 1) % 2, 0:T], xc[:, f, :], ALU.mult).then_inc(cu_ready, 1)
                dve.wait_ge(cu_ready, f + 1)
                order(ve.tensor_scalar(convy[:, f, :], convu[:, f, 2:2 + T], convw[:, 2, f:f + 1], None, ALU.mult))
                for tap in (1, 0):
                    order(ve.scalar_tensor_tensor(convy[:, f, :], convu[:, f, tap:tap + T], convw[:, tap, f:f + 1], convy[:, f, :],
                                                  ALU.mult, ALU.add))

            def conv_gate(f, p):
                dve.wait_ge(quarters_used, 4 * N_IN + p)
                ve.tensor_tensor(convy[:, f, :], ps[:, 3 + (p - 1) % 2, 0:T], convy[:, f, :], ALU.mult).then_inc(conv_gated, 1)

            def conv_normed(f):
                wide_rsqrt(2 + f)
                ve.scalar_tensor_tensor(convy[:, f, :], convy[:, f, :], convg[:, f:f + 1], part(wr1, 2 + f), ALU.mult, ALU.mult)\
                  .then_inc(n2_ready, 1)

            def output_mean_squares(s):
                q = slice(4 * s, 4 * s + 4)
                dve.wait_ge(o2sq_ready, s + 1)
                order(ve.tensor_tensor(sub[:, 3, q], inv_sum[:, q], inv_sum[:, q], ALU.mult))
                order(ve.tensor_reduce(sub[:, 0, q], o2[:, s, :].rearrange("p (m d) -> p m d", m=4), AX.X, ALU.add))
                order(ve.tensor_tensor(sub[:, 0, q], sub[:, 0, q], sub[:, 3, q], ALU.mult))
                ve.tensor_scalar(sub[:, 1, q], sub[:, 0, q], 1.0 / VD, EPS, ALU.mult, ALU.add).then_inc(subms_ready, 1)

            def output_normed(s):
                q = slice(4 * s, 4 * s + 4)
                dve.wait_ge(subr_ready, s + 1)
                order(ve.tensor_tensor(sub[:, 4, q], sub[:, 3, q], sub[:, 3, q], ALU.mult))
                order(ve.scalar_tensor_tensor(sub[:, 4, q], sub[:, 4, q], -0.5, sub[:, 1, q], ALU.mult, ALU.mult))
                order(ve.scalar_tensor_tensor(sub[:, 5, q], sub[:, 4, q], 1.5, sub[:, 3, q], ALU.add, ALU.mult))
                order(ve.tensor_tensor(sub[:, 5, q], sub[:, 5, q], inv_sum[:, q], ALU.mult))
                for m in range(4):
                    last = ve.scalar_tensor_tensor(o2[:, s, m * VD:(m + 1) * VD], ps[:, 6 + s, m * VD:(m + 1) * VD],
                                                   sub[:, 5, 4 * s + m:4 * s + m + 1], subg[:, :], ALU.mult, ALU.mult)
                last.then_inc(o2n_ready, 1)

            for p in range(STEPS):
                if p in UNIT_STEP:
                    u = UNIT_STEP[p]
                    dve.wait_ge(s2_done, u + 1)
                    ve.tensor_reduce(st2[:, u % 2, 0:2], ps[:, 0:2, 0:(u // 4 + 1) * P], AX.X, ALU.max,
                                     negate=True).then_inc(nm_ready, 1)
                if GATED < p <= OUT and (p - GATED) % 3 == 0:
                    conv_gate((p - GATED) // 3 - 1, p)
                ahead_step(p)
                if p == 6 or p == 10:
                    normed(p // 8)
                if GATED < p <= OUT and (p - GATED) % 3 == 2:
                    conv_input((p - GATED) // 3, p)
                if p in UNIT_STEP:
                    u = UNIT_STEP[p]
                    b, nk = u % 2, (u // 4 + 1) * P
                    dve.wait_ge(e2_ready, 2 * u + 2)
                    order(ve.reciprocal(st2[:, b, 4:5], st2[:, b, 3:4]))
                    order(ve.scalar_tensor_tensor(st2[:, b, 6:7], st2[:, b, 4:5], lam[:, 5:6], st2[:, b, 2:3], ALU.mult, ALU.mult))
                    order(ve.reciprocal(inv_sum[:, u:u + 1], st2[:, b, 2:3]))
                    ve.scalar_tensor_tensor(a2[:, b, 0:nk], e2[:, b, 1, 0:nk], st2[:, b, 6:7], e2[:, b, 0, 0:nk],
                                            ALU.mult, ALU.add).then_inc(a2_ready, 1)
                if GATED + 4 <= p <= OUT + 1 and (p - GATED) % 3 == 1:
                    conv_normed((p - GATED - 4) // 3)
                if GATED + 5 <= p <= OUT + 2 and (p - GATED) % 3 == 2:
                    f = (p - GATED - 5) // 3
                    dve.wait_ge(cT_hi, f + 1)
                    ve.tensor_tensor(mixT_lo[:, f, :], convy[:, f, :], mixT_hi[:, f, :].bitcast(F32), ALU.subtract)\
                      .then_inc(cT_ready, 1)
                if p == GATED + 9:
                    output_mean_squares(0)
                if p == OUT:
                    output_mean_squares(1)
                if p == GATED + 11:
                    output_normed(0)
                if p == OUT + 1:
                    output_normed(1)
                if p == OUT + 2 or p == OUT + 3:
                    s = p - OUT - 2
                    dve.wait_ge(o2T_hi, s + 1)
                    ve.tensor_tensor(mixT_lo[:, 4:8, s * P:(s + 1) * P], ps[:, 4 + s, :].rearrange("p (m t) -> p m t", m=4),
                                     mixT_hi[:, 4:8, s * P:(s + 1) * P].bitcast(F32), ALU.subtract).then_inc(o2T_ready, 1)
            dve.wait_ge(quarters_used, 4 * N_MOE)
            for s in range(TT):
                ve.tensor_tensor(x[:, s, :], x[:, s, :], acc[:, s, :], ALU.add).then_inc(x_ready, 1)
            xs[0] += 2
            dve.wait_ge(x_ready, xs[0])

            normalise()
            take_hT(16, 5, hT_hi, hT_lo, hT_hi_ready, hT_lo_ready)

            def piece(c, n, *shape):
                ap = small[:, c:c + n]
                if len(shape) == 2:
                    return ap.rearrange("p (a b) -> p a b", a=shape[0])
                if len(shape) == 3:
                    return ap.rearrange("p (a b c) -> p a b c", a=shape[0], b=shape[1])
                return ap

            def over(ap, n):
                return ap.unsqueeze(2).to_broadcast([P, ap.shape[1], n])

            LG = piece(64, 72, TT, 36)
            dve.wait_ge(lg_done, 1)
            order(ve.tensor_copy(LG, wk(0)[:, 0:128].rearrange("p (s c) -> p s c", s=TT)[:, :, 0:36]))
            lgg = LG[:, :, 0:NG]
            gmax, gsum, ggate, gr = piece(0, 2), piece(2, 2), piece(4, 2), piece(6, 2)
            gd, ge = piece(8, 8, TT, NG), piece(16, 8, TT, NG)
            dd, de, w1, w2 = piece(24, 2), piece(26, 2), piece(28, 2), piece(30, 2)
            m1, m2, rr = piece(32, 2), piece(34, 2), piece(36, 2)
            goh = piece(40, 8, TT, NG)
            sel, oh1, oh2, t8, cw, o12 = (piece(140 + 16 * i, 16, TT, NE) for i in range(6))
            prod = piece(256, 64, TT, NG, NE)
            order(ve.tensor_reduce(gmax, lgg, AX.X, ALU.max))
            ve.tensor_tensor(gd, lgg, over(gmax, NG), ALU.subtract).then_inc(gd_ready, 1)
            dve.wait_ge(ge_ready, 1)
            order(ve.tensor_reduce(gsum, ge, AX.X, ALU.add))
            order(ve.reciprocal(ggate, gsum))

            def first_max(dst, src, top, n):
                order(ve.tensor_tensor(dst, src, over(top, n), ALU.is_ge))
                r = rank[:, NE - n:NE].unsqueeze(1).to_broadcast([P, TT, n])
                order(ve.tensor_tensor(dst, dst, r, ALU.mult))
                order(ve.tensor_reduce(rr, dst, AX.X, ALU.max))
                order(ve.tensor_tensor(dst, dst, over(rr, n), ALU.is_equal))

            first_max(goh, lgg, gmax, NG)
            gohb = goh.unsqueeze(3).to_broadcast([P, TT, NG, NE])
            for s in range(TT):
                order(ve.tensor_tensor(prod[:, s], LG[:, s, NG:].rearrange("p (g e) -> p g e", g=NG), gohb[:, s], ALU.mult))
            for s in range(TT):
                order(ve.tensor_reduce(sel[:, s, :], prod[:, s].rearrange("p g e -> p e g"), AX.X, ALU.add))
            order(ve.tensor_reduce(m1, sel, AX.X, ALU.max))
            first_max(oh1, sel, m1, NE)
            order(ve.scalar_tensor_tensor(t8, oh1, NEG, sel, ALU.mult, ALU.add))
            order(ve.tensor_reduce(m2, t8, AX.X, ALU.max))
            first_max(oh2, t8, m2, NE)
            ve.tensor_tensor(dd, m2, m1, ALU.subtract).then_inc(dd_ready, 1)
            order(ve.tensor_tensor(o12, oh1, oh2, ALU.add))
            for s in range(TT):
                order(ve.tensor_tensor(ind[:, s, :].rearrange("p (g e) -> p g e", g=NG), gohb[:, s],
                                       o12[:, s, :].unsqueeze(1).to_broadcast([P, NG, NE]), ALU.mult))
            ve.tensor_copy(ind[:, 0, :], ind[:, 0, :]).then_inc(ind_ready, 1)
            dve.wait_ge(de_ready, 1)
            order(ve.tensor_scalar(w2, de, 1.0, None, ALU.add))
            order(ve.reciprocal(w1, w2))
            order(ve.tensor_tensor(w1, w1, ggate, ALU.mult))
            order(ve.tensor_tensor(w2, w1, de, ALU.mult))
            order(ve.tensor_tensor(oh1, oh1, over(w1, NE), ALU.mult))
            order(ve.tensor_tensor(oh2, oh2, over(w2, NE), ALU.mult))
            order(ve.tensor_tensor(cw, oh1, oh2, ALU.add))
            for s in range(TT):
                order(ve.tensor_tensor(comb[:, s, :].rearrange("p (g e) -> p g e", g=NG), gohb[:, s],
                                       cw[:, s, :].unsqueeze(1).to_broadcast([P, NG, NE]), ALU.mult))
            dve.wait_ge(pos_done, 1)
            pos = wk(1)[:, 0:128].rearrange("p (s e) -> p s e", s=TT)[:, :, 0:NG * NE]
            order(ve.scalar_tensor_tensor(posm[:, :, :], pos, 1.0, ind[:, :, :], ALU.add, ALU.mult))
            order(ve.tensor_scalar(posm[:, :, :], posm[:, :, :], -1.0, None, ALU.add))
            order(ve.tensor_reduce(mostf[:, :], wk(1)[:, 128:160], AX.X, ALU.max))
            ve.tensor_copy(most[:, :], mostf[:, :]).then_inc(most_ready, 1)

            order_base = order.n

            def experts(g, it):
                for s in range(TT):
                    slots = slot_ids.unsqueeze(1).to_broadcast([P, BATCH, SLOTS])
                    e4 = posm[:, s, bass.ds(g * BATCH, BATCH)].unsqueeze(2).to_broadcast([P, BATCH, SLOTS])
                    w4 = comb[:, s, bass.ds(g * BATCH, BATCH)].unsqueeze(2).to_broadcast([P, BATCH, SLOTS])
                    g4 = G[:, s, :].rearrange("p (j c) -> p j c", j=BATCH)
                    order(ve.tensor_tensor(g4, slots, e4, ALU.is_equal))
                    last = ve.tensor_tensor(Gw[:, s, :].rearrange("p (j c) -> p j c", j=BATCH), g4, w4, ALU.mult)
                last.then_inc(G_ready, 1)
                dve.wait_ge(xg_done, it * 2 + 2)
                for k in range(4, 8):
                    last = ve.tensor_scalar(xgT[:, k, :], wk(3)[:, (k - 4) * P:(k - 3) * P], gains[:, 5, k:k + 1], None, ALU.mult)
                last.then_inc(xg_hi, 1)
                dve.wait_ge(ex_ready, it + 1)
                order(ve.tensor_scalar(act_d, act_e, 1.0, None, ALU.add))
                order(ve.reciprocal(act_r, act_d))
                order(ve.tensor_tensor(act_t, wk(0), act_r, ALU.mult))
                dve.wait_ge(chunks_used, it * CPB + (8))
                ve.tensor_tensor(act_s, wk(1), act_t, ALU.mult).then_inc(act_ready, 1)
                dve.wait_ge(chunks_used, it * CPB + (12))
                ve.tensor_copy(ysb[:, COLS:D], wk(3)).then_inc(y_hi, 1)

            PER = 5
            dve.wait_ge(most_ready, 1)
            n_most = dve.value_load(most[0:1, 0:1], min_val=0, max_val=T)
            with dve.Fori(0, GROUPS) as g:
                order.base, order.n = g * PER + order_base, 0
                experts(g, g)
                assert order.n == PER
            with dve.Fori(1, PASSES) as b:
                with dve.If(n_most > b * SLOTS):
                    ve.tensor_scalar(slot_ids, slot_ids, float(SLOTS), None, ALU.add).then_inc(slots_moved, 1)
                    with dve.Fori(0, GROUPS) as g:
                        order.base, order.n = (b * GROUPS + g) * PER + order_base, 0
                        dve.wait_ge(slots_moved, b)
                        experts(g, b * GROUPS + g)
            dve.wait_ge(moe_done, 1)
            ve.tensor_copy(outsb[:, 1, :], acc[:, 1, :]).then_inc(out_hi, 1)


_INS = ['x', 'pool_w', 'pool_scale', 'w_q', 'w_kv', 'w_o', 'w_up', 'w_down', 'mix_post_g', 'mlp_post_g', 'w_in_2', 'w_out_2',
        'w_exp_gate_2', 'w_exp_up_2', 'w_exp_down_2']


def kernel(**inputs):
    import concourse.bacc as bacc
    from concourse.bass_utils import run_bass_kernel_spmd

    nc = bacc.Bacc("TRN2", target_bir_lowering=False, num_devices=1)
    consts, poolm = shape_constants()
    given = {name: np.ascontiguousarray(inputs[name]) for name in _INS}
    given["consts"], given["poolm"], given["packed"] = consts, poolm, pack_small(inputs)
    arrays, args = {}, {}
    for name, arr in given.items():
        arrays[f"in_{name}"] = arr
        args[name] = nc.dram_tensor(f"in_{name}", arr.shape, mybir.dt.from_np(arr.dtype), kind="ExternalInput").ap()
    out = nc.dram_tensor("out_0", (1, T, D), F32, kind="ExternalOutput").ap()
    build(nc, args, out)
    r = run_bass_kernel_spmd(nc, [arrays], core_ids=[0])
    return r.results[0]["out_0"]
```
